# Optimizing a Trainium2 kernel written in Bass

```python
import math
import jax, jax.numpy as jnp
from jax import lax
import numpy as np

D_MODEL = 1024
BATCH = 1
SEQ = 512
DEPTH = 1

D_MIX = D_MODEL
ATTN_QK_DIM = 32
ATTN_V_DIM = 2 * ATTN_QK_DIM
N_ATTN_HEADS = (D_MIX // 2) // ATTN_V_DIM
W_ATTN_QK = N_ATTN_HEADS * 2 * ATTN_QK_DIM
W_ATTN = N_ATTN_HEADS * ATTN_V_DIM
ROT_DIM = ATTN_QK_DIM // 4
ROPE_THETA = 500000.0
Q_BLOCK = 128
POS_OFFSET_MAX = 1024
S5_GROUP_CH = 16
S5_STATE = 64
W_S5 = D_MIX - W_ATTN
S5_GROUPS = W_S5 // S5_GROUP_CH
S5_MIN_STEP = 1e-3
S5_MAX_STEP = 1e-1
D_IN_PROJ = 2 * W_ATTN_QK + W_ATTN + W_S5
N_EXPERTS = 32
TOP_K = 4
D_FF = D_MODEL
SWIGLU_ALPHA = 1.702
SWIGLU_LIMIT = 7.0
MOE_BLOCK = 128
RMS_EPS = 1e-6

kernel_name = "hybrid_diffattn_s5_moe_block"

def rms_norm(x, w, eps=RMS_EPS):
    xf = x.astype(jnp.float32)
    y = xf * lax.rsqrt(jnp.mean(xf * xf, axis=-1, keepdims=True) + eps)
    return y.astype(x.dtype) * w

def rope_tables(positions):
    inv_freq = ROPE_THETA ** (-jnp.arange(0, ROT_DIM, 2, dtype=jnp.float32) / ROT_DIM)
    ang = positions.astype(jnp.float32)[..., None] * inv_freq
    return jnp.cos(ang), jnp.sin(ang)

def apply_partial_rope(t, cos, sin):
    half = ROT_DIM // 2
    cos = cos[:, :, None, None, :].astype(t.dtype)
    sin = sin[:, :, None, None, :].astype(t.dtype)
    t1 = t[..., :half]
    t2 = t[..., half:ROT_DIM]
    return jnp.concatenate([t1 * cos - t2 * sin, t2 * cos + t1 * sin, t[..., ROT_DIM:]], axis=-1)

def diff_attention(q, k, v, cos, sin, q_norm_w, k_norm_w, lam, subln_w, lambda_init):
    B, S, _ = q.shape
    H, d, dv = N_ATTN_HEADS, ATTN_QK_DIM, ATTN_V_DIM
    q = rms_norm(q.reshape(B, S, H, 2, d), q_norm_w)
    k = rms_norm(k.reshape(B, S, H, 2, d), k_norm_w)
    q = apply_partial_rope(q, cos, sin)
    k = apply_partial_rope(k, cos, sin)
    q = jnp.transpose(q, (0, 2, 3, 1, 4))
    k = jnp.transpose(k, (0, 2, 3, 1, 4))
    v = jnp.transpose(v.reshape(B, S, H, dv), (0, 2, 1, 3))
    n_qb = S // Q_BLOCK
    qb = jnp.moveaxis(q.reshape(B, H, 2, n_qb, Q_BLOCK, d), 3, 0)
    scale = 1.0 / math.sqrt(d)

    def block(q_blk):
        s = jnp.einsum('bhcqd,bhckd->bhcqk', q_blk, k).astype(jnp.float32) * scale
        p = jax.nn.softmax(s, axis=-1)
        a = p[:, :, 0] - lam * p[:, :, 1]
        return jnp.einsum('bhqk,bhkv->bhqv', a.astype(v.dtype), v)

    o = lax.map(block, qb)
    o = jnp.transpose(o, (1, 0, 3, 2, 4)).reshape(B, S, H, dv)
    o = rms_norm(o, subln_w) * (1.0 - lambda_init)
    return o.reshape(B, S, W_ATTN)

def complex_combine(e_i, e_j):
    ar_i, ai_i, br_i, bi_i = e_i
    ar_j, ai_j, br_j, bi_j = e_j
    return (ar_j * ar_i - ai_j * ai_i,
            ar_j * ai_i + ai_j * ar_i,
            ar_j * br_i - ai_j * bi_i + br_j,
            ar_j * bi_i + ai_j * br_i + bi_j)

def s5_mixer(u, lam_re, lam_im, log_step, b_re, b_im, cm_re, cm_im, d_skip, glu_w, glu_b, out_w):
    Bsz, S, _ = u.shape
    uf = u.astype(jnp.float32).reshape(Bsz, S, S5_GROUPS, S5_GROUP_CH)
    y = uf * d_skip.astype(jnp.float32).reshape(S5_GROUPS, S5_GROUP_CH)
    for di in range(2):
        lr = lam_re[di].astype(jnp.float32)
        li = lam_im[di].astype(jnp.float32)
        delta = jnp.exp(log_step[di].astype(jnp.float32))[:, None]
        mag = jnp.exp(lr * delta)
        abar_re = mag * jnp.cos(li * delta)
        abar_im = mag * jnp.sin(li * delta)
        den = lr * lr + li * li
        num_re = abar_re - 1.0
        f_re = (num_re * lr + abar_im * li) / den
        f_im = (abar_im * lr - num_re * li) / den
        br = b_re[di].astype(jnp.float32)
        bi = b_im[di].astype(jnp.float32)
        bbar_re = f_re[..., None] * br - f_im[..., None] * bi
        bbar_im = f_re[..., None] * bi + f_im[..., None] * br
        bu_re = jnp.einsum('bsgc,gpc->bsgp', uf, bbar_re)
        bu_im = jnp.einsum('bsgc,gpc->bsgp', uf, bbar_im)
        a_re = jnp.broadcast_to(abar_re, bu_re.shape)
        a_im = jnp.broadcast_to(abar_im, bu_im.shape)
        _, _, xr, xi = lax.associative_scan(complex_combine, (a_re, a_im, bu_re, bu_im),
                                            reverse=(di == 1), axis=1)
        y = y + (jnp.einsum('bsgp,gcp->bsgc', xr, cm_re[di].astype(jnp.float32))
                 - jnp.einsum('bsgp,gcp->bsgc', xi, cm_im[di].astype(jnp.float32)))
    y = jax.nn.gelu(y.reshape(Bsz, S, W_S5))
    y = y * jax.nn.sigmoid(y @ glu_w.astype(jnp.float32) + glu_b.astype(jnp.float32))
    return rms_norm(y.astype(u.dtype), out_w)

def expert_ffn(xb, w1, b1, w2, b2):
    z = xb @ w1 + b1
    x_glu = jnp.minimum(z[..., ::2], SWIGLU_LIMIT)
    x_lin = jnp.clip(z[..., 1::2], -SWIGLU_LIMIT, SWIGLU_LIMIT)
    act = x_glu * jax.nn.sigmoid(SWIGLU_ALPHA * x_glu) * (x_lin + 1.0)
    return act @ w2 + b2

def moe(h, router_w, router_b, mlp1_w, mlp1_b, mlp2_w, mlp2_b):
    B, S, D = h.shape
    T = B * S
    ht = h.reshape(T, D)
    logits = (ht @ router_w + router_b).astype(jnp.float32)
    top_vals, top_idx = lax.top_k(logits, TOP_K)
    gates = jax.nn.softmax(top_vals, axis=-1)
    n_assign = T * TOP_K
    flat_e = top_idx.reshape(-1).astype(jnp.int32)
    flat_tok = jnp.arange(n_assign, dtype=jnp.int32) // TOP_K
    flat_g = gates.reshape(-1)
    order = jnp.argsort(flat_e, stable=True)
    sorted_e = flat_e[order]
    sorted_tok = flat_tok[order]
    sorted_g = flat_g[order]
    counts = jnp.bincount(flat_e, length=N_EXPERTS).astype(jnp.int32)
    padded = ((counts + MOE_BLOCK - 1) // MOE_BLOCK) * MOE_BLOCK
    pad_end = jnp.cumsum(padded)
    pad_start = pad_end - padded
    start = jnp.cumsum(counts) - counts
    dest = pad_start[sorted_e] + jnp.arange(n_assign, dtype=jnp.int32) - start[sorted_e]
    n_rows = n_assign + N_EXPERTS * MOE_BLOCK
    n_blocks = n_rows // MOE_BLOCK
    xs = jnp.zeros((n_rows, D), h.dtype).at[dest].set(ht[sorted_tok])
    block_e = jnp.minimum(
        jnp.searchsorted(pad_end, jnp.arange(n_blocks, dtype=jnp.int32) * MOE_BLOCK, side='right'),
        N_EXPERTS - 1).astype(jnp.int32)

    def run(args):
        xb, e = args
        return expert_ffn(xb, mlp1_w[e], mlp1_b[e], mlp2_w[e], mlp2_b[e])

    ys = lax.map(run, (xs.reshape(n_blocks, MOE_BLOCK, D), block_e)).reshape(n_rows, D)
    y = ys[dest] * sorted_g[:, None].astype(ys.dtype)
    out = jnp.zeros((T, D), h.dtype).at[sorted_tok].add(y.astype(h.dtype))
    return out.reshape(B, S, D)

def setup_inputs(seed: int = 0) -> dict:
    key = jax.random.key(seed)
    ks = jax.random.split(key, 40)
    L = DEPTH
    f32 = jnp.float32

    def nrm(k, shape, s):
        return jax.random.normal(k, shape, f32) * s

    n_idx = jnp.arange(S5_STATE, dtype=f32)
    return {
        "x": nrm(ks[0], (BATCH, SEQ, D_MODEL), 1.0),
        "c": nrm(ks[1], (BATCH, D_MODEL), 1.0),
        "positions": (jnp.arange(SEQ, dtype=jnp.int32)[None, :]
                      + jax.random.randint(ks[2], (BATCH, 1), 0, POS_OFFSET_MAX, dtype=jnp.int32)),
        "ada_w": nrm(ks[3], (L, D_MODEL, 6 * D_MODEL), D_MODEL ** -0.5),
        "ada_b": nrm(ks[4], (L, 6 * D_MODEL), 0.02),
        "norm1_w": 1.0 + nrm(ks[5], (L, D_MODEL), 0.02),
        "w_in": nrm(ks[6], (L, D_MODEL, D_IN_PROJ), D_MODEL ** -0.5),
        "q_norm_w": 1.0 + nrm(ks[7], (L, ATTN_QK_DIM), 0.02),
        "k_norm_w": 1.0 + nrm(ks[8], (L, ATTN_QK_DIM), 0.02),
        "lambda_q1": nrm(ks[9], (L, ATTN_QK_DIM), 0.1),
        "lambda_k1": nrm(ks[10], (L, ATTN_QK_DIM), 0.1),
        "lambda_q2": nrm(ks[11], (L, ATTN_QK_DIM), 0.1),
        "lambda_k2": nrm(ks[12], (L, ATTN_QK_DIM), 0.1),
        "subln_w": 1.0 + nrm(ks[13], (L, ATTN_V_DIM), 0.02),
        "s5_lambda_re": -0.5 + nrm(ks[14], (L, 2, S5_GROUPS, S5_STATE), 0.01),
        "s5_lambda_im": math.pi * n_idx + nrm(ks[15], (L, 2, S5_GROUPS, S5_STATE), 0.01),
        "s5_log_step": jax.random.uniform(ks[16], (L, 2, S5_GROUPS), f32,
                                          math.log(S5_MIN_STEP), math.log(S5_MAX_STEP)),
        "s5_b_re": nrm(ks[17], (L, 2, S5_GROUPS, S5_STATE, S5_GROUP_CH), (2 * S5_GROUP_CH) ** -0.5),
        "s5_b_im": nrm(ks[18], (L, 2, S5_GROUPS, S5_STATE, S5_GROUP_CH), (2 * S5_GROUP_CH) ** -0.5),
        "s5_cmat_re": nrm(ks[19], (L, 2, S5_GROUPS, S5_GROUP_CH, S5_STATE), (2 * S5_STATE) ** -0.5),
        "s5_cmat_im": nrm(ks[20], (L, 2, S5_GROUPS, S5_GROUP_CH, S5_STATE), (2 * S5_STATE) ** -0.5),
        "s5_d": nrm(ks[21], (L, W_S5), 1.0),
        "s5_glu_w": nrm(ks[22], (L, W_S5, W_S5), W_S5 ** -0.5),
        "s5_glu_b": nrm(ks[23], (L, W_S5), 0.02),
        "s5_out_norm_w": 1.0 + nrm(ks[24], (L, W_S5), 0.02),
        "w_out": nrm(ks[25], (L, D_MIX, D_MODEL), D_MIX ** -0.5),
        "norm2_w": 1.0 + nrm(ks[26], (L, D_MODEL), 0.02),
        "router_w": nrm(ks[27], (L, D_MODEL, N_EXPERTS), D_MODEL ** -0.5),
        "router_b": nrm(ks[28], (L, N_EXPERTS), 0.01),
        "mlp1_w": nrm(ks[29], (L, N_EXPERTS, D_MODEL, 2 * D_FF), D_MODEL ** -0.5),
        "mlp1_b": nrm(ks[30], (L, N_EXPERTS, 2 * D_FF), 0.02),
        "mlp2_w": nrm(ks[31], (L, N_EXPERTS, D_FF, D_MODEL), D_FF ** -0.5),
        "mlp2_b": nrm(ks[32], (L, N_EXPERTS, D_MODEL), 0.02),
    }

def reference(x, c, positions, ada_w, ada_b, norm1_w, w_in, q_norm_w, k_norm_w,
              lambda_q1, lambda_k1, lambda_q2, lambda_k2, subln_w,
              s5_lambda_re, s5_lambda_im, s5_log_step, s5_b_re, s5_b_im, s5_cmat_re, s5_cmat_im,
              s5_d, s5_glu_w, s5_glu_b, s5_out_norm_w, w_out, norm2_w,
              router_w, router_b, mlp1_w, mlp1_b, mlp2_w, mlp2_b):
    cos, sin = rope_tables(positions)
    c_act = jax.nn.silu(c)
    for l in range(DEPTH):
        mod = c_act @ ada_w[l] + ada_b[l]
        sh1, sc1, g1, sh2, sc2, g2 = jnp.split(mod[:, None, :], 6, axis=-1)
        h = rms_norm(x, norm1_w[l]) * (1.0 + sc1) + sh1
        proj = h @ w_in[l]
        q, k, v, u = jnp.split(proj, [W_ATTN_QK, 2 * W_ATTN_QK, 2 * W_ATTN_QK + W_ATTN], axis=-1)
        lambda_init = 0.8 - 0.6 * math.exp(-0.3 * l)
        lam = (jnp.exp(jnp.sum(lambda_q1[l].astype(jnp.float32) * lambda_k1[l].astype(jnp.float32)))
               - jnp.exp(jnp.sum(lambda_q2[l].astype(jnp.float32) * lambda_k2[l].astype(jnp.float32)))
               + lambda_init)
        a_out = diff_attention(q, k, v, cos, sin, q_norm_w[l], k_norm_w[l], lam, subln_w[l], lambda_init)
        s_out = s5_mixer(u, s5_lambda_re[l], s5_lambda_im[l], s5_log_step[l], s5_b_re[l], s5_b_im[l],
                         s5_cmat_re[l], s5_cmat_im[l], s5_d[l], s5_glu_w[l], s5_glu_b[l],
                         s5_out_norm_w[l])
        mix = jnp.concatenate([a_out, s_out], axis=-1) @ w_out[l]
        x = x + g1 * mix
        h2 = rms_norm(x, norm2_w[l]) * (1.0 + sc2) + sh2
        x = x + g2 * moe(h2, router_w[l], router_b[l], mlp1_w[l], mlp1_b[l], mlp2_w[l], mlp2_b[l])
    return x


_drawn_inputs = setup_inputs


def setup_inputs(seed=0):
    import zlib

    import numpy as np

    out = dict(_drawn_inputs(seed))
    spreads = {}
    factors = {'q_norm_w': 6.664,
     'k_norm_w': 8.0,
     'lambda_q1': 4.42,
     'lambda_k1': 4.609,
     'lambda_q2': 8.0,
     'lambda_k2': 2.94,
     'subln_w': 2.973,
     's5_lambda_re': 7.031,
     's5_glu_b': 3.702,
     's5_out_norm_w': 2.724,
     'mlp1_b': 6.79,
     'mlp2_b': 8.0}
    for name, (base, spread) in spreads.items():
        noise = np.random.default_rng([zlib.crc32(name.encode()), seed]).standard_normal(out[name].shape)
        drawn = base * np.exp(spread * noise) if base else spread * noise
        out[name] = __import__('jax').numpy.asarray(drawn.astype(out[name].dtype))
    for name, factor in factors.items():
        out[name] = (out[name] * factor).astype(out[name].dtype)
    return out
```

```python
import math
from contextlib import ExitStack

import numpy as np

import concourse.bass as bass
from concourse import mybir

F32 = mybir.dt.float32
BF16 = mybir.dt.bfloat16
I32 = mybir.dt.int32
U32 = mybir.dt.uint32
ALU = mybir.AluOpType
ACT = mybir.ActivationFunctionType
AX = mybir.AxisListType

P = 128
KIB = 1024
S, D = 512, 1024
KT = D // P
NT = S // P
HEADS, QK, DV = 8, 32, 64
ROT_HALF = 4
ROPE_THETA = 500000.0
STEPS = 8
CHUNKS = S // STEPS
GC, NG, NP = 16, 32, 64
DG = 2 * NG
E, TOPK, FF = 32, 4, 1024
MAXB = S * TOPK // P + E
EPS = 1e-6
LAMBDA_INIT = 0.8 - 0.6 * math.exp(0.0)
C1, C2 = 6.28125, 0.0019350051879882812
C3 = 2 * math.pi - C1 - C2
GELU_A, GELU_B = 2 * math.sqrt(2 / math.pi), 0.044715
ADA_CHUNKS = 6 * D // 512
U_CHUNK, Q_CHUNK, K_CHUNK, V_CHUNK = range(ADA_CHUNKS, ADA_CHUNKS + 4)
RING = 3
W1C, W2C = 16, 8
WCH = W1C + W2C
UNUSED = 4096.0
SBUF0 = 16512


def bc(ap, axis, n, shape):
    return ap.unsqueeze(axis).to_broadcast(shape)


class Chain:

    def __init__(self, eng, sem):
        self.eng, self.sem, self.n = eng, sem, 0

    def __call__(self, ins):
        self.n += 1
        ins.then_inc(self.sem, 1)
        self.eng.wait_ge(self.sem, self.n)

    def free(self, ins):
        self.n += 1
        ins.then_inc(self.sem, 1)

    def sync(self):
        self.eng.wait_ge(self.sem, self.n)


def program(nc, I, out):
    ctx = ExitStack()

    def at(name, kib, shape, dt=F32):
        return nc.alloc_sbuf_tensor_at(name, shape, dt, offset=SBUF0 + int(kib * KIB))

    def sem(name):
        return ctx.enter_context(nc.semaphore(name))

    with ctx:
        A, B, C, DD, EE, FV = 0, 64, 96, 132, 156, 172
        G = 196
        K0 = 204.5
        ident = at("ident", K0, [P, P])
        sgn = at("sgn", K0 + 0.5, [P, 4])
        ab8 = at("ab8", K0 + 0.5 + 0.0625, [P, 2, DG])
        cs = at("rope", K0 + 1.0625 + 0.0625, [P, 2, NT, ROT_HALF])
        qkw = at("qkw", K0 + 1.25, [P, 2, QK])
        subw = at("subw", K0 + 1.5, [P, DV])
        lamv = at("lamv", K0 + 1.75, [P, 16])
        dcol = at("dcol", K0 + 1.8125, [P, NG])
        glub = at("glub", K0 + 1.9375, [P, 4])
        outw = at("outw", K0 + 1.9375 + 0.03125, [P, 4])
        att_s = at("att_small", K0 + 2.0, [P, 2, 8])
        qk_s = at("qk_small", K0 + 2.0625, [P, 3, 2 * HEADS])
        sq_s = at("sq_small", K0 + 2.25, [P, 32])
        ring = at("dense_ring", A, [P, RING, KT, 512])
        toep = at("toeplitz", A + 48, [P, NG, P])
        cbc = at("c_bcast", A + 48, [P, KT, P])
        S1 = at("state_ri", A, [P, DG, CHUNKS])
        S2 = at("state_ir", A + 16, [P, DG, CHUNKS])
        scan_t = at("scan_tmp", A + 32, [P, 4, 256])
        Y = at("s5_y", A + 32, [P, NG, CHUNKS])
        aT = at("probs_T", A + 40, [P, 2, NT, P])
        o_n = at("o_norm", A + 44, [P, 2, 512])
        yT = at("y_T", A + 16, [P, 4, S])
        gluw = at("glu_w", A + 24, [P, 4, 512])
        sT = at("s_T", A, [P, 4, S])
        sqT = at("sq_T", A + 8, [P, 4, S])
        w1 = at("w1_ring", A, [P, W1C, 1024])
        inT = at("in_ops", B, [P, DG, P])
        wout = at("w_out", B, [P, KT, D])
        w2 = at("w2_ring", B, [P, W2C, 1024])
        outM = at("out_ops", C, [P, DG, STEPS + 1, GC])
        mod = at("modulation", DD, [P, 6, D])
        uT = at("u_T", DD, [P, 4, S])
        U = at("u_chunks", DD, [P, NG, CHUNKS])
        P2 = at("p2", EE, [P, GC, DG])
        Q2 = at("q2", EE + 4, [P, GC, DG])
        CP = at("cp", EE + 8, [P, DG, GC])
        CQ = at("cq", EE + 12, [P, DG, GC])
        BB = at("b_nat", FV, [DG, 3, NP * GC])
        tB = at("tmp_b", FV, [P, 1024])
        CC = at("c_nat", FV + 12, [P, 8, 3, NP])
        PW = at("powers", FV + 18, [P, 2, STEPS + 1, DG])
        t1 = at("tmp_1", FV + 22.5, [P, 1024])
        quad = at("quad", FV + 26.5, [DG, 4, 2, NP])
        AF = at("a_f", FV + 28.5, [P, 4, DG])
        lam_t = at("lam_tiles", FV + 22.5, [DG, 16, NP])
        kpad = at("kpad", FV, [GC, NG // 2, 15, GC])
        ccol = at("c_col", FV + 29.5, [P, 4, KT])
        lam_in = at("lam_in", FV + 29.625, [P, 4, QK])
        lam_w = at("lam_w", FV + 30.125, [P, 2, QK])
        posi = at("pos_i", FV + 30.5, [P, NT], I32)
        rope_t = at("rope_tmp", FV + 30.5625, [P, 8, NT, ROT_HALF])
        rope_i = at("rope_int", FV + 31.0625, [P, 64], I32)
        lstep = at("log_step", FV + 31.3125, [DG, 2])
        n1w = at("norm1_w", FV + 16, [P, D])
        hT = at("h_T", EE, [P, KT, S])
        catT = at("cat_T", EE, [P, 8, S])
        qkT = at("qk_T", FV, [P, 2, 4, S])
        vv = at("v", FV + 16, [P, NT, 512])
        xt = at("x_tile", G, [P, 2, D])
        stg = at("qk_stage", G, [P, 2, 512])
        sqb = at("qk_square", G + 4, [P, 2, 512])
        ee = at("probs", G, [P, 2, 2, 512])
        psq = at("chunk_powers", EE + 8, [P, 2, 9, DG])
        scan_w = at("power_tmp", EE + 12.5, [P, 4 * DG])
        xr = at("x_again", C, [P, 2, D])
        x1 = at("x1_tile", C + 8, [P, 2, D])
        h2 = at("h2_tile", C + 16, [P, 2, D])
        h2T = at("h2_T", C + 24, [P, KT, P])
        n2w = at("norm2_w", C + 28, [P, D])
        packed = [C + 32]

        def pack(name, shape, dt=F32):
            t = at(name, packed[0], shape, dt)
            packed[0] += -(-int(np.prod(shape[1:])) * (2 if dt == BF16 else 4) // 32) / 32
            assert packed[0] <= DD
            return t

        rw = pack("router_w", [P, KT, E])
        rb = pack("router_b", [P, E])
        lg = pack("logits", [P, E])
        mx8 = pack("max8", [P, 8])
        ix8 = pack("ix8", [P, 8], U32)
        ixf = pack("ixf", [P, 8])
        gat = pack("gates", [P, NT, TOPK])
        gs = pack("gate_sum", [P, 8])
        iotaE = pack("iota_e", [P, MAXB])
        tri = pack("tri", [P, P], BF16)
        onb = pack("ones_bf", [P, P], BF16)
        mask = pack("mask", [P, NT, E], BF16)
        oh4 = at("onehot4", FV + 18, [P, NT, TOPK, E])
        slotE = at("slot_e", EE + 2, [P, NT, E])
        rt = at("route_tmp", EE + 2.5, [P, 8, E])
        cmpb = at("block_cmp", EE + 4, [P, MAXB, E])
        prod = at("route_prod", EE + 10, [P, NT * TOPK, E])
        tokid = pack("tok_id", [P, NT * TOPK, 4], BF16)
        dslot = pack("slots", [P, NT * TOPK])
        ebf = pack("expert_f", [P, MAXB + 2])
        ebi = pack("expert_i", [P, MAXB + 2], I32)
        nbi = pack("n_blocks", [P, 2], I32)
        eye96 = pack("sel_cols", [96, MAXB + 2], BF16)
        pm = pack("part_mod", [P, 4])
        ones = pack("ones", [P, P])
        xs = at("xs", EE, [P, D])
        xT = at("xs_T", EE + 4, [P, KT, P])
        actT = at("act_T", EE + 8, [P, KT, P])
        ysb = at("y_rows_sb", EE + 12, [P, D])
        glu = at("glu", FV, [P, 3, 512])
        lin = at("lin", FV + 6, [P, 3, 512])
        bsrc = at("b_src", FV, [96, 3072])
        bcat = at("b_cat", FV + 12, [96, 3072], BF16)
        ohs = at("slot_onehot", FV + 18, [P, NT * TOPK, P], BF16)
        iotab = at("iota_slots", FV + 22, [P, P])
        selb = at("expert_sel", FV + 22.5, [96, P], BF16)
        idx = at("row_idx", FV + 22.75, [P, 4], I32)
        idf = at("row_idx_f", FV + 22.8125, [P, 2])
        fing = at("final_rows", A, [P, 16, D])
        fx1 = at("final_x1", B, [P, NT, D])
        facc = at("final_acc", B + 16, [P, NT, D])
        bank = [ctx.enter_context(nc.psum_tensor(f"bank{i}", [P, 512], F32)) for i in range(8)]

        dram = {n: nc.dram_tensor(n, sh, F32, kind="Internal").ap() for n, sh in {
            "u_rows": [512, 512], "y_rows": [512, 512], "x1_rows": [S, D], "h2_rows": [S, D],
            "ys_rows": [S * TOPK, D]}.items()}

        names = """ident_ready  s5_nat lam_loaded c_loaded adab_loaded x_loaded0 x_loaded1 n1w_loaded misc_loaded
          pe_prep cq_ready bx_ready quad_ready af_psum af_ready inraw_ready in_tr in_done outm_ready k_mm k_ev kp_half
           sg_ready cbc_ready ada_mm ada_ev dve act pool   lam_e act_lam act_trig act_rope
          sq1 rs1 h_ready h_tr h_ev u_mm u_ev u_stored u_loaded q_mm q_sq q_ss q_rt q_n q_tr q_ev v_ev s_mm s_ev scan_done
          sc_mm sc_max sc_exp a_ready a_tr a_ev pv_mm o_sq o_ss o_rt o_n o_tr o_ev 
          y_mm y_ev y_gp y_sig y_done y_stored y_loaded gluw_loaded g_mm g_sig s_act s_sq n_mm n_rt s5_done
          wout_loaded xr_loaded0 xr_loaded1 n2w_loaded rw_loaded mix_mm x1_ready x1_stored0 x1_stored1 m_sq m_rt h2_ready h2_stored0 h2_stored1 h2_tr h2_ev
          r_mm lg_ready g_exp mask_ready pos_mm blocks_ready consts2 bias_src bias_ready d_ready
          oh_ready idx_mm idx_ready xs_loaded idx_sum scat_ready x_tr0 x_tr1 x_ev0 x_ev1 sel_ready  
          g_min0 g_min1 g_sg0 g_sg1 l_a0 l_a1 l_b0 l_b1 act_ready0 act_ready1 a_tr0 a_tr1 a_ev0 a_ev1  y2_ev y2_stored
          fin_g0 fin_g1 fin_g2 fin_g3 fin_x1 fin_done fin_stored""".split()
        s = {n: sem(n) for n in names}
        ring_sem = [sem(f"ring_loaded{i}") for i in range(RING)]
        w_loaded = [sem(f"w_loaded{c}") for c in range(WCH // 2)]
        w_used = sem("w_used")
        ctx.enter_context(nc.allow_non_contiguous_dma(reason="vectors of a few hundred words"))
        ctx.enter_context(nc.allow_low_precision(reason="sums of a one and zeros, or small whole numbers"))
        block = ctx.enter_context(nc.Block())

        ada_v = I["ada_w"][0].rearrange("(k p) n -> p k n", p=P)
        win_v = I["w_in"][0].rearrange("(k p) n -> p k n", p=P)
        xv = I["x"][0].rearrange("(j i) d -> i j d", i=STEPS)
        ov = out[0].rearrange("(j i) d -> i j d", i=STEPS)

        @block.sync
        def _(sp):
            for k, n in enumerate(("s5_cmat_re", "s5_cmat_im", "s5_cmat_re")):
                sp.dma_start(CC[:, :, k, :], I[n][0].rearrange("d g c p -> (d g c) p")
                             .rearrange("(t q) p -> q t p", q=P)).then_inc(s["s5_nat"], 16)
            for k, n in enumerate(("s5_b_re", "s5_b_im", "s5_b_re")):
                sp.dma_start(BB[:, k, :], I[n][0].rearrange("d g p c -> (d g) (p c)")).then_inc(s["s5_nat"], 16)
            sp.dma_start(lam_t[:, 0, :], I["s5_lambda_re"][0].rearrange("d g p -> (d g) p")).then_inc(s["lam_loaded"], 16)
            sp.dma_start(lam_t[:, 1, :], I["s5_lambda_im"][0].rearrange("d g p -> (d g) p")).then_inc(s["lam_loaded"], 16)
            sp.dma_start(lstep[:, 0:1], I["s5_log_step"][0].rearrange("d (g o) -> (d g) o", o=1)).then_inc(s["lam_loaded"], 16)
            w_in_at = {U_CHUNK: 3, Q_CHUNK: 0, K_CHUNK: 1, V_CHUNK: 2}

            def dense(n):
                if n - RING >= ADA_CHUNKS:
                    sp.wait_ge(s["u_mm"], 4)
                elif n >= RING:
                    sp.wait_ge(s["ada_mm"], n - RING + 1)
                src = ada_v[:, :, n * 512:(n + 1) * 512] if n < ADA_CHUNKS else \
                    win_v[:, :, w_in_at[n] * 512:(w_in_at[n] + 1) * 512]
                sp.dma_start(ring[:, n % RING], src).then_inc(ring_sem[n % RING], 16)
            for n in range(V_CHUNK):
                dense(n)
                if n == 0:
                    sp.dma_start(mod[:].rearrange("p a d -> p (a d)"),
                                 I["ada_b"][0].partition_broadcast(P)).then_inc(s["adab_loaded"], 16)
            for half in range(2):
                sp.wait_ge(s["k_ev"], 8 * (half + 1))
                if half == 0:
                    sp.wait_ge(s["ada_mm"], ADA_CHUNKS)
                gsl = slice(half * NG // 2, (half + 1) * NG // 2)
                for i in range(STEPS):
                    sp.dma_start(toep[i * GC:(i + 1) * GC, gsl, :].rearrange("p g (a c) -> p g a c", c=GC),
                                 kpad[:, :, 7 - i:15 - i, :]).then_inc(s["kp_half"], 16)
                if half == 0:
                    sp.wait_ge(s["kp_half"], 16 * STEPS)
            sp.wait_ge(s["inraw_ready"], 1)
            sp.wait_ge(s["outm_ready"], 1)
            sp.dma_start(n1w[:], I["norm1_w"][0].partition_broadcast(P)).then_inc(s["n1w_loaded"], 16)
            for t in range(NT):
                if t >= 2:
                    sp.wait_ge(s["h_tr"], t - 1)
                for k in range(2):
                    sp.dma_start(xt[64 * k:64 * k + 64, t % 2, :], xv[2 * t + k]).then_inc(s[f"x_loaded{t % 2}"], 16)
            dense(V_CHUNK)
            sp.wait_ge(s["u_ev"], 4)
            sp.dma_start(dram["u_rows"].rearrange("(t p) n -> p t n", p=P), uT[:]).then_inc(s["u_stored"], 16)
            sp.wait_ge(s["u_stored"], 16)
            u_v = dram["u_rows"].rearrange("(g c) (i j) -> i c g j", c=GC, i=STEPS)
            for i in range(STEPS):
                sp.dma_start(U[i * GC:(i + 1) * GC], u_v[i]).then_inc(s["u_loaded"], 16)
            sp.wait_ge(s["s_mm"], 2 * DG // 8)
            sp.dma_start(wout[:], I["w_out"][0].rearrange("(k p) n -> p k n", p=P)).then_inc(s["wout_loaded"], 16)
            sp.wait_ge(s["scan_done"], 2)
            sp.dma_start(gluw[:], I["s5_glu_w"][0].rearrange("(k p) n -> p k n", p=P)).then_inc(s["gluw_loaded"], 16)
            sp.wait_ge(s["y_done"], 1)
            y_v = dram["y_rows"].rearrange("(g c) (i j) -> i c g j", c=GC, i=STEPS)
            for i in range(STEPS):
                sp.dma_start(y_v[i], Y[i * GC:(i + 1) * GC]).then_inc(s["y_stored"], 16)
            sp.wait_ge(s["y_stored"], 128)
            sp.dma_start(yT[:], dram["y_rows"].rearrange("(t p) n -> p t n", p=P)).then_inc(s["y_loaded"], 16)
            sp.dma_start(n2w[:], I["norm2_w"][0].partition_broadcast(P)).then_inc(s["n2w_loaded"], 16)
            sp.dma_start(rw[:], I["router_w"][0].rearrange("(k p) n -> p k n", p=P)).then_inc(s["rw_loaded"], 16)
            sp.dma_start(rb[:], I["router_b"][0].partition_broadcast(P)).then_inc(s["rw_loaded"], 16)
            sp.wait_ge(s["pv_mm"], NT * HEADS)
            for q in range(3):
                sp.dma_start(bsrc[32 * q:32 * q + 32, 0:2048], I["mlp1_b"][0]).then_inc(s["bias_src"], 16)
                sp.dma_start(bsrc[32 * q:32 * q + 32, 2048:3072], I["mlp2_b"][0]).then_inc(s["bias_src"], 16)
            for t in range(NT):
                if t >= 2:
                    sp.wait_ge(s["x1_ready"], t - 1)
                for k in range(2):
                    sp.dma_start(xr[64 * k:64 * k + 64, t % 2, :], xv[2 * t + k]).then_inc(s[f"xr_loaded{t % 2}"], 16)
                sp.wait_ge(s["x1_ready"], t + 1)
                sp.dma_start(dram["x1_rows"][t * P:(t + 1) * P, :], x1[:, t % 2, :]).then_inc(s[f"x1_stored{t % 2}"], 16)
                sp.wait_ge(s["h2_ready"], t + 1)
                sp.dma_start(dram["h2_rows"][t * P:(t + 1) * P, :], h2[:, t % 2, :]).then_inc(s[f"h2_stored{t % 2}"], 16)
            sp.wait_ge(s["s5_done"], 4)
            sp.wait_ge(s["mix_mm"], NT)
            sp.wait_ge(s["blocks_ready"], 1)
            n_blocks = sp.value_load(nbi[0:1, 0:1], min_val=1, max_val=MAXB)

            def weights(e, b):
                for c in range(W1C):
                    if b is not None:
                        sp.wait_ge(w_used, b * WCH + (c + 1 - WCH))
                    half, k = c // KT, c % KT
                    sp.dma_start(w1[:, c, :], I["mlp1_w"][0, bass.ds(e, 1), k * P:(k + 1) * P,
                                                          half * 1024:half * 1024 + 1024]
                                 .rearrange("e p n -> (e p) n")).then_inc(w_loaded[c // 2], 16)
                for k in range(W2C):
                    if b is not None:
                        sp.wait_ge(w_used, b * WCH + (W1C + k + 1 - WCH))
                    sp.dma_start(w2[:, k, :], I["mlp2_w"][0, bass.ds(e, 1), k * P:(k + 1) * P, :]
                                 .rearrange("e p n -> (e p) n")).then_inc(w_loaded[(W1C + k) // 2], 16)

            weights(sp.value_load(ebi[0:1, 0:1], min_val=0, max_val=E - 1), None)
            with sp.Fori(1, n_blocks) as b:
                weights(sp.value_load(ebi[0:1, bass.ds(b, 1)], min_val=0, max_val=E - 1), b)
            sp.wait_ge(s["y2_stored"], n_blocks * 16)
            for t in range(NT):
                sp.dma_start(fing[:, TOPK * t:TOPK * t + TOPK, :].rearrange("p k d -> p (k d)"),
                             dram["ys_rows"][t * P * TOPK:(t + 1) * P * TOPK, :]
                             .rearrange("(p k) d -> p (k d)", k=TOPK)).then_inc(s[f"fin_g{t}"], 16)
            sp.dma_start(fx1[:], dram["x1_rows"].rearrange("(t p) n -> p t n", p=P)).then_inc(s["fin_x1"], 16)
            for t in range(NT):
                sp.wait_ge(s["fin_done"], t + 1)
                for k in range(2):
                    sp.dma_start(ov[2 * t + k], facc[64 * k:64 * k + 64, t, :]).then_inc(s["fin_stored"], 16)
            sp.wait_ge(s["fin_stored"], 32 * NT)

        @block.gpsimd
        def _(pool):
            ch = Chain(pool, s["pool"])
            ch(pool.memset(ident[:], 0.0))
            ch(pool.memset(ones[:], 1.0))
            pool.affine_select(out=ident[:], in_=ident[:], compare_op=ALU.not_equal, fill=1.0, base=0,
                               pattern=[[-1, P]], channel_multiplier=1).then_inc(s["ident_ready"], 1)
            pool.wait_ge(s["ident_ready"], 1)
            ch(pool.memset(sgn[0:64, 0:1], -1.0))
            ch(pool.memset(sgn[64:128, 0:1], 1.0))
            ch(pool.memset(sgn[0:64, 1:2], 1.0))
            ch(pool.memset(sgn[64:128, 1:2], -1.0))
            ch(pool.memset(sgn[:, 2:3], EPS))
            ch.sync()
            pool.dma_start(lam_in[:, 0], I["lambda_q1"][0].partition_broadcast(P)).then_inc(s["misc_loaded"], 16)
            pool.dma_start(lam_in[:, 1], I["lambda_q2"][0].partition_broadcast(P)).then_inc(s["misc_loaded"], 16)
            pool.dma_start(lam_in[:, 2], I["lambda_k1"][0].partition_broadcast(P)).then_inc(s["misc_loaded"], 16)
            pool.dma_start(lam_in[:, 3], I["lambda_k2"][0].partition_broadcast(P)).then_inc(s["misc_loaded"], 16)
            pool.dma_start(qkw[:, 0], I["q_norm_w"][0].partition_broadcast(P)).then_inc(s["misc_loaded"], 16)
            pool.dma_start(qkw[:, 1], I["k_norm_w"][0].partition_broadcast(P)).then_inc(s["misc_loaded"], 16)
            pool.dma_start(subw[:], I["subln_w"][0].partition_broadcast(P)).then_inc(s["misc_loaded"], 16)
            pos_v = I["positions"][0].rearrange("(j i o) -> i j o", i=STEPS, o=1)
            for i in range(STEPS):
                pool.dma_start(posi[64 * (i % 2):64 * (i % 2) + 64, i // 2:i // 2 + 1], pos_v[i]).then_inc(s["misc_loaded"], 16)
                pool.dma_start(dcol[i * GC:(i + 1) * GC, :], I["s5_d"][0].rearrange("(g c) -> c g", c=GC)).then_inc(s["misc_loaded"], 16)
            pool.dma_start(glub[:], I["s5_glu_b"][0].rearrange("(t p) -> p t", p=P)).then_inc(s["misc_loaded"], 16)
            pool.dma_start(outw[:], I["s5_out_norm_w"][0].rearrange("(t p) -> p t", p=P)).then_inc(s["misc_loaded"], 16)
            pool.dma_start(ccol[:, 0, :], I["c"][0].rearrange("(t p) -> p t", p=P)).then_inc(s["c_loaded"], 16)
            pool.wait_ge(s["v_ev"], 4)

            def cmul(dst, x, y, n):
                X = [psq[:, q, x:x + n, :] for q in range(2)]
                Yb = [bc(psq[:, q, y, :], 1, n, [P, n, DG]) for q in range(2)]
                T = scan_w[:, 0:n * DG].rearrange("p (n g) -> p n g", g=DG)
                O = [psq[:, q, dst:dst + n, :] for q in range(2)]
                ch(pool.tensor_tensor(O[0], X[0], Yb[0], ALU.mult))
                ch(pool.tensor_tensor(T, X[1], Yb[1], ALU.mult))
                ch(pool.tensor_tensor(O[0], O[0], T, ALU.subtract))
                ch(pool.tensor_tensor(O[1], X[0], Yb[1], ALU.mult))
                ch(pool.tensor_tensor(T, X[1], Yb[0], ALU.mult))
                ch(pool.tensor_tensor(O[1], O[1], T, ALU.add))

            pool.wait_ge(s["sg_ready"], 1)
            ch(pool.tensor_copy(psq[:, 0, 1, :], ab8[:, 0, :]))
            ch(pool.tensor_copy(psq[:, 1, 1, :], ab8[:, 1, :]))
            cmul(2, 1, 1, 1)
            cmul(3, 1, 2, 2)
            cmul(5, 1, 4, 4)
            pool.wait_ge(s["s_ev"], 2 * DG // 8)
            dirs = ((0, range(1, 8), -1), (1, range(6, -1, -1), 1))

            def view(T, di):
                return T[:, di * NG:(di + 1) * NG, :].rearrange("p g (c m) -> p g c m", m=8)

            def step(x1n, x2n, x1p, x2p, are, aim, sub, shape, keep2=True):
                T = [scan_t[:, q, 0:int(np.prod(shape))].rearrange("p (g c) -> p g c", g=NG) for q in range(4)]
                ch(pool.tensor_tensor(T[0], x1p, are, ALU.mult))
                if keep2:
                    ch(pool.tensor_tensor(T[2], x2p, are, ALU.mult))
                    ch(pool.tensor_tensor(T[3], x1p, aim, ALU.mult))
                ch(pool.tensor_tensor(T[1], x2p, aim, ALU.mult))
                ch(pool.tensor_tensor(x1n, x1n, T[0], ALU.add))
                if keep2:
                    ch(pool.tensor_tensor(x2n, x2n, T[2], ALU.add))
                ch.sync()
                if keep2:
                    ch(pool.tensor_tensor(x2n, x2n, T[3], ALU.subtract))
                ch(pool.tensor_tensor(x1n, x1n, T[1], ALU.add))

            for di, order, back in dirs:
                V1, V2 = view(S1, di), view(S2, di)
                gs_ = slice(di * NG, (di + 1) * NG)

                def pw(q, k, n):
                    return bc(psq[:, q, k, gs_], 2, n, [P, NG, n])
                for m in order:
                    step(V1[:, :, :, m], V2[:, :, :, m], V1[:, :, :, m + back], V2[:, :, :, m + back],
                         pw(0, 1, 8), pw(1, 1, 8), None, [NG, 8])
                end = 7 if di == 0 else 0
                for c in (range(1, 8) if di == 0 else range(6, -1, -1)):
                    step(V1[:, :, c:c + 1, end], V2[:, :, c:c + 1, end], V1[:, :, c + back:c + back + 1, end],
                         V2[:, :, c + back:c + back + 1, end], pw(0, 8, 1), pw(1, 8, 1), None, [NG, 1])
                for m in range(7) if di == 0 else range(7, 0, -1):
                    k = m + 1 if di == 0 else 8 - m
                    dst = slice(1, 8) if di == 0 else slice(0, 7)
                    src = slice(0, 7) if di == 0 else slice(1, 8)
                    step(V1[:, :, dst, m], None, V1[:, :, src, end], V2[:, :, src, end],
                         pw(0, k, 7), pw(1, k, 7), None, [NG, 7], keep2=False)
                pool.nop().then_inc(s["scan_done"], 1)
            pool.wait_ge(s["y_ev"], 4)
            ch(pool.iota(iotaE[:], pattern=[[1, MAXB]], base=0, channel_multiplier=0, allow_small_or_imprecise_dtypes=True))
            ch(pool.memset(onb[:], 1.0))
            ch(pool.memset(tri[:], 1.0))
            ch(pool.memset(ones[:], 1.0))
            for q in range(3):
                ch(pool.iota(pm[32 * q:32 * q + 32, 0:1], pattern=[[1, 1]], base=0, channel_multiplier=1, allow_small_or_imprecise_dtypes=True))
            for col, pat, mult in ((0, [[0, NT], [0, TOPK]], 4), (1, [[TOPK * P, NT], [0, TOPK]], 0),
                                   (2, [[0, NT], [1, TOPK]], 0)):
                ch(pool.iota(tokid[:, :, col].rearrange("p (t k) -> p t k", k=TOPK), pattern=pat, base=0,
                             channel_multiplier=mult, allow_small_or_imprecise_dtypes=True))
            ch(pool.memset(tokid[:, :, 3:4], -UNUSED))
            ch.sync()
            pool.affine_select(out=tri[:], in_=tri[:], compare_op=ALU.is_gt, fill=0.0, base=0,
                               pattern=[[1, P]], channel_multiplier=-1).then_inc(s["consts2"], 1)
            pool.wait_ge(s["bias_src"], 96)
            ch(pool.tensor_copy(bcat[:], bsrc[:]))
            for q in (1, 2):
                ch(pool.tensor_tensor(bsrc[32 * q:32 * q + 32], bsrc[32 * q:32 * q + 32],
                                           bcat[32 * q:32 * q + 32], ALU.subtract))
            ch.sync()
            for q in (1, 2):
                ch(pool.tensor_copy(bcat[32 * q:32 * q + 32], bsrc[32 * q:32 * q + 32]))
            ch.sync()
            ch(pool.tensor_tensor(bsrc[64:96], bsrc[64:96], bcat[64:96], ALU.subtract))
            pool.tensor_copy(bcat[64:96], bsrc[64:96]).then_inc(s["bias_ready"], 1)
            pool.wait_ge(s["bias_ready"], 1)
            pool.iota(iotab[:], pattern=[[1, P]], base=0, channel_multiplier=0,
                      allow_small_or_imprecise_dtypes=True).then_inc(s["bias_ready"], 1)
            pool.wait_ge(s["h2_stored0"], 32)
            pool.wait_ge(s["h2_stored1"], 32)
            pool.wait_ge(s["blocks_ready"], 1)
            n_blocks = pool.value_load(nbi[0:1, 0:1], min_val=1, max_val=MAXB)

            last_token, last_row = pool.to_reg(S - 1), pool.to_reg(S * TOPK - 1)

            def gather(n2):
                pool.wait_ge(s["idx_ready"], n2)
                pool.sem_inc(s["pool"], 1)
                pool.indirect_dma_start(out=xs[:], out_offset=None, in_=dram["h2_rows"],
                                        in_offset=bass.IndirectOffsetOnAxis(ap=idx[:, 0:1], axis=0),
                                        bounds_check=last_token).then_inc(s["xs_loaded"], 16)
            gather(2)
            with pool.Fori(0, n_blocks) as b:
                v, next2 = b + 1, b * 2 + 4
                pool.wait_ge(s["x_tr1"], v)
                gather(next2)
                pool.wait_ge(s["y2_ev"], next2)
                pool.wait_ge(s["scat_ready"], v)
                pool.sem_inc(s["pool"], 1)
                pool.indirect_dma_start(out=dram["ys_rows"], in_=ysb[:], in_offset=None,
                                        out_offset=bass.IndirectOffsetOnAxis(ap=idx[:, 2:3], axis=0),
                                        bounds_check=last_row, oob_is_err=False).then_inc(s["y2_stored"], 16)
        @block.scalar
        def _(act):
            ch = Chain(act, s["act"])
            act.wait_ge(s["c_loaded"], 16)
            act.activation(ccol[:, 1, :], ccol[:, 0, :], ACT.Sigmoid).then_inc(s["lam_e"], 1)
            act.wait_ge(s["ident_ready"], 1)
            act.wait_ge(s["pool"], 7)
            act.wait_ge(s["pe_prep"], 1)
            for b in range(2):
                ch.free(act.activation(CP[:].rearrange("p g c -> p (g c)")[:, 512 * b:512 * b + 512], bank[b][:], ACT.Identity,
                                       scale=sgn[:, 1:2]))
                act.activation(CQ[:].rearrange("p g c -> p (g c)")[:, 512 * b:512 * b + 512], bank[2 + b][:], ACT.Identity,
                               scale=-1.0).then_inc(s["cq_ready"], 1)
            ch.sync()
            act.wait_ge(s["pe_prep"], 2)
            for b in range(2):
                act.activation(P2[:].rearrange("p c g -> p (c g)")[:, 512 * b:512 * b + 512], bank[4 + b][:], ACT.Identity).then_inc(s["bx_ready"], 1)
                act.activation(Q2[:].rearrange("p c g -> p (c g)")[:, 512 * b:512 * b + 512], bank[6 + b][:], ACT.Identity,
                               scale=sgn[:, 0:1]).then_inc(s["bx_ready"], 1)
            act.wait_ge(s["lam_loaded"], 48)
            ch(act.activation(lstep[:, 1:2], lstep[:, 0:1], ACT.Exp))
            act.activation(lam_t[:, 2, :], lam_t[:, 0, :], ACT.Exp, scale=lstep[:, 1:2]).then_inc(s["act_lam"], 1)
            act.wait_ge(s["act_rope"], 1)
            act.activation(lamv[:, 2:4], lamv[:, 0:2], ACT.Exp).then_inc(s["act_lam"], 1)
            act.wait_ge(s["act_trig"], 1)
            act.activation(lam_t[:, 4:6, :], lam_t[:, 4:6, :], ACT.Sin).then_inc(s["lam_e"], 1)
            act.wait_ge(s["act_rope"], 2)
            act.activation(cs[:].rearrange("p a t k -> p (a t k)"), rope_t[:, 0:2].rearrange("p a t k -> p (a t k)"),
                           ACT.Sin).then_inc(s["lam_e"], 1)
            act.wait_ge(s["af_psum"], 1)
            act.activation(AF[:].rearrange("p a g -> p (a g)"), bank[2][:, 0:4 * DG], ACT.Identity).then_inc(s["af_ready"], 1)
            for n in range(DG // 4):
                act.wait_ge(s["in_tr"], n + 1)
                act.activation(inT[:, 4 * n:4 * n + 4, :].rearrange("p g m -> p (g m)"), bank[2 + n % 4][:], ACT.Identity).then_inc(s["in_done"], 1)
            for n in range(NG // 2):
                act.wait_ge(s["k_mm"], n + 1)
                if n == 8:
                    act.wait_ge(s["kp_half"], 16 * STEPS)
                act.activation(kpad[:, 2 * (n % 8):2 * (n % 8) + 2].rearrange("p g a c -> p (g a c)"),
                               bank[6 + n % 2][0:GC, 0:480], ACT.Identity).then_inc(s["k_ev"], 1)
            for t in range(NT):
                act.wait_ge(s[f"x_loaded{t % 2}"], 32 * (t // 2 + 1))
                if t:
                    act.wait_ge(s["rs1"], t)
                for k in range(2):
                    ch.free(act.activation(bank[6 + k][:], xt[:, t % 2, 512 * k:512 * k + 512], ACT.Square,
                                           accum_out=sq_s[:, k:k + 1]))
                ch.sync()
                act.nop().then_inc(s["sq1"], 1)
                act.wait_ge(s["m_sq"], t + 1)
                act.activation(sq_s[:, 3:4], sq_s[:, 2:3], ACT.Sqrt, scale=1.0 / D, bias=sgn[:, 2:3]).then_inc(s["sq1"], 1)
                act.wait_ge(s["h_tr"], t + 1)
                for k in range(2):
                    act.activation(hT[:, 4 * k:4 * k + 4, t * P:(t + 1) * P],
                                   bank[2 * (t % 2) + k][:].rearrange("p (k n) -> p k n", n=P), ACT.Identity).then_inc(s["h_ev"], 1)
            for n in range(4):
                act.wait_ge(s["u_mm"], n + 1)
                act.activation(uT[:, n, :], bank[n][:], ACT.Identity).then_inc(s["u_ev"], 1)
            def qk_rms(n):
                bk = bank[4 + n] if n < 4 else bank[n - 4]
                act.wait_ge(s["q_mm"], n + 1)
                if n >= 2:
                    act.wait_ge(s["q_ss"], n - 1)
                act.activation(sqb[:, n % 2, :], bk[:], ACT.Square).then_inc(s["q_sq"], 1)
                act.wait_ge(s["q_ss"], n + 1)
                act.activation(qk_s[:, 1, :], qk_s[:, 0, :], ACT.Sqrt, scale=1.0 / QK, bias=sgn[:, 2:3]).then_inc(s["q_rt"], 1)

            def qk_out(n):
                act.wait_ge(s["q_tr"], n + 1)
                bk = bank[4 + n] if n < 4 else bank[n - 4]
                act.activation(qkT[:, n // 4, :, (n % 4) * P:(n % 4) * P + P],
                               bk[:].rearrange("p (b n) -> p b n", n=P), ACT.Identity).then_inc(s["q_ev"], 1)
            for n in range(8):
                qk_rms(n)
                qk_out(n)
            for n in range(4):
                act.wait_ge(s["q_mm"], 8 + n + 1)
                act.activation(vv[:, n, :], bank[4 + n][:], ACT.Identity).then_inc(s["v_ev"], 1)
            for n in range(DG // 8):
                for k in range(2):
                    act.wait_ge(s["s_mm"], 2 * n + k + 1)
                    act.activation((S1, S2)[k][:, 8 * n:8 * n + 8, :].rearrange("p g j -> p (g j)"),
                                   bank[2 * (n % 2) + k][:], ACT.Identity).then_inc(s["s_ev"], 1)
            scale = QK ** -0.5
            for n in range(NT * HEADS):
                t, h = n // HEADS, n % HEADS
                act.wait_ge(s["sc_max"], n + 1)
                if n >= 2:
                    act.wait_ge(s["a_tr"], n - 1)
                for c in range(2):
                    act.activation(ee[:, n % 2, c, :], bank[2 * (n % 2) + c][:], ACT.Exp, scale=scale,
                                   bias=att_s[:, n % 2, 2 + c:3 + c],
                                   accum_out=att_s[:, n % 2, 4 + c:5 + c]).then_inc(s["sc_exp"], 1)
                if n >= 1:
                    act.wait_ge(s["a_tr"], n)
                    if n >= 3:
                        act.wait_ge(s["pv_mm"], n - 2)
                    act.activation(aT[:, (n - 1) % 2].rearrange("p k q -> p (k q)"), bank[4 + (n - 1) % 2][:],
                                   ACT.Identity).then_inc(s["a_ev"], 1)
                if h == 2 and t >= 1:
                    o_norm_act(act, ch, s, bank, o_n, att_s, qk_s, sgn, catT, t - 1)
            n = NT * HEADS
            act.wait_ge(s["a_tr"], n)
            act.wait_ge(s["pv_mm"], n - 2)
            act.activation(aT[:, (n - 1) % 2].rearrange("p k q -> p (k q)"), bank[4 + (n - 1) % 2][:],
                           ACT.Identity).then_inc(s["a_ev"], 1)
            o_norm_act(act, ch, s, bank, o_n, att_s, qk_s, sgn, catT, NT - 1)
            for n in range(4):
                act.wait_ge(s["y_mm"], n + 1)
                act.activation(Y[:, 8 * n:8 * n + 8, :].rearrange("p g j -> p (g j)"), bank[n][:], ACT.Identity).then_inc(s["y_ev"], 1)
            act.wait_ge(s["y_gp"], 1)
            act.activation(S2[:, 0:NG, :], S2[:, 0:NG, :], ACT.Sigmoid, scale=GELU_A).then_inc(s["y_sig"], 1)
            for n in range(4):
                act.wait_ge(s["g_mm"], n + 1)
                act.activation(sT[:, n, :], bank[4 + n][:], ACT.Sigmoid, bias=glub[:, n:n + 1]).then_inc(s["g_sig"], 1)
            for n in range(4):
                act.wait_ge(s["s_act"], n + 1)
                act.activation(sqT[:, n, :], sT[:, n, :], ACT.Square).then_inc(s["s_sq"], 1)
            act.wait_ge(s["n_mm"], 1)
            act.activation(gluw[:, 0, :], bank[0][:], ACT.Sqrt, scale=1.0 / 512, bias=sgn[:, 2:3]).then_inc(s["n_rt"], 1)
            for t in range(NT):
                act.wait_ge(s["x1_ready"], t + 1)
                if t:
                    act.wait_ge(s["h2_ready"], t)
                if t >= 2:
                    act.wait_ge(s[f"h2_stored{t % 2}"], 16 * (t // 2))
                    act.wait_ge(s["h2_tr"], t - 1)
                for k in range(2):
                    ch.free(act.activation(h2[:, t % 2, 512 * k:512 * k + 512], x1[:, t % 2, 512 * k:512 * k + 512],
                                           ACT.Square, accum_out=sq_s[:, 8 + k:9 + k]))
                ch.sync()
                act.nop().then_inc(s["o_sq"], 1)
                act.wait_ge(s["m_rt"], t + 1)
                act.activation(sq_s[:, 11:12], sq_s[:, 10:11], ACT.Sqrt, scale=1.0 / D, bias=sgn[:, 2:3]).then_inc(s["o_sq"], 1)
                act.wait_ge(s["h2_tr"], t + 1)
                for k in range(2):
                    act.activation(h2T[:, 4 * k:4 * k + 4, :].rearrange("p k n -> p (k n)"), bank[4 + k][:],
                                   ACT.Identity).then_inc(s["h2_ev"], 1)
                act.wait_ge(s["lg_ready"], t + 1)
                act.activation(gat[:, t, :], mx8[:, 0:TOPK], ACT.Exp, bias=gs[:, 2:3], accum_out=gs[:, 0:1]).then_inc(s["g_exp"], 1)
            act.wait_ge(s["blocks_ready"], 1)
            n_blocks = act.value_load(nbi[0:1, 0:1], min_val=1, max_val=MAXB)

            def x_out(v):
                for k in range(2):
                    act.wait_ge(s[f"x_tr{k}"], v)
                    act.activation(xT[:, 4 * k:4 * k + 4, :].rearrange("p k n -> p (k n)"), bank[7 - k][:],
                                   ACT.Identity).then_inc(s[f"x_ev{k}"], 1)

            def gate(k, v):
                act.wait_ge(s[f"g_min{k}"], v)
                act.activation(glu[:, 1 + k, :] if k == 0 else lin[:, 2, :], glu[:, 0, :] if k == 0 else glu[:, 2, :],
                               ACT.Sigmoid, scale=1.702).then_inc(s[f"g_sg{k}"], 1)

            def act_out(k, v):
                act.wait_ge(s[f"a_tr{k}"], v)
                act.activation(actT[:, 4 * k:4 * k + 4, :].rearrange("p k n -> p (k n)"), bank[6 + k][:],
                               ACT.Identity).then_inc(s[f"a_ev{k}"], 1)
            x_out(1)
            act.sem_inc(s["y2_ev"], 2)
            with act.Fori(0, n_blocks) as b:
                gate(0, b + 1)
                gate(1, b + 1)
                act_out(0, b + 1)
                x_out(b + 2)
                act_out(1, b + 1)
                act.wait_ge(w_used, b * WCH + WCH)
                for k in range(2):
                    act.activation(ysb[:, 512 * k:512 * k + 512], bank[4 + k][:], ACT.Identity).then_inc(s["y2_ev"], 1)
                act.wait_ge(s["y2_stored"], b * 16 + 16)

        @block.vector
        def _(dve):
            ch = Chain(dve, s["dve"])

            def tt(o, a, b_, op):
                return dve.tensor_tensor(o, a, b_, op)

            dve.wait_ge(s["c_loaded"], 16)
            dve.wait_ge(s["lam_e"], 1)
            ch(tt(ccol[:, 2, :], ccol[:, 0, :], ccol[:, 1, :], ALU.mult))
            dve.tensor_copy(cbc[:], bc(ccol[:, 2, :], 2, P, [P, KT, P])).then_inc(s["cbc_ready"], 1)

            def reduce_angle(dst, src, shift, tmp, tmpi):
                ch(dve.tensor_scalar(tmp, src, 1 / (2 * math.pi), shift / (2 * math.pi), ALU.mult, ALU.add))
                ch(dve.tensor_copy(tmpi, tmp))
                ch(dve.tensor_copy(tmp, tmpi))
                ch(dve.scalar_tensor_tensor(dst, tmp, -C1, src, ALU.mult, ALU.add))
                ch(dve.scalar_tensor_tensor(dst, tmp, -C2, dst, ALU.mult, ALU.add))
                ch(dve.scalar_tensor_tensor(dst, tmp, -C3, dst, ALU.mult, ALU.add))
                if shift:
                    ch(dve.tensor_scalar(dst, dst, shift, None, ALU.add))
                ch(dve.tensor_scalar(tmp, dst, -math.pi, 2 * math.pi, ALU.is_lt, ALU.mult))
                ch(tt(dst, dst, tmp, ALU.add))
                ch(dve.tensor_scalar(tmp, dst, math.pi, -2 * math.pi, ALU.is_gt, ALU.mult))
                ch(tt(dst, dst, tmp, ALU.add))
                ch(dve.tensor_scalar(dst, dst, 3.1415925, -3.1415925, ALU.min, ALU.max))

            L = [lam_t[:, k, :] for k in range(16)]
            dve.wait_ge(s["lam_loaded"], 48)
            dve.wait_ge(s["act_lam"], 1)
            ch(dve.tensor_scalar(L[3], L[1], lstep[:, 1:2], None, ALU.mult))
            reduce_angle(L[4], L[3], 0.0, L[6], rope_i[0:DG, :])
            reduce_angle(L[5], L[3], math.pi / 2, L[6], rope_i[0:DG, :])
            dve.nop().then_inc(s["act_trig"], 1)
            dve.wait_ge(s["misc_loaded"], 16 * 25)
            ch(tt(lam_w[:], lam_in[:, 0:2], lam_in[:, 2:4], ALU.mult))
            dve.tensor_reduce(lamv[:, 0:2], lam_w[:], AX.X, ALU.add).then_inc(s["act_rope"], 1)
            inv = [np.float32(ROPE_THETA) ** np.float32(-2 * k / (2 * ROT_HALF)) for k in range(ROT_HALF)]
            ch(dve.tensor_copy(rope_t[:, 2, :, 0], posi[:]))
            for k in range(ROT_HALF):
                ch.free(dve.tensor_scalar(rope_t[:, 3, :, k], rope_t[:, 2, :, 0], float(inv[k]), None, ALU.mult))
            ch.sync()

            def flat(k):
                return rope_t[:, k].rearrange("p t k -> p (t k)")
            reduce_angle(flat(0), flat(3), math.pi / 2, flat(4), rope_i[:, 0:16])
            reduce_angle(flat(1), flat(3), 0.0, flat(4), rope_i[:, 0:16])
            dve.nop().then_inc(s["act_rope"], 1)
            dve.wait_ge(s["act_lam"], 2)
            ch(tt(lamv[:, 4:5], lamv[:, 3:4], lamv[:, 2:3], ALU.subtract))
            ch(dve.tensor_scalar(lamv[:, 5:6], lamv[:, 4:5], -LAMBDA_INIT, None, ALU.add))
            dve.wait_ge(s["lam_e"], 2)
            ch.free(tt(quad[:, 0, 0, :], L[2], L[5], ALU.mult))
            ch.free(tt(quad[:, 1, 0, :], L[2], L[4], ALU.mult))
            ch.free(tt(L[7], L[0], L[0], ALU.mult))
            ch(tt(L[8], L[1], L[1], ALU.mult))
            ch.free(tt(L[7], L[7], L[8], ALU.add))
            ch(dve.tensor_scalar(L[9], quad[:, 0, 0, :], -1.0, None, ALU.add))
            ch.free(dve.reciprocal(L[7], L[7]))
            ch.free(tt(L[10], L[9], L[0], ALU.mult))
            ch.free(tt(L[11], quad[:, 1, 0, :], L[1], ALU.mult))
            ch.free(tt(L[12], quad[:, 1, 0, :], L[0], ALU.mult))
            ch(tt(L[13], L[9], L[1], ALU.mult))
            ch.free(tt(L[10], L[10], L[11], ALU.add))
            ch(tt(L[12], L[12], L[13], ALU.subtract))
            ch.free(tt(quad[:, 2, 0, :], L[10], L[7], ALU.mult))
            ch(tt(quad[:, 3, 0, :], L[12], L[7], ALU.mult))
            dve.tensor_copy(quad[:, :, 1, :], quad[:, :, 0, :]).then_inc(s["quad_ready"], 1)
            modf = mod[:].rearrange("p a d -> p (a d)")
            dve.wait_ge(s["adab_loaded"], 16)

            def ada_out(n):
                dve.wait_ge(s["ada_mm"], n + 1)
                tt(modf[:, n * 512:(n + 1) * 512], bank[n % 2][:], modf[:, n * 512:(n + 1) * 512],
                   ALU.add).then_inc(s["ada_ev"], 1)
            ada_out(0)
            dve.wait_ge(s["af_ready"], 1)
            ch.free(dve.memset(PW[:, 0, 0, :], 1.0))
            ch.free(dve.memset(PW[:, 1, 0, :], 0.0))
            ch.free(dve.tensor_copy(PW[:, 0, 1, :], AF[:, 0, :]))
            ch(dve.tensor_copy(PW[:, 1, 1, :], AF[:, 1, :]))

            def cmul(dst, x, y, n):
                X = [PW[:, q, x:x + n, :] for q in range(2)]
                Yb = [bc(PW[:, q, y, :], 1, n, [P, n, DG]) for q in range(2)]
                T = t1[:, 0:n * DG].rearrange("p (n g) -> p n g", g=DG)
                O = [PW[:, q, dst:dst + n, :] for q in range(2)]
                ch.free(tt(O[0], X[0], Yb[0], ALU.mult))
                ch(tt(T, X[1], Yb[1], ALU.mult))
                ch(tt(O[0], O[0], T, ALU.subtract))
                ch.free(tt(O[1], X[0], Yb[1], ALU.mult))
                ch(tt(T, X[1], Yb[0], ALU.mult))
                ch(tt(O[1], O[1], T, ALU.add))
            cmul(2, 1, 1, 1)
            cmul(3, 1, 2, 2)
            cmul(5, 1, 4, 4)
            ch.free(dve.tensor_copy(ab8[:, 0, :], PW[:, 0, 8, :]))
            dve.tensor_scalar(ab8[:, 1, :], PW[:, 1, 8, :], sgn[:, 0:1], None, ALU.mult).then_inc(s["sg_ready"], 1)
            dve.wait_ge(s["bx_ready"], 4)
            dve.wait_ge(s["pe_prep"], 2)
            fr, fi = (bc(AF[:, 2 + q, :], 1, GC, [P, GC, DG]) for q in range(2))
            T1, TB = (x[:].rearrange("p (c g) -> p c g", g=DG) for x in (t1, tB))
            ch.free(tt(T1, Q2[:], fi, ALU.mult))
            ch(tt(TB, P2[:], fi, ALU.mult))
            ch.free(tt(P2[:], P2[:], fr, ALU.mult))
            ch(tt(Q2[:], Q2[:], fr, ALU.mult))
            ch.free(tt(P2[:], P2[:], T1, ALU.add))
            ch(tt(Q2[:], Q2[:], TB, ALU.subtract))
            TG = t1[:].rearrange("p (g c) -> p g c", c=GC)
            TH = tB[:].rearrange("p (g c) -> p g c", c=GC)
            p2g, q2g = (x[:].rearrange("p c g -> p g c") for x in (P2, Q2))
            inv_v = inT[:].rearrange("p g (i c) -> p g i c", c=GC)
            for i in range(STEPS):
                for di, pwr in ((0, 7 - i), (1, i)):
                    g = slice(di * NG, di * NG + NG)
                    pr, pi = (bc(PW[:, q, pwr, g], 2, GC, [P, NG, GC]) for q in range(2))
                    ch.free(tt(inv_v[:, g, i, :], p2g[:, g, :], pr, ALU.mult))
                    ch.free(tt(TG[:, g, :], q2g[:, g, :], pi, ALU.mult))
                ch.sync()
                ch(tt(inv_v[:, :, i, :], inv_v[:, :, i, :], TG, ALU.add))
                if i % 2 == 0:
                    ada_out(1 + i // 2)
            dve.nop().then_inc(s["inraw_ready"], 1)
            dve.wait_ge(s["cq_ready"], 2)
            dve.wait_ge(s["act"], 2)
            for l in range(STEPS + 1):
                for di, pwr in ((0, l), (1, 8 - l)):
                    g = slice(di * NG, di * NG + NG)
                    pr, pi = (bc(PW[:, q, pwr, g], 2, GC, [P, NG, GC]) for q in range(2))
                    ch.free(tt(outM[:, g, l, :], CP[:, g, :], pr, ALU.mult))
                    ch.free(tt((TG, TH)[l % 2][:, g, :], CQ[:, g, :], pi, ALU.mult))
                ch.sync()
                ch(tt(outM[:, :, l, :], outM[:, :, l, :], (TG, TH)[l % 2], ALU.add))
                if l % 2 == 0:
                    ada_out(5 + l // 2)
            dve.nop().then_inc(s["outm_ready"], 1)
            ada_out(10)
            ada_out(11)
            dve.wait_ge(s["ada_ev"], ADA_CHUNKS)
            dve.wait_ge(s["n1w_loaded"], 16)
            ch(dve.scalar_tensor_tensor(mod[:, 1], mod[:, 1], 1.0, n1w[:], ALU.add, ALU.mult))
            for t in range(NT):
                dve.wait_ge(s["sq1"], 2 * t + 1)
                tt(sq_s[:, 2:3], sq_s[:, 0:1], sq_s[:, 1:2], ALU.add).then_inc(s["m_sq"], 1)
                dve.wait_ge(s["sq1"], 2 * t + 2)
                dve.reciprocal(sq_s[:, 4:5], sq_s[:, 3:4]).then_inc(s["rs1"], 1)
                dve.wait_ge(s["rs1"], t + 1)
                ch(dve.scalar_tensor_tensor(xt[:, t % 2], xt[:, t % 2], sq_s[:, 4:5], mod[:, 1], ALU.mult, ALU.mult))
                tt(xt[:, t % 2], xt[:, t % 2], mod[:, 0], ALU.add).then_inc(s["h_ready"], 1)
            dve.wait_ge(s["h_tr"], NT)
            for n in range(8):
                t, w = n % 4, n // 4
                bk = bank[4 + n] if n < 4 else bank[n - 4]
                dve.wait_ge(s["q_sq"], n + 1)
                dve.tensor_reduce(qk_s[:, 0, :], sqb[:, n % 2, :].rearrange("p (g d) -> p g d", d=QK), AX.X,
                                  ALU.add).then_inc(s["q_ss"], 1)
                dve.wait_ge(s["q_rt"], n + 1)
                ch(dve.reciprocal(qk_s[:, 2, :], qk_s[:, 1, :]))
                if n >= 2:
                    dve.wait_ge(s["q_tr"], n - 1)
                X = stg[:, n % 2, :].rearrange("p (g d) -> p g d", d=QK)
                NGP = 2 * HEADS
                ch(tt(X, bk[:].rearrange("p (g d) -> p g d", d=QK), bc(qk_s[:, 2, :], 2, QK, [P, NGP, QK]), ALU.mult))
                ch(tt(X, X, bc(qkw[:, w, :], 1, NGP, [P, NGP, QK]), ALU.mult))
                cb, sb_ = (bc(cs[:, q, t, :], 1, NGP, [P, NGP, ROT_HALF]) for q in range(2))
                a, b_ = X[:, :, 0:ROT_HALF], X[:, :, ROT_HALF:2 * ROT_HALF]
                R = sqb[:, n % 2, 0:256].rearrange("p (q g k) -> p q g k", q=4, k=ROT_HALF)
                if n == 0:
                    dve.wait_ge(s["lam_e"], 3)
                ch.free(tt(R[:, 0], a, cb, ALU.mult))
                ch.free(tt(R[:, 1], b_, sb_, ALU.mult))
                ch.free(tt(R[:, 2], b_, cb, ALU.mult))
                ch(tt(R[:, 3], a, sb_, ALU.mult))
                ch.free(tt(a, R[:, 0], R[:, 1], ALU.subtract))
                ch(tt(b_, R[:, 2], R[:, 3], ALU.add))
                dve.nop().then_inc(s["q_n"], 1)
            def o_norm(t):
                dve.wait_ge(s["pv_mm"], HEADS * (t + 1))
                bk = bank[6]
                ch(dve.tensor_copy(o_n[:, 0, :], bk[:]))
                ch(tt(o_n[:, 1, :], o_n[:, 0, :], o_n[:, 0, :], ALU.mult))
                dve.tensor_reduce(qk_s[:, 0, 0:8], o_n[:, 1, :].rearrange("p (h d) -> p h d", d=DV), AX.X,
                                  ALU.add).then_inc(s["o_ss"], 1)
                dve.wait_ge(s["o_rt"], t + 1)
                ch(dve.reciprocal(qk_s[:, 2, 0:8], qk_s[:, 1, 0:8]))
                O = o_n[:, 0, :].rearrange("p (h d) -> p h d", d=DV)
                ch(tt(O, O, bc(qk_s[:, 2, 0:8], 2, DV, [P, HEADS, DV]), ALU.mult))
                ch(tt(O, O, bc(subw[:], 1, HEADS, [P, HEADS, DV]), ALU.mult))
                dve.nop().then_inc(s["o_n"], 1)
            ch(dve.tensor_scalar(subw[:], subw[:], 1.0 - LAMBDA_INIT, None, ALU.mult))
            dve.wait_ge(s["q_ev"], 8)
            for n in range(NT * HEADS + 1):
                if n < NT * HEADS:
                    dve.wait_ge(s["sc_mm"], 2 * (n + 1))
                    for c in range(2):
                        ch.free(dve.tensor_reduce(att_s[:, n % 2, c:c + 1], bank[2 * (n % 2) + c][:], AX.X, ALU.max))
                    ch.sync()
                    dve.tensor_scalar(att_s[:, n % 2, 2:4], att_s[:, n % 2, 0:2], -(QK ** -0.5), None,
                                      ALU.mult).then_inc(s["sc_max"], 1)
                if n >= 1:
                    m = n - 1
                    dve.wait_ge(s["sc_exp"], 2 * n)
                    ch(dve.reciprocal(att_s[:, m % 2, 6:8], att_s[:, m % 2, 4:6]))
                    ch.free(dve.tensor_scalar(att_s[:, m % 2, 7:8], att_s[:, m % 2, 7:8], lamv[:, 5:6], None, ALU.mult))
                    ch(dve.tensor_scalar(ee[:, m % 2, 0, :], ee[:, m % 2, 0, :], att_s[:, m % 2, 6:7], None, ALU.mult))
                    dve.scalar_tensor_tensor(ee[:, m % 2, 0, :], ee[:, m % 2, 1, :], att_s[:, m % 2, 7:8],
                                             ee[:, m % 2, 0, :], ALU.mult, ALU.add).then_inc(s["a_ready"], 1)
                if n % HEADS == 2 and n > HEADS:
                    o_norm(n // HEADS - 1)
            o_norm(NT - 1)
            dve.wait_ge(s["scan_done"], 2)
            dve.wait_ge(s["y_ev"], 4)
            ch(tt(U[:], U[:], bc(dcol[:], 2, CHUNKS, [P, NG, CHUNKS]), ALU.mult))
            ch(tt(Y[:], Y[:], U[:], ALU.add))
            T = S2[:, 0:NG, :]
            ch(tt(T, Y[:], Y[:], ALU.mult))
            ch(dve.tensor_scalar(T, T, GELU_B, 1.0, ALU.mult, ALU.add))
            tt(T, T, Y[:], ALU.mult).then_inc(s["y_gp"], 1)
            dve.wait_ge(s["y_sig"], 1)
            tt(Y[:], Y[:], T, ALU.mult).then_inc(s["y_done"], 1)
            for n in range(4):
                dve.wait_ge(s["g_sig"], n + 1)
                tt(sT[:, n, :], sT[:, n, :], yT[:, n, :], ALU.mult).then_inc(s["s_act"], 1)
            dve.wait_ge(s["n_rt"], 1)
            dve.wait_ge(s["s_act"], 4)
            ch(dve.reciprocal(gluw[:, 1, :], gluw[:, 0, :]))
            for n in range(4):
                dve.scalar_tensor_tensor(catT[:, 4 + n, :], sT[:, n, :], outw[:, n:n + 1], gluw[:, 1, :],
                                         ALU.mult, ALU.mult).then_inc(s["s5_done"], 1)
            dve.wait_ge(s["n2w_loaded"], 16)
            ch(dve.scalar_tensor_tensor(mod[:, 4], mod[:, 4], 1.0, n2w[:], ALU.add, ALU.mult))
            dve.wait_ge(s["rw_loaded"], 32)
            dve.wait_ge(s["consts2"], 1)
            for t in range(NT):
                dve.wait_ge(s["mix_mm"], t + 1)
                dve.wait_ge(s[f"xr_loaded{t % 2}"], 32 * (t // 2 + 1))
                if t >= 2:
                    dve.wait_ge(s[f"x1_stored{t % 2}"], 16 * (t // 2))
                for k in range(2):
                    cc_ = slice(512 * k, 512 * k + 512)
                    ch.free(tt(x1[:, t % 2, cc_], bank[2 * (t % 2) + k][:], mod[:, 2, cc_], ALU.mult))
                ch.sync()
                tt(x1[:, t % 2], x1[:, t % 2], xr[:, t % 2], ALU.add).then_inc(s["x1_ready"], 1)
                dve.wait_ge(s["o_sq"], 2 * t + 1)
                tt(sq_s[:, 10:11], sq_s[:, 8:9], sq_s[:, 9:10], ALU.add).then_inc(s["m_rt"], 1)
                dve.wait_ge(s["o_sq"], 2 * t + 2)
                ch(dve.reciprocal(sq_s[:, 12:13], sq_s[:, 11:12]))
                ch(dve.scalar_tensor_tensor(h2[:, t % 2], x1[:, t % 2], sq_s[:, 12:13], mod[:, 4], ALU.mult, ALU.mult))
                tt(h2[:, t % 2], h2[:, t % 2], mod[:, 3], ALU.add).then_inc(s["h2_ready"], 1)
                dve.wait_ge(s["r_mm"], t + 1)
                ch(tt(lg[:], bank[6][:, 0:E], rb[:], ALU.add))
                ch(dve.max(mx8[:], lg[:]))
                ch.free(dve.max_index(ix8[:], mx8[:], lg[:]))
                dve.tensor_scalar(gs[:, 2:3], mx8[:, 0:1], -1.0, None, ALU.mult).then_inc(s["lg_ready"], 1)
                ch.sync()
                ch(dve.tensor_copy(ixf[:], ix8[:]))
                ch(tt(oh4[:, t], bc(iotaE[:, 0:E], 1, TOPK, [P, TOPK, E]), bc(ixf[:, 0:TOPK], 2, E, [P, TOPK, E]), ALU.is_equal))
                dve.tensor_reduce(mask[:, t], oh4[:, t].rearrange("p k e -> p e k"), AX.X, ALU.add).then_inc(s["mask_ready"], 1)
                dve.wait_ge(s["g_exp"], t + 1)
                ch(dve.reciprocal(gs[:, 1:2], gs[:, 0:1]))
                ch(dve.tensor_scalar(gat[:, t, :], gat[:, t, :], gs[:, 1:2], None, ALU.mult))
            dve.wait_ge(s["mix_mm"], NT)
            dve.wait_ge(s["pos_mm"], 1)
            R = [rt[:, k, :] for k in range(8)]
            cnt = bank[7][:, NT * E:NT * E + E]
            ch.free(dve.tensor_scalar(R[0], cnt, 0.5, None, ALU.is_gt))
            for k in range(1, NT):
                ch.free(dve.tensor_scalar(R[k], cnt, k * P + 0.5, None, ALU.is_gt))
            ch.sync()
            ch(tt(R[0], R[0], R[1], ALU.add))
            ch(tt(R[0], R[0], R[2], ALU.add))
            ch(tt(R[0], R[0], R[3], ALU.add))
            a, b_ = R[1], R[2]
            ch(dve.tensor_copy(a, R[0]))
            dist = 1
            while dist < E:
                ch.free(dve.tensor_copy(b_[:, 0:dist], a[:, 0:dist]))
                ch(tt(b_[:, dist:E], a[:, dist:E], a[:, 0:E - dist], ALU.add))
                a, b_ = b_, a
                dist *= 2
            end = a
            ch.free(dve.tensor_copy(nbi[:, 0:1], end[:, E - 1:E]))
            ch.free(tt(cmpb[:], bc(iotaE[:], 2, E, [P, MAXB, E]), bc(end, 1, MAXB, [P, MAXB, E]), ALU.is_ge))
            ch(tt(R[3], end, R[0], ALU.subtract))
            ch.free(dve.tensor_reduce(ebf[:, 0:MAXB], cmpb[:], AX.X, ALU.add))
            ch(dve.tensor_scalar(R[4], R[3], float(P), None, ALU.mult))
            ch.free(dve.memset(ebf[:, MAXB:MAXB + 2], 0.0))
            ch.free(tt(slotE[:], bank[7][:, 0:NT * E].rearrange("p (t e) -> p t e", e=E), bc(R[4], 1, NT, [P, NT, E]), ALU.add))
            ch(dve.tensor_scalar(ebf[:, 0:MAXB], ebf[:, 0:MAXB], float(E - 1), None, ALU.min))
            ch.free(dve.tensor_copy(ebi[:], ebf[:]))
            ch.free(dve.tensor_scalar(eye96[:], ebf[0:96, :], pm[0:96, 0:1], None, ALU.is_equal))
            for t in range(NT):
                ch.free(tt(prod[:, TOPK * t:TOPK * t + TOPK], oh4[:, t], bc(slotE[:, t], 1, TOPK, [P, TOPK, E]), ALU.mult))
            ch.sync()
            ch(dve.tensor_reduce(dslot[:], prod[:], AX.X, ALU.add))
            dve.nop().then_inc(s["blocks_ready"], 1)
            n_blocks = dve.value_load(nbi[0:1, 0:1], min_val=1, max_val=MAXB)
            dve.wait_ge(s["bias_ready"], 2)

            def slots(v):
                tt(ohs[:], bc(iotab[:], 1, NT * TOPK, [P, NT * TOPK, P]), bc(dslot[:], 2, P, [P, NT * TOPK, P]),
                   ALU.is_equal).then_inc(s["oh_ready"], 1)
                dve.wait_ge(s["oh_ready"], v)
                dve.tensor_scalar(iotab[:], iotab[:], float(P), None, ALU.add).then_inc(s["d_ready"], 1)

            def rows(v):
                dve.wait_ge(s["idx_mm"], v)
                dve.tensor_reduce(idf[:, 0:1], bank[6][:, 0:2], AX.X, ALU.add).then_inc(s["idx_sum"], 1)
                dve.tensor_reduce(idf[:, 1:2], bank[6][:, 0:4], AX.X, ALU.add).then_inc(s["idx_sum"], 1)
                dve.wait_ge(s["idx_sum"], v * 2)
                dve.tensor_scalar(idx[:, 1:2], idf[:, 1:2], UNUSED, None, ALU.add).then_inc(s["idx_ready"], 1)
                dve.tensor_scalar(idx[:, 0:1], idf[:, 0:1], 1 / TOPK, None, ALU.mult).then_inc(s["idx_ready"], 1)

            def select(b, v):
                dve.tensor_copy(selb[:], eye96[:, bass.ds(b, 1)].to_broadcast([96, P])).then_inc(s["sel_ready"], 1)

            def gated(k, v):
                z = [bank[2 * k][:].rearrange("p (f two) -> p two f", two=2),
                     bank[2 * k + 1][:].rearrange("p (f two) -> p two f", two=2)]
                g = glu[:, 0, :] if k == 0 else glu[:, 2, :]
                l = lin[:, k, :]
                sg = glu[:, 1, :] if k == 0 else lin[:, 2, :]
                dve.wait_ge(w_used, (v - 1) * WCH + KT * (k + 1))
                for q in range(2):
                    dve.tensor_scalar(g[:, 256 * q:256 * q + 256], z[q][:, 0, :], 7.0, None, ALU.min).then_inc(s[f"l_a{k}"], 1)
                dve.wait_ge(s[f"l_a{k}"], 4 * v - 2)
                dve.nop().then_inc(s[f"g_min{k}"], 1)
                for q in range(2):
                    dve.tensor_scalar(l[:, 256 * q:256 * q + 256], z[q][:, 1, :], 7.0, -7.0, ALU.min,
                                      ALU.max).then_inc(s[f"l_a{k}"], 1)
                dve.wait_ge(s[f"l_a{k}"], 4 * v)
                dve.scalar_tensor_tensor(l, l, 1.0, g, ALU.add, ALU.mult).then_inc(s[f"l_b{k}"], 1)
                dve.wait_ge(s[f"l_b{k}"], v)
                dve.wait_ge(s[f"g_sg{k}"], v)
                tt(l, l, sg, ALU.mult).then_inc(s[f"act_ready{k}"], 1)

            slots(1)
            select(0, 1)
            rows(1)
            dve.wait_ge(s["idx_ready"], 2)
            dve.tensor_copy(idx[:, 2:3], idx[:, 1:2]).then_inc(s["scat_ready"], 1)
            with dve.Fori(0, n_blocks) as b:
                dve.wait_ge(s["d_ready"], b + 1)
                slots(b + 2)
                rows(b + 2)
                gated(0, b + 1)
                gated(1, b + 1)
                dve.wait_ge(w_used, b * WCH + W1C + 1)
                select(b + 1, b + 2)
                dve.wait_ge(s["y2_stored"], b * 16 + 16)
                dve.wait_ge(s["idx_ready"], b * 2 + 4)
                dve.tensor_copy(idx[:, 2:3], idx[:, 1:2]).then_inc(s["scat_ready"], 1)
            dve.wait_ge(s["fin_x1"], 16)
            for t in range(NT):
                dve.wait_ge(s[f"fin_g{t}"], 16)
                o = facc[:, t]
                ch(dve.tensor_scalar(o, fing[:, TOPK * t], gat[:, t, 0:1], None, ALU.mult))
                for k in range(1, TOPK):
                    ch(dve.scalar_tensor_tensor(o, fing[:, TOPK * t + k], gat[:, t, k:k + 1], o, ALU.mult, ALU.add))
                ch(tt(o, o, mod[:, 5], ALU.mult))
                tt(o, o, fx1[:, t], ALU.add).then_inc(s["fin_done"], 1)

        @block.tensor
        def _(pe):
            mm, tr = pe.matmul, pe.transpose
            pe.wait_ge(s["ident_ready"], 1)
            pe.wait_ge(s["s5_nat"], 96)
            for q in range(2):
                for n in range(8):
                    last = tr(bank[2 * q + n // 4][:, (n % 4) * P:(n % 4) * P + P],
                              CC[:, n, q:q + 2, :].rearrange("p a b -> p (a b)"), ident[:])
            last.then_inc(s["pe_prep"], 1)
            bbf = BB[:].rearrange("p a b -> p (a b)")
            for q in range(2):
                for c in range(GC):
                    o = q * NP * GC + c
                    last = tr(bank[4 + 2 * q + c // 8][:, (c % 8) * DG:(c % 8) * DG + DG],
                              bbf[:, o:o + GC * (P - 1) + 1:GC], ident[0:DG, 0:DG])
            last.then_inc(s["pe_prep"], 1)

            def ada(n):
                pe.wait_ge(ring_sem[n % RING], 16 * (n // RING + 1))
                if n >= 2:
                    pe.wait_ge(s["ada_ev"], n - 1)
                for k in range(KT):
                    last = mm(bank[n % 2][:], cbc[:, k, :], ring[:, n % RING, k, :], start=(k == 0), stop=(k == KT - 1))
                last.then_inc(s["ada_mm"], 1)

            pe.wait_ge(s["cbc_ready"], 1)
            pe.wait_ge(s["cq_ready"], 2)
            pe.wait_ge(s["act"], 2)
            ada(0)
            ada(1)
            pe.wait_ge(s["quad_ready"], 1)
            for q in range(4):
                last = tr(bank[2][:, q * DG:(q + 1) * DG], quad[:, q].rearrange("p a b -> p (a b)"), ident[0:DG, 0:DG])
            last.then_inc(s["af_psum"], 1)
            pe.wait_ge(s["af_ready"], 1)
            pe.wait_ge(s["bx_ready"], 4)
            for n in range(2, ADA_CHUNKS):
                ada(n)
            pe.wait_ge(s["inraw_ready"], 1)
            for n in range(DG // 4):
                if n >= 4:
                    pe.wait_ge(s["in_done"], n - 3)
                for g in range(4):
                    last = tr(bank[2 + n % 4][:, g * P:(g + 1) * P], inT[:, 4 * n + g, :], ident[:])
                last.then_inc(s["in_tr"], 1)
            pe.wait_ge(s["outm_ready"], 1)
            for n in range(NG // 2):
                if n >= 2:
                    pe.wait_ge(s["k_ev"], n - 1)
                for q in range(2):
                    g = 2 * n + q
                    o = q * 240
                    mm(bank[6 + n % 2][0:GC, o + 112:o + 240], P2[:, :, g],
                       outM[:, g, 0:STEPS, :].rearrange("p l c -> p (l c)"), start=(q == 0), stop=False, skip_group_check=True)
                    last = mm(bank[6 + n % 2][0:GC, o:o + P], P2[:, :, NG + g],
                              outM[:, NG + g, 1:STEPS + 1, :].rearrange("p l c -> p (l c)"), start=False, stop=(q == 1),
                              skip_group_check=True)
                last.then_inc(s["k_mm"], 1)
            pe.wait_ge(s["ada_ev"], ADA_CHUNKS)
            pe.wait_ge(s["in_done"], DG // 4)
            for t in range(NT):
                pe.wait_ge(s["h_ready"], t + 1)
                if t >= 2:
                    pe.wait_ge(s["h_ev"], 2 * (t - 1))
                for k in range(KT):
                    last = tr(bank[2 * (t % 2) + k // 4][:, (k % 4) * P:(k % 4) * P + P], xt[:, t % 2, k * P:(k + 1) * P], ident[:])
                last.then_inc(s["h_tr"], 1)
            pe.wait_ge(s["h_ev"], 2 * NT)
            pe.wait_ge(ring_sem[U_CHUNK % RING], 16 * (U_CHUNK // RING + 1))
            for n in range(4):
                for k in range(KT):
                    last = mm(bank[n][:], ring[:, U_CHUNK % RING, k, n * P:(n + 1) * P], hT[:, k, :],
                              start=(k == 0), stop=(k == KT - 1))
                last.then_inc(s["u_mm"], 1)
            def proj(c, t, bk):
                if t == 0:
                    pe.wait_ge(ring_sem[c % RING], 16 * (c // RING + 1))
                for k in range(KT):
                    last = mm(bk[:], hT[:, k, t * P:(t + 1) * P], ring[:, c % RING, k, :], start=(k == 0), stop=(k == KT - 1))
                last.then_inc(s["q_mm"], 1)

            def qk_tr(n):
                bk = bank[4 + n] if n < 4 else bank[n - 4]
                pe.wait_ge(s["q_n"], n + 1)
                for b in range(4):
                    last = tr(bk[:, b * P:(b + 1) * P], stg[:, n % 2, b * P:(b + 1) * P], ident[:])
                last.then_inc(s["q_tr"], 1)
            pe.wait_ge(s["k_ev"], NG // 2)
            pe.wait_ge(s["sq1"], 2 * NT)
            for t in range(NT):
                proj(Q_CHUNK, t, bank[4 + t])
            pe.wait_ge(s["u_ev"], 4)
            for t in range(NT):
                proj(K_CHUNK, t, bank[t])
            for n in range(8):
                qk_tr(n)
            pe.wait_ge(s["q_ev"], 8)
            for t in range(NT):
                proj(V_CHUNK, t, bank[4 + t])
            pe.wait_ge(s["u_loaded"], 16 * STEPS)
            for n in range(DG // 8):
                for k in range(2):
                    if n >= 2:
                        pe.wait_ge(s["s_ev"], 2 * (n - 2) + k + 1)
                    bk = bank[2 * (n % 2) + k]
                    for g in range(8):
                        d = 8 * n + g
                        if k == 0:
                            last = mm(bk[:, g * 64:g * 64 + 64], inT[:, d, :], U[:, d % NG, :], start=True, stop=True)
                        else:
                            mm(bk[0:64, g * 64:g * 64 + 64], inT[:, d, 64:128], U[:, d % NG, :], start=True, stop=True)
                            last = mm(bk[64:128, g * 64:g * 64 + 64], inT[:, d, 0:64], U[:, d % NG, :], start=True, stop=True)
                    last.then_inc(s["s_mm"], 1)
            pe.wait_ge(s["s_ev"], 2 * DG // 8)
            pe.wait_ge(s["v_ev"], 4)

            def scores(n):
                t, h = n // HEADS, n % HEADS
                if n >= 2:
                    pe.wait_ge(s["sc_exp"], 2 * (n - 1))
                for c in range(2):
                    g = 2 * h + c
                    p0 = 32 * (g % 4)
                    mm(bank[2 * (n % 2) + c][:], qkT[p0:p0 + 32, 0, g // 4, t * P:(t + 1) * P],
                       qkT[p0:p0 + 32, 1, g // 4, :], start=True, stop=True).then_inc(s["sc_mm"], 1)

            def values(n):
                t, h = n // HEADS, n % HEADS
                pe.wait_ge(s["a_ev"], n + 1)
                if h == 0 and t:
                    pe.wait_ge(s["o_ss"], t)
                for k in range(NT):
                    last = mm(bank[6][:, h * DV:(h + 1) * DV], aT[:, n % 2, k, :], vv[:, k, h * DV:(h + 1) * DV],
                              start=(k == 0), stop=(k == NT - 1))
                last.then_inc(s["pv_mm"], 1)

            def o_tr(t):
                pe.wait_ge(s["o_n"], t + 1)
                if t:
                    pe.wait_ge(s["o_ev"], t)
                for k in range(4):
                    last = tr(bank[7][:, k * P:(k + 1) * P], o_n[:, 0, k * P:(k + 1) * P], ident[:])
                last.then_inc(s["o_tr"], 1)
            for n in range(NT * HEADS + 2):
                if n < NT * HEADS:
                    scores(n)
                if 1 <= n <= NT * HEADS:
                    m = n - 1
                    pe.wait_ge(s["a_ready"], m + 1)
                    if m >= 2:
                        pe.wait_ge(s["a_ev"], m - 1)
                    for k in range(NT):
                        last = tr(bank[4 + m % 2][:, k * P:(k + 1) * P], ee[:, m % 2, 0, k * P:(k + 1) * P], ident[:])
                    last.then_inc(s["a_tr"], 1)
                if n >= 2:
                    values(n - 2)
                if n % HEADS == 3 and n > HEADS:
                    o_tr(n // HEADS - 1)
            o_tr(NT - 1)
            pe.wait_ge(s["scan_done"], 2)
            pe.wait_ge(s["kp_half"], 32 * STEPS)
            pe.wait_ge(s["sc_exp"], 2 * NT * HEADS)
            for n in range(4):
                for q in range(8):
                    g = 8 * n + q
                    o = 64 * q
                    mm(bank[n][:, o:o + 64], toep[:, g, :], U[:, g, :], start=True, stop=False, skip_group_check=True)
                    mm(bank[n][:, o + 1:o + 64], outM[:, g, 1:STEPS + 1, :].rearrange("p l c -> p (l c)"),
                       S1[:, g, 0:63], start=False, stop=False, skip_group_check=True)
                    last = mm(bank[n][:, o:o + 63], outM[:, NG + g, 0:STEPS, :].rearrange("p l c -> p (l c)"),
                              S1[:, NG + g, 1:64], start=False, stop=True, skip_group_check=True)
                last.then_inc(s["y_mm"], 1)
            pe.wait_ge(s["y_loaded"], 16)
            pe.wait_ge(s["gluw_loaded"], 16)
            pe.wait_ge(s["o_ev"], NT)
            for n in range(4):
                for k in range(4):
                    last = mm(bank[4 + n][:], gluw[:, k, n * P:(n + 1) * P], yT[:, k, :], start=(k == 0), stop=(k == 3))
                last.then_inc(s["g_mm"], 1)
            pe.wait_ge(s["s_sq"], 4)
            pe.wait_ge(s["y_ev"], 4)
            pe.wait_ge(s["consts2"], 1)
            for k in range(4):
                last = mm(bank[0][:], ones[:], sqT[:, k, :], start=(k == 0), stop=(k == 3))
            last.then_inc(s["n_mm"], 1)
            pe.wait_ge(s["s5_done"], 4)
            pe.wait_ge(s["wout_loaded"], 16)

            def mix(t):
                if t >= 2:
                    pe.wait_ge(s["x1_ready"], t - 1)
                for k in range(2):
                    for c in range(KT):
                        last = mm(bank[2 * (t % 2) + k][:], catT[:, c, t * P:(t + 1) * P],
                                  wout[:, c, 512 * k:512 * k + 512], start=(c == 0), stop=(c == KT - 1))
                last.then_inc(s["mix_mm"], 1)

            def route(t):
                pe.wait_ge(s["h2_ready"], t + 1)
                if t == 0:
                    pe.wait_ge(s["g_sig"], 4)
                else:
                    pe.wait_ge(s["h2_ev"], 2 * t)
                for k in range(KT):
                    last = tr(bank[4 + k // 4][:, (k % 4) * P:(k % 4) * P + P], h2[:, t % 2, k * P:(k + 1) * P], ident[:])
                last.then_inc(s["h2_tr"], 1)
                pe.wait_ge(s["h2_ev"], 2 * (t + 1))
                if t == 0:
                    pe.wait_ge(s["rw_loaded"], 32)
                else:
                    pe.wait_ge(s["lg_ready"], t)
                for k in range(KT):
                    last = mm(bank[6][:, 0:E], h2T[:, k, :], rw[:, k, :], start=(k == 0), stop=(k == KT - 1))
                last.then_inc(s["r_mm"], 1)

            mix(0)
            mix(1)
            for t in range(NT):
                route(t)
                if t + 2 < NT:
                    mix(t + 2)
            pe.wait_ge(s["mask_ready"], NT)
            for t in range(NT):
                for q in range(t + 1):
                    mm(bank[7][:, t * E:(t + 1) * E], tri[:] if q == t else onb[:], mask[:, q, :], start=(q == 0), stop=(q == t))
            for q in range(NT):
                last = mm(bank[7][:, NT * E:(NT + 1) * E], onb[:], mask[:, q, :], start=(q == 0), stop=(q == NT - 1))
            last.then_inc(s["pos_mm"], 1)
            pe.wait_ge(s["blocks_ready"], 1)
            n_blocks = pe.value_load(nbi[0:1, 0:1], min_val=1, max_val=MAXB)

            def rows(v):
                pe.wait_ge(s["oh_ready"], v)
                for q in range(NT * TOPK):
                    last = mm(bank[6][:, 0:4], ohs[:, q, :], tokid[:, q, :], start=(q == 0), stop=(q == NT * TOPK - 1))
                last.then_inc(s["idx_mm"], 1)

            def x_turn(v):
                pe.wait_ge(s["xs_loaded"], v * 16)
                for k in range(2):
                    for c in range(4):
                        last = tr(bank[7 - k][:, c * P:(c + 1) * P], xs[:, (4 * k + c) * P:(4 * k + c + 1) * P], ident[:])
                    last.then_inc(s[f"x_tr{k}"], 1)

            def up(k, v, w32):
                if k == 0:
                    pe.wait_ge(s["sel_ready"], v)
                for q in range(2):
                    mm(bank[2 * k + q][:], selb[:], bcat[:, (2 * k + q) * 512:(2 * k + q + 1) * 512], start=True, stop=False)
                for c in range(KT):
                    if c % 2 == 0:
                        pe.wait_ge(w_loaded[(KT * k + c) // 2], w32)
                    for q in range(2):
                        last = mm(bank[2 * k + q][:], xT[:, c, :], w1[:, KT * k + c, 512 * q:512 * q + 512],
                                  start=False, stop=(c == KT - 1))
                    last.then_inc(w_used, 1)

            def act_turn(k, v):
                pe.wait_ge(s[f"act_ready{k}"], v)
                if k == 0:
                    pe.wait_ge(s["idx_ready"], v * 2 + 2)
                else:
                    pe.wait_ge(s["x_ev0"], v + 1)
                for c in range(4):
                    last = tr(bank[6 + k][:, c * P:(c + 1) * P], lin[:, k, c * P:(c + 1) * P], ident[:])
                last.then_inc(s[f"a_tr{k}"], 1)

            def down(k, v, w32):
                pe.wait_ge(s[f"a_ev{k}"], v)
                if k == 0:
                    for q in range(2):
                        mm(bank[4 + q][:], selb[:], bcat[:, 2048 + 512 * q:2560 + 512 * q], start=True, stop=False)
                for c in range(4 * k, 4 * k + 4):
                    if c % 2 == 0:
                        pe.wait_ge(w_loaded[(W1C + c) // 2], w32)
                    for q in range(2):
                        last = mm(bank[4 + q][:], actT[:, c, :], w2[:, c, 512 * q:512 * q + 512],
                                  start=False, stop=(c == KT - 1))
                    last.then_inc(w_used, 1)

            pe.wait_ge(s["bias_ready"], 1)
            rows(1)
            x_turn(1)
            with pe.Fori(0, n_blocks) as b:
                v = b + 1
                w32 = v * 32
                pe.wait_ge(s["x_ev0"], v)
                pe.wait_ge(s["x_ev1"], v)
                up(0, v, w32)
                rows(b + 2)
                up(1, v, w32)
                act_turn(0, v)
                pe.wait_ge(s["y2_ev"], b * 2 + 2)
                down(0, v, w32)
                x_turn(b + 2)
                act_turn(1, v)
                down(1, v, w32)


def o_norm_act(act, ch, s, bank, o_n, att_s, qk_s, sgn, catT, t):
    act.wait_ge(s["o_ss"], t + 1)
    act.activation(qk_s[:, 1, 0:8], qk_s[:, 0, 0:8], ACT.Sqrt, scale=1.0 / DV, bias=sgn[:, 2:3]).then_inc(s["o_rt"], 1)
    act.wait_ge(s["o_tr"], t + 1)
    act.activation(catT[:, 0:4, t * P:(t + 1) * P], bank[7][:].rearrange("p (k n) -> p k n", n=P),
                   ACT.Identity).then_inc(s["o_ev"], 1)


NAMES = ["x", "c", "positions", "ada_w", "ada_b", "norm1_w", "w_in", "q_norm_w", "k_norm_w", "lambda_q1", "lambda_k1",
         "lambda_q2", "lambda_k2", "subln_w", "s5_lambda_re", "s5_lambda_im", "s5_log_step", "s5_b_re", "s5_b_im",
         "s5_cmat_re", "s5_cmat_im", "s5_d", "s5_glu_w", "s5_glu_b", "s5_out_norm_w", "w_out", "norm2_w", "router_w",
         "router_b", "mlp1_w", "mlp1_b", "mlp2_w", "mlp2_b"]


def kernel(**inputs):
    from concourse import bacc
    from concourse.bass_utils import run_bass_kernel_spmd

    nc = bacc.Bacc("TRN2", target_bir_lowering=False, num_devices=1)
    arrays = {n: np.ascontiguousarray(inputs[n]) for n in NAMES}
    params = {n: nc.dram_tensor(n, a.shape, mybir.dt.from_np(a.dtype), kind="ExternalInput").ap()
              for n, a in arrays.items()}
    out = nc.dram_tensor("out", (1, S, D), F32, kind="ExternalOutput").ap()
    program(nc, params, out)
    r = run_bass_kernel_spmd(nc, [arrays], core_ids=[0])
    return r.results[0]["out"]
```

```python
import math
from contextlib import ExitStack

import numpy as np

import concourse.bass as bass
from concourse import mybir

F32 = mybir.dt.float32
F32R = mybir.dt.float32r
BF16 = mybir.dt.bfloat16
I32 = mybir.dt.int32
U32 = mybir.dt.uint32
ALU = mybir.AluOpType
ACT = mybir.ActivationFunctionType
AX = mybir.AxisListType

P = 128
KIB = 1024
S, D = 512, 1024
KT = D // P
NT = S // P
HEADS, QK, DV = 8, 32, 64
ROT_HALF = 4
ROPE_THETA = 500000.0
STEPS = 8
CHUNKS = S // STEPS
GC, NG, NP = 16, 32, 64
DG = 2 * NG
E, TOPK, FF = 32, 4, 1024
MAXB = S * TOPK // P + E
EPS = 1e-6
LAMBDA_INIT = 0.8 - 0.6 * math.exp(0.0)
C1, C2 = 6.28125, 0.0019350051879882812
C3 = 2 * math.pi - C1 - C2
GELU_A, GELU_B = 2 * math.sqrt(2 / math.pi), 0.044715
ADA_CHUNKS = 6 * D // 512
U_CHUNK, Q_CHUNK, K_CHUNK, V_CHUNK = range(ADA_CHUNKS, ADA_CHUNKS + 4)
RING = 3
W1C, W2C = 16, 8
WCH = W1C + W2C
SPLIT = 6
POOL_LOW = (8, 13, 18, 23)
DVE_LOW = tuple(c for c in range(WCH) if c not in POOL_LOW)
UNUSED = 4096.0
SBUF0 = 16512


def bc(ap, axis, n, shape):
    return ap.unsqueeze(axis).to_broadcast(shape)


class Chain:

    def __init__(self, eng, sem):
        self.eng, self.sem, self.n = eng, sem, 0

    def __call__(self, ins):
        self.n += 1
        ins.then_inc(self.sem, 1)
        self.eng.wait_ge(self.sem, self.n)

    def free(self, ins):
        self.n += 1
        ins.then_inc(self.sem, 1)

    def sync(self):
        self.eng.wait_ge(self.sem, self.n)


def program(nc, I, out):
    ctx = ExitStack()

    def at(name, kib, shape, dt=F32):
        return nc.alloc_sbuf_tensor_at(name, shape, dt, offset=SBUF0 + int(kib * KIB))

    def sem(name):
        return ctx.enter_context(nc.semaphore(name))

    with ctx:
        A, B, C, DD, EE, FV = 0, 64, 96, 132, 156, 172
        G = 196
        K0 = 204.5
        ident = at("ident", K0, [P, P])
        sgn = at("sgn", K0 + 0.5, [P, 4])
        ab8 = at("ab8", K0 + 0.5 + 0.0625, [P, 2, DG])
        cs = at("rope", K0 + 1.0625 + 0.0625, [P, 2, NT, ROT_HALF])
        qkw = at("qkw", K0 + 1.25, [P, 2, QK])
        subw = at("subw", K0 + 1.5, [P, DV])
        lamv = at("lamv", K0 + 1.75, [P, 8])
        strip = at("strip_mask", K0 + 1.78125, [P, 4])
        dcol = at("dcol", K0 + 1.8125, [P, NG])
        glub = at("glub", K0 + 1.9375, [P, 4])
        outw = at("outw", K0 + 1.9375 + 0.03125, [P, 4])
        att_s = at("att_small", K0 + 2.0, [P, 2, 8])
        qk_s = at("qk_small", K0 + 2.0625, [P, 3, 2 * HEADS])
        sq_s = at("sq_small", K0 + 2.25, [P, 32])
        ring = at("dense_ring", A, [P, RING, KT, 512])
        toep = at("toeplitz", A + 48, [P, NG, P])
        cbc = at("c_bcast", A + 48, [P, KT, P])
        S1 = at("state_ri", A + 32, [P, DG, CHUNKS])
        S2 = at("state_ir", A + 16, [P, DG, CHUNKS])
        scan_t = at("scan_tmp", B + 22, [P, 4, 256])
        Y = at("s5_y", A, [P, NG, CHUNKS])
        aT = at("probs_T", A + 8, [P, 2, NT, P])
        o_n = at("o_norm", A + 12, [P, 2, 512])
        yT = at("y_T", A + 16, [P, 4, S])
        gluw = at("glu_w", A + 24, [P, 4, 512])
        sT = at("s_T", A + 32, [P, 4, S])
        sqT = at("sq_T", A + 40, [P, 4, S])
        w1 = at("w1_ring", A, [P, W1C, 1024])
        inT = at("in_ops", B, [P, DG, P])
        wout = at("w_out", B, [P, KT, D])
        w2 = at("w2_ring", B, [P, W2C, 1024])
        outM = at("out_ops", C, [P, DG, STEPS + 1, GC])
        mod = at("modulation", DD, [P, 6, D])
        uT = at("u_T", DD, [P, 4, S])
        U = at("u_chunks", DD, [P, NG, CHUNKS])
        P2 = at("p2", EE, [P, GC, DG])
        Q2 = at("q2", EE + 4, [P, GC, DG])
        CP = at("cp", EE + 8, [P, DG, GC])
        CQ = at("cq", EE + 12, [P, DG, GC])
        BB = at("b_nat", FV, [DG, 3, NP * GC])
        tB = at("tmp_b", FV, [P, 1024])
        CC = at("c_nat", FV + 12, [P, 8, 3, NP])
        PW = at("powers", FV + 18, [P, 2, STEPS + 1, DG])
        t1 = at("tmp_1", FV + 22.5, [P, 1024])
        quad = at("quad", FV + 26.5, [DG, 4, 2, NP])
        AF = at("a_f", FV + 28.5, [P, 4, DG])
        lam_t = at("lam_tiles", FV + 22.5, [DG, 16, NP])
        kpad = at("kpad", FV, [GC, NG // 2, 15, GC])
        ccol = at("c_col", FV + 29.5, [P, 4, KT])
        lam_in = at("lam_in", FV + 29.625, [P, 4, QK])
        lam_w = at("lam_w", FV + 30.125, [P, 2, QK])
        posi = at("pos_i", FV + 30.5, [P, NT], I32)
        rope_t = at("rope_tmp", FV + 30.5625, [P, 8, NT, ROT_HALF])
        rope_i = at("rope_int", FV + 31.0625, [P, 64], I32)
        lstep = at("log_step", FV + 31.3125, [DG, 2])
        n1w = at("norm1_w", FV + 16, [P, D])
        hT = at("h_T", EE, [P, KT, S])
        catT = at("cat_T", EE, [P, 8, S])
        qkT = at("qk_T", FV, [P, 2, 4, S])
        vv = at("v", FV + 16, [P, NT, 512])
        xt = at("x_tile", G, [P, 2, D])
        stg = at("qk_stage", G, [P, 2, 512])
        sqb = at("qk_square", G + 4, [P, 2, 512])
        ee = at("probs", G, [P, 2, 2, 512])
        psq = at("chunk_powers", B + 16, [P, 2, 9, DG])
        scan_w = at("power_tmp", B + 20.75, [P, 4 * DG])
        qm = at("q_T_masked", B, [P, 2, 4, 4, P])
        xr = at("x_again", C, [P, 2, D])
        x1 = at("x1_tile", C + 8, [P, 2, D])
        h2 = at("h2_tile", C + 16, [P, 2, D])
        h2T = at("h2_T", C + 24, [P, KT, P])
        n2w = at("norm2_w", C + 28, [P, D])
        packed = [C + 32]

        def pack(name, shape, dt=F32):
            t = at(name, packed[0], shape, dt)
            packed[0] += -(-int(np.prod(shape[1:])) * (2 if dt == BF16 else 4) // 32) / 32
            assert packed[0] <= DD
            return t

        rw = pack("router_w", [P, KT, E])
        rb = pack("router_b", [P, E])
        lg = pack("logits", [P, E])
        mx8 = pack("max8", [P, 8])
        ix8 = pack("ix8", [P, 8], U32)
        ixf = pack("ixf", [P, 8])
        gat = pack("gates", [P, NT, TOPK])
        gs = pack("gate_sum", [P, 8])
        iotaE = pack("iota_e", [P, MAXB])
        tri = pack("tri", [P, P], BF16)
        onb = pack("ones_bf", [P, P], BF16)
        mask = pack("mask", [P, NT, E], BF16)
        oh4 = at("onehot4", FV + 18, [P, NT, TOPK, E])
        slotE = at("slot_e", EE + 2, [P, NT, E])
        rt = at("route_tmp", EE + 2.5, [P, 8, E])
        ec = at("expert_counts", EE + 12, [P, 3, 2, E])
        cmpl = at("load_cmp", G, [P, E + 2, E])
        tabf = at("tables_f", G + 4.25, [P, 3, MAXB + 2])
        cmpb = at("block_cmp", EE + 4, [P, MAXB, E])
        prod = at("route_prod", EE + 10, [P, NT * TOPK, E])
        tokid = pack("tok_id", [P, NT * TOPK, 4], BF16)
        dslot = pack("slots", [P, NT * TOPK])
        ebf = pack("block_expert", [P, MAXB + 2])
        load_expert = pack("load_expert", [P, E + 2], I32)
        load_after = pack("load_after", [P, E + 2], I32)
        block_load = pack("block_load", [P, MAXB + 2], I32)
        nbi = pack("n_blocks", [P, 2], I32)
        eye96 = pack("sel_cols", [96, MAXB + 2], BF16)
        pm = pack("part_mod", [P, 4])
        ones = pack("ones", [P, P])
        xs = at("xs", EE, [P, D])
        xT = [at("xs_T_hi", EE + 4, [P, KT, P], F32R), at("xs_T_lo", G, [P, KT, P], F32R)]
        actT = [at("act_T_hi", EE + 8, [P, KT, P], F32R), at("act_T_lo", G + 4, [P, KT, P], F32R)]
        w_split = [[at(f"w_{part}{i}", (C if i < 4 else DD - 32) + 8 * i + 4 * j, [P, 1024], F32R)
                    for j, part in enumerate(("hi", "lo"))] for i in range(SPLIT)]
        ysb = at("y_rows_sb", EE + 12, [P, D])
        glu = at("glu", FV, [P, 3, 512])
        lin = at("lin", FV + 6, [P, 3, 512])
        bsrc = at("b_src", FV, [96, 3072])
        bcat = at("b_cat", FV + 12, [96, 3072], BF16)
        ohs = at("slot_onehot", FV + 18, [P, NT * TOPK, P], BF16)
        iotab = at("iota_slots", FV + 22, [P, P])
        selb = at("expert_sel", FV + 22.5, [96, P], BF16)
        idx = at("row_idx", FV + 22.75, [P, 4], I32)
        idf = at("row_idx_f", FV + 22.8125, [P, 2])
        fing = at("final_rows", A, [P, 16, D])
        fx1 = at("final_x1", B, [P, NT, D])
        facc = at("final_acc", B + 16, [P, NT, D])

        def raw(c):
            return w1[:, c, :] if c < W1C else w2[:, c - W1C, :]
        bank = [ctx.enter_context(nc.psum_tensor(f"bank{i}", [P, 512], F32)) for i in range(8)]

        dram = {n: nc.dram_tensor(n, sh, F32, kind="Internal").ap() for n, sh in {
            "u_rows": [512, 512], "y_rows": [512, 512], "x1_rows": [S, D], "h2_rows": [S, D],
            "ys_rows": [S * TOPK, D]}.items()}

        names = """ident_ready  s5_nat lam_loaded c_loaded adab_loaded x_loaded0 x_loaded1 n1w_loaded misc_loaded
          pe_prep cq_ready bx_ready quad_ready af_psum af_ready inraw_ready in_tr in_done outm_ready k_mm k_ev kp_half
           sg_ready cbc_ready ada_mm ada_ev dve act pool   lam_e act_lam act_trig act_rope
          sq1 rs1 h_ready h_tr h_ev u_mm u_ev u_stored u_loaded q_mm q_sq q_ss q_rt q_n q_tr q_ev v_ev qm_ready s_mm s_ev scan_done
          sc_mm sc_max sc_exp a_ready a_tr a_ev pv_mm o_sq o_copied o_ss o_rt o_n o_tr o_ev 
          y_mm y_ev y_gp y_sig y_done y_stored y_loaded gluw_loaded g_mm g_sig s_act s_sq n_mm n_rt s5_done
          wout_loaded xr_loaded0 xr_loaded1 n2w_loaded rw_loaded mix_mm x1_ready x1_stored0 x1_stored1 m_sq m_rt h2_ready h2_stored0 h2_stored1 h2_tr h2_ev
          r_mm lg_ready g_exp mask_ready pos_mm blocks_ready consts2 bias_src bias_ready d_ready
          oh_ready idx_mm idx_ready xs_loaded idx_sum scat_ready xs_tr xs_ev x_lo sel_ready hi_done lo_dve lo_pool
          g_min g_sg l_a l_b act_ready act_tr act_ev act_lo y2_ev y2_stored
          fin_g0 fin_g1 fin_g2 fin_g3 fin_x1 fin_done fin_stored""".split()
        s = {n: sem(n) for n in names}
        ring_sem = [sem(f"ring_loaded{i}") for i in range(RING)]
        w_loaded = [sem(f"w_loaded{c}") for c in range(WCH // 2)]
        w_used = sem("w_used")
        ctx.enter_context(nc.allow_non_contiguous_dma(reason="vectors of a few hundred words"))
        ctx.enter_context(nc.allow_low_precision(reason="sums of a one and zeros, or small whole numbers"))
        block = ctx.enter_context(nc.Block())

        ada_v = I["ada_w"][0].rearrange("(k p) n -> p k n", p=P)
        win_v = I["w_in"][0].rearrange("(k p) n -> p k n", p=P)
        xv = I["x"][0].rearrange("(j i) d -> i j d", i=STEPS)
        ov = out[0].rearrange("(j i) d -> i j d", i=STEPS)

        def low_ready(c, b):
            mine, name = (POOL_LOW, "lo_pool") if c in POOL_LOW else (DVE_LOW, "lo_dve")
            return s[name], b * len(mine) + (mine.index(c) + 1)

        @block.sync
        def _(sp):
            for k, n in enumerate(("s5_cmat_re", "s5_cmat_im", "s5_cmat_re")):
                sp.dma_start(CC[:, :, k, :], I[n][0].rearrange("d g c p -> (d g c) p")
                             .rearrange("(t q) p -> q t p", q=P)).then_inc(s["s5_nat"], 16)
            for k, n in enumerate(("s5_b_re", "s5_b_im", "s5_b_re")):
                sp.dma_start(BB[:, k, :], I[n][0].rearrange("d g p c -> (d g) (p c)")).then_inc(s["s5_nat"], 16)
            sp.dma_start(lam_t[:, 0, :], I["s5_lambda_re"][0].rearrange("d g p -> (d g) p")).then_inc(s["lam_loaded"], 16)
            sp.dma_start(lam_t[:, 1, :], I["s5_lambda_im"][0].rearrange("d g p -> (d g) p")).then_inc(s["lam_loaded"], 16)
            sp.dma_start(lstep[:, 0:1], I["s5_log_step"][0].rearrange("d (g o) -> (d g) o", o=1)).then_inc(s["lam_loaded"], 16)
            w_in_at = {U_CHUNK: 3, Q_CHUNK: 0, K_CHUNK: 1, V_CHUNK: 2}

            def dense(n):
                if n - RING >= ADA_CHUNKS:
                    sp.wait_ge(s["u_mm"], 4)
                elif n >= RING:
                    sp.wait_ge(s["ada_mm"], n - RING + 1)
                src = ada_v[:, :, n * 512:(n + 1) * 512] if n < ADA_CHUNKS else \
                    win_v[:, :, w_in_at[n] * 512:(w_in_at[n] + 1) * 512]
                sp.dma_start(ring[:, n % RING], src).then_inc(ring_sem[n % RING], 16)
            for n in range(V_CHUNK):
                dense(n)
                if n == 0:
                    sp.dma_start(mod[:].rearrange("p a d -> p (a d)"),
                                 I["ada_b"][0].partition_broadcast(P)).then_inc(s["adab_loaded"], 16)
            for half in range(2):
                sp.wait_ge(s["k_ev"], 8 * (half + 1))
                if half == 0:
                    sp.wait_ge(s["ada_mm"], ADA_CHUNKS)
                gsl = slice(half * NG // 2, (half + 1) * NG // 2)
                for i in range(STEPS):
                    sp.dma_start(toep[i * GC:(i + 1) * GC, gsl, :].rearrange("p g (a c) -> p g a c", c=GC),
                                 kpad[:, :, 7 - i:15 - i, :]).then_inc(s["kp_half"], 16)
                if half == 0:
                    sp.wait_ge(s["kp_half"], 16 * STEPS)
            sp.wait_ge(s["inraw_ready"], 1)
            sp.wait_ge(s["outm_ready"], 1)
            sp.dma_start(n1w[:], I["norm1_w"][0].partition_broadcast(P)).then_inc(s["n1w_loaded"], 16)
            for t in range(NT):
                if t >= 2:
                    sp.wait_ge(s["h_tr"], t - 1)
                for k in range(2):
                    sp.dma_start(xt[64 * k:64 * k + 64, t % 2, :], xv[2 * t + k]).then_inc(s[f"x_loaded{t % 2}"], 16)
            dense(V_CHUNK)
            sp.wait_ge(s["u_ev"], 4)
            sp.dma_start(dram["u_rows"].rearrange("(t p) n -> p t n", p=P), uT[:]).then_inc(s["u_stored"], 16)
            sp.wait_ge(s["u_stored"], 16)
            u_v = dram["u_rows"].rearrange("(g c) (i j) -> i c g j", c=GC, i=STEPS)
            for i in range(STEPS):
                sp.dma_start(U[i * GC:(i + 1) * GC], u_v[i]).then_inc(s["u_loaded"], 16)
            sp.wait_ge(s["scan_done"], 2)
            sp.dma_start(gluw[:], I["s5_glu_w"][0].rearrange("(k p) n -> p k n", p=P)).then_inc(s["gluw_loaded"], 16)
            sp.wait_ge(s["sc_mm"], 2 * NT * HEADS)
            sp.dma_start(wout[:], I["w_out"][0].rearrange("(k p) n -> p k n", p=P)).then_inc(s["wout_loaded"], 16)
            sp.wait_ge(s["y_done"], 1)
            y_v = dram["y_rows"].rearrange("(g c) (i j) -> i c g j", c=GC, i=STEPS)
            for i in range(STEPS):
                sp.dma_start(y_v[i], Y[i * GC:(i + 1) * GC]).then_inc(s["y_stored"], 16)
            sp.wait_ge(s["y_stored"], 128)
            sp.dma_start(yT[:], dram["y_rows"].rearrange("(t p) n -> p t n", p=P)).then_inc(s["y_loaded"], 16)
            sp.dma_start(n2w[:], I["norm2_w"][0].partition_broadcast(P)).then_inc(s["n2w_loaded"], 16)
            sp.dma_start(rw[:], I["router_w"][0].rearrange("(k p) n -> p k n", p=P)).then_inc(s["rw_loaded"], 16)
            sp.dma_start(rb[:], I["router_b"][0].partition_broadcast(P)).then_inc(s["rw_loaded"], 16)
            sp.wait_ge(s["pv_mm"], NT * HEADS)
            for q in range(3):
                sp.dma_start(bsrc[32 * q:32 * q + 32, 0:2048], I["mlp1_b"][0]).then_inc(s["bias_src"], 16)
                sp.dma_start(bsrc[32 * q:32 * q + 32, 2048:3072], I["mlp2_b"][0]).then_inc(s["bias_src"], 16)
            for t in range(NT):
                if t >= 2:
                    sp.wait_ge(s["x1_ready"], t - 1)
                for k in range(2):
                    sp.dma_start(xr[64 * k:64 * k + 64, t % 2, :], xv[2 * t + k]).then_inc(s[f"xr_loaded{t % 2}"], 16)
                sp.wait_ge(s["x1_ready"], t + 1)
                sp.dma_start(dram["x1_rows"][t * P:(t + 1) * P, :], x1[:, t % 2, :]).then_inc(s[f"x1_stored{t % 2}"], 16)
                sp.wait_ge(s["h2_ready"], t + 1)
                sp.dma_start(dram["h2_rows"][t * P:(t + 1) * P, :], h2[:, t % 2, :]).then_inc(s[f"h2_stored{t % 2}"], 16)
            sp.wait_ge(s["s5_done"], 4)
            sp.wait_ge(s["mix_mm"], NT)
            sp.wait_ge(s["blocks_ready"], 1)
            n_blocks = sp.value_load(nbi[0:1, 0:1], min_val=1, max_val=MAXB)
            n_loads = sp.value_load(nbi[0:1, 1:2], min_val=1, max_val=E)

            def weights(chunks, n):
                e = sp.value_load(load_expert[0:1, bass.ds(n, 1)], min_val=0, max_val=E - 1)
                first = isinstance(n, int) and n == 0
                if not first:
                    last_block = sp.value_load(load_after[0:1, bass.ds(n, 1)], min_val=0, max_val=MAXB - 1)
                for c in chunks:
                    if not first:
                        sp.wait_ge(*low_ready(c, last_block))
                    half, k = c // KT, c % KT
                    src = I["mlp1_w"][0, bass.ds(e, 1), k * P:(k + 1) * P, half * 1024:half * 1024 + 1024] \
                        if c < W1C else I["mlp2_w"][0, bass.ds(e, 1), k * P:(k + 1) * P, :]
                    sp.dma_start(raw(c), src.rearrange("e p n -> (e p) n")).then_inc(w_loaded[c // 2], 16)

            weights(range(WCH), 0)
            weights(range(SPLIT), 1)
            with sp.Fori(1, n_loads) as n:
                weights(range(SPLIT, WCH), n)
                weights(range(SPLIT), n + 1)
            sp.wait_ge(s["y2_stored"], n_blocks * 16 + 16)
            sp.wait_ge(s["fin_done"], 1)
            for t in range(NT):
                sp.dma_start(fing[:, TOPK * t:TOPK * t + TOPK, :].rearrange("p k d -> p (k d)"),
                             dram["ys_rows"][t * P * TOPK:(t + 1) * P * TOPK, :]
                             .rearrange("(p k) d -> p (k d)", k=TOPK)).then_inc(s[f"fin_g{t}"], 16)
            sp.dma_start(fx1[:], dram["x1_rows"].rearrange("(t p) n -> p t n", p=P)).then_inc(s["fin_x1"], 16)
            for t in range(NT):
                sp.wait_ge(s["fin_done"], t + 2)
                for k in range(2):
                    sp.dma_start(ov[2 * t + k], facc[64 * k:64 * k + 64, t, :]).then_inc(s["fin_stored"], 16)
            sp.wait_ge(s["fin_stored"], 32 * NT)

        @block.gpsimd
        def _(pool):
            ch = Chain(pool, s["pool"])
            ch(pool.memset(ident[:], 0.0))
            ch(pool.memset(ones[:], 1.0))
            pool.affine_select(out=ident[:], in_=ident[:], compare_op=ALU.not_equal, fill=1.0, base=0,
                               pattern=[[-1, P]], channel_multiplier=1).then_inc(s["ident_ready"], 1)
            pool.wait_ge(s["ident_ready"], 1)
            ch(pool.memset(sgn[0:64, 0:1], -1.0))
            ch(pool.memset(sgn[64:128, 0:1], 1.0))
            ch(pool.memset(sgn[0:64, 1:2], 1.0))
            ch(pool.memset(sgn[64:128, 1:2], -1.0))
            ch(pool.memset(sgn[:, 2:3], EPS))
            ch(pool.memset(strip[:], 0.0))
            for m in range(4):
                ch(pool.memset(strip[32 * m:32 * m + 32, m:m + 1], 1.0))
            ch.sync()
            pool.dma_start(lam_in[:, 0], I["lambda_q1"][0].partition_broadcast(P)).then_inc(s["misc_loaded"], 16)
            pool.dma_start(lam_in[:, 1], I["lambda_q2"][0].partition_broadcast(P)).then_inc(s["misc_loaded"], 16)
            pool.dma_start(lam_in[:, 2], I["lambda_k1"][0].partition_broadcast(P)).then_inc(s["misc_loaded"], 16)
            pool.dma_start(lam_in[:, 3], I["lambda_k2"][0].partition_broadcast(P)).then_inc(s["misc_loaded"], 16)
            pool.dma_start(qkw[:, 0], I["q_norm_w"][0].partition_broadcast(P)).then_inc(s["misc_loaded"], 16)
            pool.dma_start(qkw[:, 1], I["k_norm_w"][0].partition_broadcast(P)).then_inc(s["misc_loaded"], 16)
            pool.dma_start(subw[:], I["subln_w"][0].partition_broadcast(P)).then_inc(s["misc_loaded"], 16)
            pos_v = I["positions"][0].rearrange("(j i o) -> i j o", i=STEPS, o=1)
            for i in range(STEPS):
                pool.dma_start(posi[64 * (i % 2):64 * (i % 2) + 64, i // 2:i // 2 + 1], pos_v[i]).then_inc(s["misc_loaded"], 16)
                pool.dma_start(dcol[i * GC:(i + 1) * GC, :], I["s5_d"][0].rearrange("(g c) -> c g", c=GC)).then_inc(s["misc_loaded"], 16)
            pool.dma_start(glub[:], I["s5_glu_b"][0].rearrange("(t p) -> p t", p=P)).then_inc(s["misc_loaded"], 16)
            pool.dma_start(outw[:], I["s5_out_norm_w"][0].rearrange("(t p) -> p t", p=P)).then_inc(s["misc_loaded"], 16)
            pool.dma_start(ccol[:, 0, :], I["c"][0].rearrange("(t p) -> p t", p=P)).then_inc(s["c_loaded"], 16)
            pool.wait_ge(s["s_mm"], 2 * DG // 8)

            def cmul(dst, x, y, n):
                X = [psq[:, q, x:x + n, :] for q in range(2)]
                Yb = [bc(psq[:, q, y, :], 1, n, [P, n, DG]) for q in range(2)]
                T = scan_w[:, 0:n * DG].rearrange("p (n g) -> p n g", g=DG)
                O = [psq[:, q, dst:dst + n, :] for q in range(2)]
                ch(pool.tensor_tensor(O[0], X[0], Yb[0], ALU.mult))
                ch(pool.tensor_tensor(T, X[1], Yb[1], ALU.mult))
                ch(pool.tensor_tensor(O[0], O[0], T, ALU.subtract))
                ch(pool.tensor_tensor(O[1], X[0], Yb[1], ALU.mult))
                ch(pool.tensor_tensor(T, X[1], Yb[0], ALU.mult))
                ch(pool.tensor_tensor(O[1], O[1], T, ALU.add))

            pool.wait_ge(s["sg_ready"], 1)
            ch(pool.tensor_copy(psq[:, 0, 1, :], ab8[:, 0, :]))
            ch(pool.tensor_copy(psq[:, 1, 1, :], ab8[:, 1, :]))
            cmul(2, 1, 1, 1)
            cmul(3, 1, 2, 2)
            cmul(5, 1, 4, 4)
            pool.wait_ge(s["s_ev"], 2 * DG // 8)
            dirs = ((0, range(1, 8), -1), (1, range(6, -1, -1), 1))

            def view(T, di):
                return T[:, di * NG:(di + 1) * NG, :].rearrange("p g (c m) -> p g c m", m=8)

            def step(x1n, x2n, x1p, x2p, are, aim, sub, shape, keep2=True):
                T = [scan_t[:, q, 0:int(np.prod(shape))].rearrange("p (g c) -> p g c", g=NG) for q in range(4)]
                ch(pool.tensor_tensor(T[0], x1p, are, ALU.mult))
                if keep2:
                    ch(pool.tensor_tensor(T[2], x2p, are, ALU.mult))
                    ch(pool.tensor_tensor(T[3], x1p, aim, ALU.mult))
                ch(pool.tensor_tensor(T[1], x2p, aim, ALU.mult))
                ch(pool.tensor_tensor(x1n, x1n, T[0], ALU.add))
                if keep2:
                    ch(pool.tensor_tensor(x2n, x2n, T[2], ALU.add))
                ch.sync()
                if keep2:
                    ch(pool.tensor_tensor(x2n, x2n, T[3], ALU.subtract))
                ch(pool.tensor_tensor(x1n, x1n, T[1], ALU.add))

            for di, order, back in dirs:
                V1, V2 = view(S1, di), view(S2, di)
                gs_ = slice(di * NG, (di + 1) * NG)

                def pw(q, k, n):
                    return bc(psq[:, q, k, gs_], 2, n, [P, NG, n])
                for m in order:
                    step(V1[:, :, :, m], V2[:, :, :, m], V1[:, :, :, m + back], V2[:, :, :, m + back],
                         pw(0, 1, 8), pw(1, 1, 8), None, [NG, 8])
                end = 7 if di == 0 else 0
                for c in (range(1, 8) if di == 0 else range(6, -1, -1)):
                    step(V1[:, :, c:c + 1, end], V2[:, :, c:c + 1, end], V1[:, :, c + back:c + back + 1, end],
                         V2[:, :, c + back:c + back + 1, end], pw(0, 8, 1), pw(1, 8, 1), None, [NG, 1])
                for m in range(7) if di == 0 else range(7, 0, -1):
                    k = m + 1 if di == 0 else 8 - m
                    dst = slice(1, 8) if di == 0 else slice(0, 7)
                    src = slice(0, 7) if di == 0 else slice(1, 8)
                    step(V1[:, :, dst, m], None, V1[:, :, src, end], V2[:, :, src, end],
                         pw(0, k, 7), pw(1, k, 7), None, [NG, 7], keep2=False)
                pool.nop().then_inc(s["scan_done"], 1)
            pool.wait_ge(s["y_ev"], 4)
            ch(pool.iota(iotaE[:], pattern=[[1, MAXB]], base=0, channel_multiplier=0, allow_small_or_imprecise_dtypes=True))
            ch(pool.memset(onb[:], 1.0))
            ch(pool.memset(tri[:], 1.0))
            ch(pool.memset(ones[:], 1.0))
            for q in range(3):
                ch(pool.iota(pm[32 * q:32 * q + 32, 0:1], pattern=[[1, 1]], base=0, channel_multiplier=1, allow_small_or_imprecise_dtypes=True))
            for col, pat, mult in ((0, [[0, NT], [0, TOPK]], 4), (1, [[TOPK * P, NT], [0, TOPK]], 0),
                                   (2, [[0, NT], [1, TOPK]], 0)):
                ch(pool.iota(tokid[:, :, col].rearrange("p (t k) -> p t k", k=TOPK), pattern=pat, base=0,
                             channel_multiplier=mult, allow_small_or_imprecise_dtypes=True))
            ch(pool.memset(tokid[:, :, 3:4], -UNUSED))
            ch.sync()
            pool.affine_select(out=tri[:], in_=tri[:], compare_op=ALU.is_gt, fill=0.0, base=0,
                               pattern=[[1, P]], channel_multiplier=-1).then_inc(s["consts2"], 1)
            pool.wait_ge(s["bias_src"], 96)
            ch(pool.tensor_copy(bcat[:], bsrc[:]))
            for q in (1, 2):
                ch(pool.tensor_tensor(bsrc[32 * q:32 * q + 32], bsrc[32 * q:32 * q + 32],
                                           bcat[32 * q:32 * q + 32], ALU.subtract))
            ch.sync()
            for q in (1, 2):
                ch(pool.tensor_copy(bcat[32 * q:32 * q + 32], bsrc[32 * q:32 * q + 32]))
            ch.sync()
            ch(pool.tensor_tensor(bsrc[64:96], bsrc[64:96], bcat[64:96], ALU.subtract))
            pool.tensor_copy(bcat[64:96], bsrc[64:96]).then_inc(s["bias_ready"], 1)
            pool.wait_ge(s["bias_ready"], 1)
            pool.iota(iotab[:], pattern=[[1, P]], base=0, channel_multiplier=0,
                      allow_small_or_imprecise_dtypes=True).then_inc(s["bias_ready"], 1)
            pool.wait_ge(s["h2_stored0"], 32)
            pool.wait_ge(s["h2_stored1"], 32)
            pool.wait_ge(s["blocks_ready"], 2)
            n_blocks = pool.value_load(nbi[0:1, 0:1], min_val=1, max_val=MAXB)

            last_token, last_row = pool.to_reg(S - 1), pool.to_reg(S * TOPK - 1)

            def low(c, b):
                pool.wait_ge(s["hi_done"], b * WCH + (c + 1))
                hi, lo = w_split[c % SPLIT]
                pool.tensor_tensor(out=lo[:], in0=raw(c), in1=hi[:].bitcast(F32), op=ALU.subtract).then_inc(s["lo_pool"], 1)

            def gather(first):
                pool.wait_ge(s["idx_ready"], first)
                pool.sem_inc(s["pool"], 1)
                pool.indirect_dma_start(out=xs[:], out_offset=None, in_=dram["h2_rows"],
                                        in_offset=bass.IndirectOffsetOnAxis(ap=idx[:, 0:1], axis=0),
                                        bounds_check=last_token).then_inc(s["xs_loaded"], 16)
            gather(1)
            pool.dma_start(ysb[:, 0:E], dram["h2_rows"][0:P, 0:E]).then_inc(s["y2_stored"], 16)
            with pool.Fori(0, n_blocks) as b:
                v, next2 = b + 1, b * 2 + 4
                low(POOL_LOW[0], b)
                pool.wait_ge(s["xs_tr"], b * 2 + 2)
                gather(b * 2 + 3)
                pool.wait_ge(s["idx_ready"], b * 2 + 2)
                pool.wait_ge(s["y2_stored"], v * 16)
                pool.sem_inc(s["pool"], 1)
                pool.tensor_copy(idx[:, 2:3], idx[:, 1:2]).then_inc(s["scat_ready"], 1)
                low(POOL_LOW[1], b)
                for c in POOL_LOW[2:]:
                    low(c, b)
                pool.wait_ge(s["y2_ev"], next2)
                pool.wait_ge(s["scat_ready"], v)
                pool.sem_inc(s["pool"], 1)
                pool.indirect_dma_start(out=dram["ys_rows"], in_=ysb[:], in_offset=None,
                                        out_offset=bass.IndirectOffsetOnAxis(ap=idx[:, 2:3], axis=0),
                                        bounds_check=last_row, oob_is_err=False).then_inc(s["y2_stored"], 16)
        @block.scalar
        def _(act):
            ch = Chain(act, s["act"])
            act.wait_ge(s["c_loaded"], 16)
            act.activation(ccol[:, 1, :], ccol[:, 0, :], ACT.Sigmoid).then_inc(s["lam_e"], 1)
            act.wait_ge(s["ident_ready"], 1)
            act.wait_ge(s["pool"], 7)
            act.wait_ge(s["pe_prep"], 1)
            for b in range(2):
                ch.free(act.activation(CP[:].rearrange("p g c -> p (g c)")[:, 512 * b:512 * b + 512], bank[b][:], ACT.Identity,
                                       scale=sgn[:, 1:2]))
                act.activation(CQ[:].rearrange("p g c -> p (g c)")[:, 512 * b:512 * b + 512], bank[2 + b][:], ACT.Identity,
                               scale=-1.0).then_inc(s["cq_ready"], 1)
            ch.sync()
            act.wait_ge(s["pe_prep"], 2)
            for b in range(2):
                act.activation(P2[:].rearrange("p c g -> p (c g)")[:, 512 * b:512 * b + 512], bank[4 + b][:], ACT.Identity).then_inc(s["bx_ready"], 1)
                act.activation(Q2[:].rearrange("p c g -> p (c g)")[:, 512 * b:512 * b + 512], bank[6 + b][:], ACT.Identity,
                               scale=sgn[:, 0:1]).then_inc(s["bx_ready"], 1)
            act.wait_ge(s["lam_loaded"], 48)
            ch(act.activation(lstep[:, 1:2], lstep[:, 0:1], ACT.Exp))
            act.activation(lam_t[:, 2, :], lam_t[:, 0, :], ACT.Exp, scale=lstep[:, 1:2]).then_inc(s["act_lam"], 1)
            act.wait_ge(s["act_rope"], 1)
            act.activation(lamv[:, 2:4], lamv[:, 0:2], ACT.Exp).then_inc(s["act_lam"], 1)
            act.wait_ge(s["act_trig"], 1)
            act.activation(lam_t[:, 4:6, :], lam_t[:, 4:6, :], ACT.Sin).then_inc(s["lam_e"], 1)
            act.wait_ge(s["act_rope"], 2)
            act.activation(cs[:].rearrange("p a t k -> p (a t k)"), rope_t[:, 0:2].rearrange("p a t k -> p (a t k)"),
                           ACT.Sin).then_inc(s["lam_e"], 1)
            act.wait_ge(s["af_psum"], 1)
            act.activation(AF[:].rearrange("p a g -> p (a g)"), bank[2][:, 0:4 * DG], ACT.Identity).then_inc(s["af_ready"], 1)
            for n in range(DG // 4):
                act.wait_ge(s["in_tr"], n + 1)
                act.activation(inT[:, 4 * n:4 * n + 4, :].rearrange("p g m -> p (g m)"), bank[2 + n % 4][:], ACT.Identity).then_inc(s["in_done"], 1)
            for n in range(NG // 2):
                act.wait_ge(s["k_mm"], n + 1)
                if n == 8:
                    act.wait_ge(s["kp_half"], 16 * STEPS)
                act.activation(kpad[:, 2 * (n % 8):2 * (n % 8) + 2].rearrange("p g a c -> p (g a c)"),
                               bank[6 + n % 2][0:GC, 0:480], ACT.Identity).then_inc(s["k_ev"], 1)
            for t in range(NT):
                act.wait_ge(s[f"x_loaded{t % 2}"], 32 * (t // 2 + 1))
                if t:
                    act.wait_ge(s["rs1"], t)
                for k in range(2):
                    ch.free(act.activation(bank[6 + k][:], xt[:, t % 2, 512 * k:512 * k + 512], ACT.Square,
                                           accum_out=sq_s[:, k:k + 1]))
                ch.sync()
                act.nop().then_inc(s["sq1"], 1)
                act.wait_ge(s["m_sq"], t + 1)
                act.activation(sq_s[:, 3:4], sq_s[:, 2:3], ACT.Sqrt, scale=1.0 / D, bias=sgn[:, 2:3]).then_inc(s["sq1"], 1)
                act.wait_ge(s["h_tr"], t + 1)
                for k in range(2):
                    act.activation(hT[:, 4 * k:4 * k + 4, t * P:(t + 1) * P],
                                   bank[2 * (t % 2) + k][:].rearrange("p (k n) -> p k n", n=P), ACT.Identity).then_inc(s["h_ev"], 1)
            for n in range(4):
                act.wait_ge(s["u_mm"], n + 1)
                act.activation(uT[:, n, :], bank[n][:], ACT.Identity).then_inc(s["u_ev"], 1)
            def qk_rms(n):
                bk = bank[4 + n] if n < 4 else bank[n - 4]
                act.wait_ge(s["q_mm"], n + 1)
                if n >= 2:
                    act.wait_ge(s["q_ss"], n - 1)
                act.activation(sqb[:, n % 2, :], bk[:], ACT.Square).then_inc(s["q_sq"], 1)
                act.wait_ge(s["q_ss"], n + 1)
                act.activation(qk_s[:, 1, :], qk_s[:, 0, :], ACT.Sqrt, scale=1.0 / QK, bias=sgn[:, 2:3]).then_inc(s["q_rt"], 1)

            def qk_out(n):
                act.wait_ge(s["q_tr"], n + 1)
                bk = bank[4 + n] if n < 4 else bank[n - 4]
                act.activation(qkT[:, n // 4, :, (n % 4) * P:(n % 4) * P + P],
                               bk[:].rearrange("p (b n) -> p b n", n=P), ACT.Identity).then_inc(s["q_ev"], 1)
            def scan_inputs(n):
                for k in range(2):
                    act.wait_ge(s["s_mm"], 2 * n + k + 1)
                    act.activation((S1, S2)[k][:, 8 * n:8 * n + 8, :].rearrange("p g j -> p (g j)"),
                                   bank[4 + 2 * (n % 2) + k][:], ACT.Identity).then_inc(s["s_ev"], 1)
            for n in range(8):
                qk_rms(n)
                if n >= 4:
                    scan_inputs(2 * n - 8)
                    scan_inputs(2 * n - 7)
                qk_out(n)
            for n in range(4):
                act.wait_ge(s["q_mm"], 8 + n + 1)
                act.activation(vv[:, n, :], bank[4 + n][:], ACT.Identity).then_inc(s["v_ev"], 1)
            scale = QK ** -0.5
            act.wait_ge(s["q_ev"], 8)
            act.wait_ge(s["pool"], 12)

            def q_masked(t, m):
                act.activation(qm[:, t % 2, m], qkT[:, 0, :, t * P:(t + 1) * P], ACT.Identity,
                               scale=strip[:, m:m + 1]).then_inc(s["qm_ready"], 1)
            for m in range(4):
                q_masked(0, m)

            def probs_out(m):
                act.wait_ge(s["a_tr"], m + 1)
                if m >= 2:
                    act.wait_ge(s["pv_mm"], m - 1)
                act.activation(aT[:, m % 2].rearrange("p k q -> p (k q)"), bank[4 + m % 2][:],
                               ACT.Identity).then_inc(s["a_ev"], 1)
            for n in range(NT * HEADS):
                t, h = n // HEADS, n % HEADS
                act.wait_ge(s["sc_max"], n + 1)
                if n >= 2:
                    act.wait_ge(s["a_tr"], n - 1)
                for c in range(2):
                    act.activation(ee[:, n % 2, c, :], bank[2 * (n % 2) + c][:], ACT.Exp, scale=scale,
                                   bias=att_s[:, n % 2, 2 + c:3 + c],
                                   accum_out=att_s[:, n % 2, 4 + c:5 + c]).then_inc(s["sc_exp"], 1)
                if n >= 2:
                    probs_out(n - 2)
                if h < 4 and t + 1 < NT:
                    if t:
                        act.wait_ge(s["sc_mm"], 2 * HEADS * t)
                    q_masked(t + 1, h)
                if h == 3 and t >= 1:
                    o_norm_act(act, ch, s, bank, o_n, att_s, qk_s, sgn, catT, t - 1)
            probs_out(NT * HEADS - 2)
            probs_out(NT * HEADS - 1)
            o_norm_act(act, ch, s, bank, o_n, att_s, qk_s, sgn, catT, NT - 1)
            for n in range(4):
                act.wait_ge(s["y_mm"], n + 1)
                act.activation(Y[:, 8 * n:8 * n + 8, :].rearrange("p g j -> p (g j)"), bank[n][:], ACT.Identity).then_inc(s["y_ev"], 1)
            act.wait_ge(s["y_gp"], 1)
            act.activation(S2[:, 0:NG, :], S2[:, 0:NG, :], ACT.Sigmoid, scale=GELU_A).then_inc(s["y_sig"], 1)
            for n in range(4):
                act.wait_ge(s["g_mm"], n + 1)
                act.activation(sT[:, n, :], bank[4 + n][:], ACT.Sigmoid, bias=glub[:, n:n + 1]).then_inc(s["g_sig"], 1)
            for n in range(4):
                act.wait_ge(s["s_act"], n + 1)
                act.activation(sqT[:, n, :], sT[:, n, :], ACT.Square).then_inc(s["s_sq"], 1)
            act.wait_ge(s["n_mm"], 1)
            act.activation(gluw[:, 0, :], bank[0][:], ACT.Sqrt, scale=1.0 / 512, bias=sgn[:, 2:3]).then_inc(s["n_rt"], 1)
            for t in range(NT):
                act.wait_ge(s["x1_ready"], t + 1)
                if t:
                    act.wait_ge(s["h2_ready"], t)
                if t >= 2:
                    act.wait_ge(s[f"h2_stored{t % 2}"], 16 * (t // 2))
                    act.wait_ge(s["h2_tr"], t - 1)
                for k in range(2):
                    ch.free(act.activation(h2[:, t % 2, 512 * k:512 * k + 512], x1[:, t % 2, 512 * k:512 * k + 512],
                                           ACT.Square, accum_out=sq_s[:, 8 + k:9 + k]))
                ch.sync()
                act.nop().then_inc(s["o_sq"], 1)
                act.wait_ge(s["m_rt"], t + 1)
                act.activation(sq_s[:, 11:12], sq_s[:, 10:11], ACT.Sqrt, scale=1.0 / D, bias=sgn[:, 2:3]).then_inc(s["o_sq"], 1)
                act.wait_ge(s["h2_tr"], t + 1)
                for k in range(2):
                    act.activation(h2T[:, 4 * k:4 * k + 4, :].rearrange("p k n -> p (k n)"), bank[4 + k][:],
                                   ACT.Identity).then_inc(s["h2_ev"], 1)
                act.wait_ge(s["lg_ready"], t + 1)
                act.activation(gat[:, t, :], mx8[:, 0:TOPK], ACT.Exp, bias=gs[:, 2:3], accum_out=gs[:, 0:1]).then_inc(s["g_exp"], 1)
            act.wait_ge(s["blocks_ready"], 2)
            n_blocks = act.value_load(nbi[0:1, 0:1], min_val=1, max_val=MAXB)

            act.wait_ge(s["h2_stored0"], 32)
            act.wait_ge(s["h2_stored1"], 32)
            act.wait_ge(s["x1_stored0"], 32)
            act.wait_ge(s["x1_stored1"], 32)

            def loaded(b):
                return act.value_load(block_load[0:1, bass.ds(b, 1)], min_val=32, max_val=32 * (E + 1))

            def high(chunks, b, w_in, first=False):
                for c in chunks:
                    if c % 2 == 0 or c == chunks[0]:
                        act.wait_ge(w_loaded[c // 2], w_in)
                    if not first:
                        act.wait_ge(w_used, b * WCH + (c + 1 - SPLIT))
                    act.activation(w_split[c % SPLIT][0][:], raw(c), ACT.Identity).then_inc(s["hi_done"], 1)

            def x_out(k, b2):
                act.wait_ge(s["xs_tr"], b2 + (k + 1))
                act.activation(xT[0][:, 4 * k:4 * k + 4, :].rearrange("p k n -> p (k n)"), bank[7 - k][:],
                               ACT.Identity).then_inc(s["xs_ev"], 1)

            def gate(k, b2):
                act.wait_ge(s["g_min"], b2 + (k + 1))
                act.activation(glu[:, 1 + k, :] if k == 0 else lin[:, 2, :], glu[:, 0, :] if k == 0 else glu[:, 2, :],
                               ACT.Sigmoid, scale=1.702).then_inc(s["g_sg"], 1)

            def act_out(k, b2):
                act.wait_ge(s["act_tr"], b2 + (k + 1))
                act.activation(actT[0][:, 4 * k:4 * k + 4, :].rearrange("p k n -> p (k n)"), bank[6 + k][:],
                               ACT.Identity).then_inc(s["act_ev"], 1)
            high(range(SPLIT), 0, 32, first=True)
            x_out(0, 0)
            x_out(1, 0)
            act.sem_inc(s["y2_ev"], 2)
            with act.Fori(0, n_blocks) as b:
                b2, w_in, next_w_in = b * 2, loaded(b), loaded(b + 1)
                high(range(SPLIT, 14), b, w_in)
                gate(0, b2)
                high(range(14, 22), b, w_in)
                act_out(0, b2)
                gate(1, b2)
                x_out(0, b2 + 2)
                high(range(22, WCH), b, w_in)
                high(range(0, 1), b + 1, next_w_in)
                act_out(1, b2)
                x_out(1, b2 + 2)
                high(range(1, SPLIT), b + 1, next_w_in)
                act.wait_ge(w_used, b * WCH + WCH)
                act.wait_ge(s["scat_ready"], b + 1)
                for k in range(2):
                    act.activation(ysb[:, 512 * k:512 * k + 512], bank[4 + k][:], ACT.Identity).then_inc(s["y2_ev"], 1)

        @block.vector
        def _(dve):
            ch = Chain(dve, s["dve"])

            def tt(o, a, b_, op):
                return dve.tensor_tensor(o, a, b_, op)

            dve.wait_ge(s["c_loaded"], 16)
            dve.wait_ge(s["lam_e"], 1)
            ch(tt(ccol[:, 2, :], ccol[:, 0, :], ccol[:, 1, :], ALU.mult))
            dve.tensor_copy(cbc[:], bc(ccol[:, 2, :], 2, P, [P, KT, P])).then_inc(s["cbc_ready"], 1)

            def reduce_angle(dst, src, shift, tmp, tmpi):
                ch(dve.tensor_scalar(tmp, src, 1 / (2 * math.pi), shift / (2 * math.pi), ALU.mult, ALU.add))
                ch(dve.tensor_copy(tmpi, tmp))
                ch(dve.tensor_copy(tmp, tmpi))
                ch(dve.scalar_tensor_tensor(dst, tmp, -C1, src, ALU.mult, ALU.add))
                ch(dve.scalar_tensor_tensor(dst, tmp, -C2, dst, ALU.mult, ALU.add))
                ch(dve.scalar_tensor_tensor(dst, tmp, -C3, dst, ALU.mult, ALU.add))
                if shift:
                    ch(dve.tensor_scalar(dst, dst, shift, None, ALU.add))
                ch(dve.tensor_scalar(tmp, dst, -math.pi, 2 * math.pi, ALU.is_lt, ALU.mult))
                ch(tt(dst, dst, tmp, ALU.add))
                ch(dve.tensor_scalar(tmp, dst, math.pi, -2 * math.pi, ALU.is_gt, ALU.mult))
                ch(tt(dst, dst, tmp, ALU.add))
                ch(dve.tensor_scalar(dst, dst, 3.1415925, -3.1415925, ALU.min, ALU.max))

            L = [lam_t[:, k, :] for k in range(16)]
            dve.wait_ge(s["lam_loaded"], 48)
            dve.wait_ge(s["act_lam"], 1)
            ch(dve.tensor_scalar(L[3], L[1], lstep[:, 1:2], None, ALU.mult))
            reduce_angle(L[4], L[3], 0.0, L[6], rope_i[0:DG, :])
            reduce_angle(L[5], L[3], math.pi / 2, L[6], rope_i[0:DG, :])
            dve.nop().then_inc(s["act_trig"], 1)
            dve.wait_ge(s["misc_loaded"], 16 * 25)
            ch(tt(lam_w[:], lam_in[:, 0:2], lam_in[:, 2:4], ALU.mult))
            dve.tensor_reduce(lamv[:, 0:2], lam_w[:], AX.X, ALU.add).then_inc(s["act_rope"], 1)
            inv = [np.float32(ROPE_THETA) ** np.float32(-2 * k / (2 * ROT_HALF)) for k in range(ROT_HALF)]
            ch(dve.tensor_copy(rope_t[:, 2, :, 0], posi[:]))
            for k in range(ROT_HALF):
                ch.free(dve.tensor_scalar(rope_t[:, 3, :, k], rope_t[:, 2, :, 0], float(inv[k]), None, ALU.mult))
            ch.sync()

            def flat(k):
                return rope_t[:, k].rearrange("p t k -> p (t k)")
            reduce_angle(flat(0), flat(3), math.pi / 2, flat(4), rope_i[:, 0:16])
            reduce_angle(flat(1), flat(3), 0.0, flat(4), rope_i[:, 0:16])
            dve.nop().then_inc(s["act_rope"], 1)
            dve.wait_ge(s["act_lam"], 2)
            ch(tt(lamv[:, 4:5], lamv[:, 3:4], lamv[:, 2:3], ALU.subtract))
            ch(dve.tensor_scalar(lamv[:, 5:6], lamv[:, 4:5], -LAMBDA_INIT, None, ALU.add))
            dve.wait_ge(s["lam_e"], 2)
            ch.free(tt(quad[:, 0, 0, :], L[2], L[5], ALU.mult))
            ch.free(tt(quad[:, 1, 0, :], L[2], L[4], ALU.mult))
            ch.free(tt(L[7], L[0], L[0], ALU.mult))
            ch(tt(L[8], L[1], L[1], ALU.mult))
            ch.free(tt(L[7], L[7], L[8], ALU.add))
            ch(dve.tensor_scalar(L[9], quad[:, 0, 0, :], -1.0, None, ALU.add))
            ch.free(dve.reciprocal(L[7], L[7]))
            ch.free(tt(L[10], L[9], L[0], ALU.mult))
            ch.free(tt(L[11], quad[:, 1, 0, :], L[1], ALU.mult))
            ch.free(tt(L[12], quad[:, 1, 0, :], L[0], ALU.mult))
            ch(tt(L[13], L[9], L[1], ALU.mult))
            ch.free(tt(L[10], L[10], L[11], ALU.add))
            ch(tt(L[12], L[12], L[13], ALU.subtract))
            ch.free(tt(quad[:, 2, 0, :], L[10], L[7], ALU.mult))
            ch(tt(quad[:, 3, 0, :], L[12], L[7], ALU.mult))
            dve.tensor_copy(quad[:, :, 1, :], quad[:, :, 0, :]).then_inc(s["quad_ready"], 1)
            modf = mod[:].rearrange("p a d -> p (a d)")
            dve.wait_ge(s["adab_loaded"], 16)

            def ada_out(n):
                dve.wait_ge(s["ada_mm"], n + 1)
                tt(modf[:, n * 512:(n + 1) * 512], bank[n % 2][:], modf[:, n * 512:(n + 1) * 512],
                   ALU.add).then_inc(s["ada_ev"], 1)
            ada_out(0)
            dve.wait_ge(s["af_ready"], 1)
            ch.free(dve.memset(PW[:, 0, 0, :], 1.0))
            ch.free(dve.memset(PW[:, 1, 0, :], 0.0))
            ch.free(dve.tensor_copy(PW[:, 0, 1, :], AF[:, 0, :]))
            ch(dve.tensor_copy(PW[:, 1, 1, :], AF[:, 1, :]))

            def cmul(dst, x, y, n):
                X = [PW[:, q, x:x + n, :] for q in range(2)]
                Yb = [bc(PW[:, q, y, :], 1, n, [P, n, DG]) for q in range(2)]
                T = t1[:, 0:n * DG].rearrange("p (n g) -> p n g", g=DG)
                O = [PW[:, q, dst:dst + n, :] for q in range(2)]
                ch.free(tt(O[0], X[0], Yb[0], ALU.mult))
                ch(tt(T, X[1], Yb[1], ALU.mult))
                ch(tt(O[0], O[0], T, ALU.subtract))
                ch.free(tt(O[1], X[0], Yb[1], ALU.mult))
                ch(tt(T, X[1], Yb[0], ALU.mult))
                ch(tt(O[1], O[1], T, ALU.add))
            cmul(2, 1, 1, 1)
            cmul(3, 1, 2, 2)
            cmul(5, 1, 4, 4)
            ch.free(dve.tensor_copy(ab8[:, 0, :], PW[:, 0, 8, :]))
            dve.tensor_scalar(ab8[:, 1, :], PW[:, 1, 8, :], sgn[:, 0:1], None, ALU.mult).then_inc(s["sg_ready"], 1)
            dve.wait_ge(s["bx_ready"], 4)
            dve.wait_ge(s["pe_prep"], 2)
            fr, fi = (bc(AF[:, 2 + q, :], 1, GC, [P, GC, DG]) for q in range(2))
            T1, TB = (x[:].rearrange("p (c g) -> p c g", g=DG) for x in (t1, tB))
            ch.free(tt(T1, Q2[:], fi, ALU.mult))
            ch(tt(TB, P2[:], fi, ALU.mult))
            ch.free(tt(P2[:], P2[:], fr, ALU.mult))
            ch(tt(Q2[:], Q2[:], fr, ALU.mult))
            ch.free(tt(P2[:], P2[:], T1, ALU.add))
            ch(tt(Q2[:], Q2[:], TB, ALU.subtract))
            TG = t1[:].rearrange("p (g c) -> p g c", c=GC)
            TH = tB[:].rearrange("p (g c) -> p g c", c=GC)
            p2g, q2g = (x[:].rearrange("p c g -> p g c") for x in (P2, Q2))
            inv_v = inT[:].rearrange("p g (i c) -> p g i c", c=GC)
            for i in range(STEPS):
                for di, pwr in ((0, 7 - i), (1, i)):
                    g = slice(di * NG, di * NG + NG)
                    pr, pi = (bc(PW[:, q, pwr, g], 2, GC, [P, NG, GC]) for q in range(2))
                    ch.free(tt(inv_v[:, g, i, :], p2g[:, g, :], pr, ALU.mult))
                    ch.free(tt(TG[:, g, :], q2g[:, g, :], pi, ALU.mult))
                ch.sync()
                ch(tt(inv_v[:, :, i, :], inv_v[:, :, i, :], TG, ALU.add))
                if i % 2 == 0:
                    ada_out(1 + i // 2)
            dve.nop().then_inc(s["inraw_ready"], 1)
            dve.wait_ge(s["cq_ready"], 2)
            dve.wait_ge(s["act"], 2)
            for l in range(STEPS + 1):
                for di, pwr in ((0, l), (1, 8 - l)):
                    g = slice(di * NG, di * NG + NG)
                    pr, pi = (bc(PW[:, q, pwr, g], 2, GC, [P, NG, GC]) for q in range(2))
                    ch.free(tt(outM[:, g, l, :], CP[:, g, :], pr, ALU.mult))
                    ch.free(tt((TG, TH)[l % 2][:, g, :], CQ[:, g, :], pi, ALU.mult))
                ch.sync()
                ch(tt(outM[:, :, l, :], outM[:, :, l, :], (TG, TH)[l % 2], ALU.add))
                if l % 2 == 0:
                    ada_out(5 + l // 2)
            dve.nop().then_inc(s["outm_ready"], 1)
            ada_out(10)
            ada_out(11)
            dve.wait_ge(s["ada_ev"], ADA_CHUNKS)
            dve.wait_ge(s["n1w_loaded"], 16)
            ch(dve.scalar_tensor_tensor(mod[:, 1], mod[:, 1], 1.0, n1w[:], ALU.add, ALU.mult))
            for t in range(NT):
                dve.wait_ge(s["sq1"], 2 * t + 1)
                tt(sq_s[:, 2:3], sq_s[:, 0:1], sq_s[:, 1:2], ALU.add).then_inc(s["m_sq"], 1)
                dve.wait_ge(s["sq1"], 2 * t + 2)
                dve.reciprocal(sq_s[:, 4:5], sq_s[:, 3:4]).then_inc(s["rs1"], 1)
                dve.wait_ge(s["rs1"], t + 1)
                ch(dve.scalar_tensor_tensor(xt[:, t % 2], xt[:, t % 2], sq_s[:, 4:5], mod[:, 1], ALU.mult, ALU.mult))
                tt(xt[:, t % 2], xt[:, t % 2], mod[:, 0], ALU.add).then_inc(s["h_ready"], 1)
            dve.wait_ge(s["h_tr"], NT)
            for n in range(8):
                t, w = n % 4, n // 4
                bk = bank[4 + n] if n < 4 else bank[n - 4]
                dve.wait_ge(s["q_sq"], n + 1)
                dve.tensor_reduce(qk_s[:, 0, :], sqb[:, n % 2, :].rearrange("p (g d) -> p g d", d=QK), AX.X,
                                  ALU.add).then_inc(s["q_ss"], 1)
                dve.wait_ge(s["q_rt"], n + 1)
                ch(dve.reciprocal(qk_s[:, 2, :], qk_s[:, 1, :]))
                if n >= 2:
                    dve.wait_ge(s["q_tr"], n - 1)
                X = stg[:, n % 2, :].rearrange("p (g d) -> p g d", d=QK)
                NGP = 2 * HEADS
                ch(tt(X, bk[:].rearrange("p (g d) -> p g d", d=QK), bc(qk_s[:, 2, :], 2, QK, [P, NGP, QK]), ALU.mult))
                ch(tt(X, X, bc(qkw[:, w, :], 1, NGP, [P, NGP, QK]), ALU.mult))
                cb, sb_ = (bc(cs[:, q, t, :], 1, NGP, [P, NGP, ROT_HALF]) for q in range(2))
                a, b_ = X[:, :, 0:ROT_HALF], X[:, :, ROT_HALF:2 * ROT_HALF]
                R = sqb[:, n % 2, 0:256].rearrange("p (q g k) -> p q g k", q=4, k=ROT_HALF)
                if n == 0:
                    dve.wait_ge(s["lam_e"], 3)
                ch.free(tt(R[:, 0], a, cb, ALU.mult))
                ch.free(tt(R[:, 1], b_, sb_, ALU.mult))
                ch.free(tt(R[:, 2], b_, cb, ALU.mult))
                ch(tt(R[:, 3], a, sb_, ALU.mult))
                ch.free(tt(a, R[:, 0], R[:, 1], ALU.subtract))
                ch(tt(b_, R[:, 2], R[:, 3], ALU.add))
                dve.nop().then_inc(s["q_n"], 1)
            def o_norm(t):
                dve.wait_ge(s["pv_mm"], HEADS * (t + 1))
                bk = bank[6]
                if t:
                    dve.wait_ge(s["o_tr"], t)
                dve.tensor_copy(o_n[:, 0, :], bk[:]).then_inc(s["o_copied"], 1)
                dve.wait_ge(s["o_copied"], t + 1)
                ch(tt(o_n[:, 1, :], o_n[:, 0, :], o_n[:, 0, :], ALU.mult))
                dve.tensor_reduce(qk_s[:, 0, 0:8], o_n[:, 1, :].rearrange("p (h d) -> p h d", d=DV), AX.X,
                                  ALU.add).then_inc(s["o_ss"], 1)
                dve.wait_ge(s["o_rt"], t + 1)
                ch(dve.reciprocal(qk_s[:, 2, 0:8], qk_s[:, 1, 0:8]))
                O = o_n[:, 0, :].rearrange("p (h d) -> p h d", d=DV)
                ch(tt(O, O, bc(qk_s[:, 2, 0:8], 2, DV, [P, HEADS, DV]), ALU.mult))
                ch(tt(O, O, bc(subw[:], 1, HEADS, [P, HEADS, DV]), ALU.mult))
                dve.nop().then_inc(s["o_n"], 1)
            ch(dve.tensor_scalar(subw[:], subw[:], 1.0 - LAMBDA_INIT, None, ALU.mult))
            dve.wait_ge(s["q_ev"], 8)
            for n in range(NT * HEADS + 1):
                if n < NT * HEADS:
                    dve.wait_ge(s["sc_mm"], 2 * (n + 1))
                    for c in range(2):
                        ch.free(dve.tensor_reduce(att_s[:, n % 2, c:c + 1], bank[2 * (n % 2) + c][:], AX.X, ALU.max))
                    ch.sync()
                    dve.tensor_scalar(att_s[:, n % 2, 2:4], att_s[:, n % 2, 0:2], -(QK ** -0.5), None,
                                      ALU.mult).then_inc(s["sc_max"], 1)
                if n >= 1:
                    m = n - 1
                    dve.wait_ge(s["sc_exp"], 2 * n)
                    ch(dve.reciprocal(att_s[:, m % 2, 6:8], att_s[:, m % 2, 4:6]))
                    ch.free(dve.tensor_scalar(att_s[:, m % 2, 7:8], att_s[:, m % 2, 7:8], lamv[:, 5:6], None, ALU.mult))
                    ch(dve.tensor_scalar(ee[:, m % 2, 0, :], ee[:, m % 2, 0, :], att_s[:, m % 2, 6:7], None, ALU.mult))
                    dve.scalar_tensor_tensor(ee[:, m % 2, 0, :], ee[:, m % 2, 1, :], att_s[:, m % 2, 7:8],
                                             ee[:, m % 2, 0, :], ALU.mult, ALU.add).then_inc(s["a_ready"], 1)
                if n % HEADS == 3 and n > HEADS:
                    o_norm(n // HEADS - 1)
            o_norm(NT - 1)
            dve.wait_ge(s["scan_done"], 2)
            dve.wait_ge(s["y_ev"], 4)
            ch(tt(U[:], U[:], bc(dcol[:], 2, CHUNKS, [P, NG, CHUNKS]), ALU.mult))
            ch(tt(Y[:], Y[:], U[:], ALU.add))
            T = S2[:, 0:NG, :]
            ch(tt(T, Y[:], Y[:], ALU.mult))
            ch(dve.tensor_scalar(T, T, GELU_B, 1.0, ALU.mult, ALU.add))
            tt(T, T, Y[:], ALU.mult).then_inc(s["y_gp"], 1)
            dve.wait_ge(s["y_sig"], 1)
            tt(Y[:], Y[:], T, ALU.mult).then_inc(s["y_done"], 1)
            for n in range(4):
                dve.wait_ge(s["g_sig"], n + 1)
                tt(sT[:, n, :], sT[:, n, :], yT[:, n, :], ALU.mult).then_inc(s["s_act"], 1)
            dve.wait_ge(s["n_rt"], 1)
            dve.wait_ge(s["s_act"], 4)
            ch(dve.reciprocal(gluw[:, 1, :], gluw[:, 0, :]))
            for n in range(4):
                dve.scalar_tensor_tensor(catT[:, 4 + n, :], sT[:, n, :], outw[:, n:n + 1], gluw[:, 1, :],
                                         ALU.mult, ALU.mult).then_inc(s["s5_done"], 1)
            dve.wait_ge(s["n2w_loaded"], 16)
            ch(dve.scalar_tensor_tensor(mod[:, 4], mod[:, 4], 1.0, n2w[:], ALU.add, ALU.mult))
            dve.wait_ge(s["rw_loaded"], 32)
            dve.wait_ge(s["consts2"], 1)
            for t in range(NT):
                dve.wait_ge(s["mix_mm"], t + 1)
                dve.wait_ge(s[f"xr_loaded{t % 2}"], 32 * (t // 2 + 1))
                if t >= 2:
                    dve.wait_ge(s[f"x1_stored{t % 2}"], 16 * (t // 2))
                for k in range(2):
                    cc_ = slice(512 * k, 512 * k + 512)
                    ch.free(tt(x1[:, t % 2, cc_], bank[2 * (t % 2) + k][:], mod[:, 2, cc_], ALU.mult))
                ch.sync()
                tt(x1[:, t % 2], x1[:, t % 2], xr[:, t % 2], ALU.add).then_inc(s["x1_ready"], 1)
                dve.wait_ge(s["o_sq"], 2 * t + 1)
                tt(sq_s[:, 10:11], sq_s[:, 8:9], sq_s[:, 9:10], ALU.add).then_inc(s["m_rt"], 1)
                dve.wait_ge(s["o_sq"], 2 * t + 2)
                ch(dve.reciprocal(sq_s[:, 12:13], sq_s[:, 11:12]))
                ch(dve.scalar_tensor_tensor(h2[:, t % 2], x1[:, t % 2], sq_s[:, 12:13], mod[:, 4], ALU.mult, ALU.mult))
                tt(h2[:, t % 2], h2[:, t % 2], mod[:, 3], ALU.add).then_inc(s["h2_ready"], 1)
                dve.wait_ge(s["r_mm"], t + 1)
                ch(tt(lg[:], bank[6][:, 0:E], rb[:], ALU.add))
                ch(dve.max(mx8[:], lg[:]))
                ch.free(dve.max_index(ix8[:], mx8[:], lg[:]))
                dve.tensor_scalar(gs[:, 2:3], mx8[:, 0:1], -1.0, None, ALU.mult).then_inc(s["lg_ready"], 1)
                ch.sync()
                ch(dve.tensor_copy(ixf[:], ix8[:]))
                ch(tt(oh4[:, t], bc(iotaE[:, 0:E], 1, TOPK, [P, TOPK, E]), bc(ixf[:, 0:TOPK], 2, E, [P, TOPK, E]), ALU.is_equal))
                dve.tensor_reduce(mask[:, t], oh4[:, t].rearrange("p k e -> p e k"), AX.X, ALU.add).then_inc(s["mask_ready"], 1)
                dve.wait_ge(s["g_exp"], t + 1)
                ch(dve.reciprocal(gs[:, 1:2], gs[:, 0:1]))
                ch(dve.tensor_scalar(gat[:, t, :], gat[:, t, :], gs[:, 1:2], None, ALU.mult))
            dve.wait_ge(s["mix_mm"], NT)
            dve.wait_ge(s["pos_mm"], 1)
            R = [rt[:, k, :] for k in range(8)]
            cnt = bank[7][:, NT * E:NT * E + E]
            ch.free(dve.tensor_scalar(R[0], cnt, 0.5, None, ALU.is_gt))
            for k in range(1, NT):
                ch.free(dve.tensor_scalar(R[k], cnt, k * P + 0.5, None, ALU.is_gt))
            ch.sync()
            ch(tt(R[0], R[0], R[1], ALU.add))
            ch(tt(R[0], R[0], R[2], ALU.add))
            ch(tt(R[0], R[0], R[3], ALU.add))
            ch.free(dve.tensor_scalar(ec[:, 0, 1], R[0], 0.5, None, ALU.is_gt))
            ch(dve.tensor_copy(ec[:, 0, 0], R[0]))
            a, b_ = ec[:, 1], ec[:, 2]
            ch(dve.tensor_copy(a, ec[:, 0]))
            dist = 1
            while dist < E:
                ch.free(dve.tensor_copy(b_[:, :, 0:dist], a[:, :, 0:dist]))
                ch(tt(b_[:, :, dist:E], a[:, :, dist:E], a[:, :, 0:E - dist], ALU.add))
                a, b_ = b_, a
                dist *= 2
            end, loads = a[:, 0], a[:, 1]
            ch.free(dve.tensor_copy(nbi[:], a[:, :, E - 1]))
            nl = E + 2
            ch(tt(cmpl[:], bc(iotaE[:, 0:nl], 2, E, [P, nl, E]), bc(loads, 1, nl, [P, nl, E]), ALU.is_ge))
            ch(dve.tensor_reduce(tabf[:, 0, 0:nl], cmpl[:], AX.X, ALU.add))
            ch(tt(cmpl[:], cmpl[:], bc(ec[:, 0, 0], 1, nl, [P, nl, E]), ALU.mult))
            ch.free(dve.tensor_scalar(load_expert[:], tabf[:, 0, 0:nl], float(E - 1), None, ALU.min))
            ch(dve.tensor_reduce(tabf[:, 1, 0:nl], cmpl[:], AX.X, ALU.add))
            dve.tensor_scalar(load_after[:], tabf[:, 1, 0:nl], -1.0, 0.0, ALU.add, ALU.max).then_inc(s["blocks_ready"], 1)
            ch(tt(cmpb[:], bc(iotaE[:], 2, E, [P, MAXB, E]), bc(end, 1, MAXB, [P, MAXB, E]), ALU.is_ge))
            ch(dve.tensor_reduce(ebf[:, 0:MAXB], cmpb[:], AX.X, ALU.add))
            ch(tt(cmpb[:], cmpb[:], bc(ec[:, 0, 1], 1, MAXB, [P, MAXB, E]), ALU.mult))
            ch.free(dve.memset(tabf[:, 2, MAXB:MAXB + 2], 0.0))
            ch(dve.tensor_reduce(tabf[:, 2, 0:MAXB], cmpb[:], AX.X, ALU.add))
            ch.free(dve.tensor_scalar(block_load[:], tabf[:, 2], 1.0, 32.0, ALU.add, ALU.mult))
            ch(tt(R[3], end, R[0], ALU.subtract))
            ch(dve.tensor_scalar(R[4], R[3], float(P), None, ALU.mult))
            ch.free(dve.memset(ebf[:, MAXB:MAXB + 2], 0.0))
            ch.free(tt(slotE[:], bank[7][:, 0:NT * E].rearrange("p (t e) -> p t e", e=E), bc(R[4], 1, NT, [P, NT, E]), ALU.add))
            ch(dve.tensor_scalar(ebf[:, 0:MAXB], ebf[:, 0:MAXB], float(E - 1), None, ALU.min))
            ch.free(dve.tensor_scalar(eye96[:], ebf[0:96, :], pm[0:96, 0:1], None, ALU.is_equal))
            for t in range(NT):
                ch.free(tt(prod[:, TOPK * t:TOPK * t + TOPK], oh4[:, t], bc(slotE[:, t], 1, TOPK, [P, TOPK, E]), ALU.mult))
            ch.sync()
            ch(dve.tensor_reduce(dslot[:], prod[:], AX.X, ALU.add))
            dve.nop().then_inc(s["blocks_ready"], 1)
            n_blocks = dve.value_load(nbi[0:1, 0:1], min_val=1, max_val=MAXB)
            dve.wait_ge(s["bias_ready"], 2)

            def slots(v):
                tt(ohs[:], bc(iotab[:], 1, NT * TOPK, [P, NT * TOPK, P]), bc(dslot[:], 2, P, [P, NT * TOPK, P]),
                   ALU.is_equal).then_inc(s["oh_ready"], 1)
                dve.wait_ge(s["oh_ready"], v)
                dve.tensor_scalar(iotab[:], iotab[:], float(P), None, ALU.add).then_inc(s["d_ready"], 1)

            def rows(v):
                dve.wait_ge(s["idx_mm"], v)
                dve.tensor_reduce(idf[:, 0:1], bank[6][:, 0:2], AX.X, ALU.add).then_inc(s["idx_sum"], 1)
                dve.tensor_reduce(idf[:, 1:2], bank[6][:, 0:4], AX.X, ALU.add).then_inc(s["idx_sum"], 1)
                dve.wait_ge(s["idx_sum"], v * 2)
                dve.tensor_scalar(idx[:, 0:1], idf[:, 0:1], 1 / TOPK, None, ALU.mult).then_inc(s["idx_ready"], 1)

            def rows_out():
                dve.tensor_scalar(idx[:, 1:2], idf[:, 1:2], UNUSED, None, ALU.add).then_inc(s["idx_ready"], 1)

            def select(b):
                dve.tensor_copy(selb[:], eye96[:, bass.ds(b, 1)].to_broadcast([96, P])).then_inc(s["sel_ready"], 1)

            def low(chunks, b, first=False):
                for c in chunks:
                    if c in POOL_LOW:
                        continue
                    dve.wait_ge(s["hi_done"], c + 1 if first else b * WCH + (c + 1))
                    hi, lo = w_split[c % SPLIT]
                    tt(lo[:], raw(c), hi[:].bitcast(F32), ALU.subtract).then_inc(s["lo_dve"], 1)

            def x_low(k, b2):
                dve.wait_ge(s["xs_ev"], b2 + (k + 1))
                part = [x[:, 4 * k:4 * k + 4, :].rearrange("p k n -> p (k n)") for x in xT]
                tt(part[1], bank[7 - k][:], part[0].bitcast(F32), ALU.subtract).then_inc(s["x_lo"], 1)

            def act_low(k, b2):
                dve.wait_ge(s["act_ev"], b2 + (k + 1))
                part = [x[:, 4 * k:4 * k + 4, :].rearrange("p k n -> p (k n)") for x in actT]
                tt(part[1], bank[6 + k][:], part[0].bitcast(F32), ALU.subtract).then_inc(s["act_lo"], 1)

            def gate_parts(k):
                z = [bank[2 * k][:].rearrange("p (f two) -> p two f", two=2),
                     bank[2 * k + 1][:].rearrange("p (f two) -> p two f", two=2)]
                return z, glu[:, 0, :] if k == 0 else glu[:, 2, :], lin[:, k, :], glu[:, 1, :] if k == 0 else lin[:, 2, :]

            def gate_min(k, b):
                z, g, l, sg = gate_parts(k)
                dve.wait_ge(w_used, b * WCH + KT * (k + 1))
                for q in range(2):
                    dve.tensor_scalar(g[:, 256 * q:256 * q + 256], z[q][:, 0, :], 7.0, None, ALU.min).then_inc(s["l_a"], 1)
                dve.wait_ge(s["l_a"], b * 8 + (4 * k + 2))
                dve.nop().then_inc(s["g_min"], 1)

            def gated(k, b):
                z, g, l, sg = gate_parts(k)
                for q in range(2):
                    dve.tensor_scalar(l[:, 256 * q:256 * q + 256], z[q][:, 1, :], 7.0, -7.0, ALU.min,
                                      ALU.max).then_inc(s["l_a"], 1)
                dve.wait_ge(s["l_a"], b * 8 + (4 * k + 4))
                dve.scalar_tensor_tensor(l, l, 1.0, g, ALU.add, ALU.mult).then_inc(s["l_b"], 1)
                dve.wait_ge(s["l_b"], b * 2 + (k + 1))
                dve.wait_ge(s["g_sg"], b * 2 + (k + 1))
                tt(l, l, sg, ALU.mult).then_inc(s["act_ready"], 1)

            slots(1)
            select(0)
            rows(1)
            rows_out()
            low(range(SPLIT), 0, first=True)
            x_low(0, 0)
            x_low(1, 0)
            with dve.Fori(0, n_blocks) as b:
                b2 = b * 2
                dve.wait_ge(s["d_ready"], b + 1)
                slots(b + 2)
                low(range(SPLIT, 10), b)
                rows(b + 2)
                low(range(10, 14), b)
                gate_min(0, b)
                gated(0, b)
                dve.wait_ge(s["scat_ready"], b + 1)
                rows_out()
                low(range(14, 20), b)
                gate_min(1, b)
                act_low(0, b2)
                gated(1, b)
                low(range(20, 22), b)
                x_low(0, b2 + 2)
                low(range(22, 23), b)
                dve.wait_ge(w_used, b * WCH + W1C + 1)
                select(b + 1)
                low(range(23, WCH), b)
                low(range(0, 1), b + 1)
                act_low(1, b2)
                x_low(1, b2 + 2)
                low(range(1, SPLIT), b + 1)
            dve.wait_ge(s["lo_pool"], n_blocks * len(POOL_LOW))
            dve.wait_ge(*low_ready(SPLIT - 1, n_blocks))
            dve.sem_inc(s["fin_done"], 1)
            dve.wait_ge(s["fin_x1"], 16)
            for t in range(NT):
                dve.wait_ge(s[f"fin_g{t}"], 16)
                o = facc[:, t]
                ch(dve.tensor_scalar(o, fing[:, TOPK * t], gat[:, t, 0:1], None, ALU.mult))
                for k in range(1, TOPK):
                    ch(dve.scalar_tensor_tensor(o, fing[:, TOPK * t + k], gat[:, t, k:k + 1], o, ALU.mult, ALU.add))
                ch(tt(o, o, mod[:, 5], ALU.mult))
                tt(o, o, fx1[:, t], ALU.add).then_inc(s["fin_done"], 1)

        @block.tensor
        def _(pe):
            mm, tr = pe.matmul, pe.transpose
            pe.wait_ge(s["ident_ready"], 1)
            pe.wait_ge(s["s5_nat"], 96)
            for q in range(2):
                for n in range(8):
                    last = tr(bank[2 * q + n // 4][:, (n % 4) * P:(n % 4) * P + P],
                              CC[:, n, q:q + 2, :].rearrange("p a b -> p (a b)"), ident[:])
            last.then_inc(s["pe_prep"], 1)
            bbf = BB[:].rearrange("p a b -> p (a b)")
            for q in range(2):
                for c in range(GC):
                    o = q * NP * GC + c
                    last = tr(bank[4 + 2 * q + c // 8][:, (c % 8) * DG:(c % 8) * DG + DG],
                              bbf[:, o:o + GC * (P - 1) + 1:GC], ident[0:DG, 0:DG])
            last.then_inc(s["pe_prep"], 1)

            def ada(n):
                pe.wait_ge(ring_sem[n % RING], 16 * (n // RING + 1))
                if n >= 2:
                    pe.wait_ge(s["ada_ev"], n - 1)
                for k in range(KT):
                    last = mm(bank[n % 2][:], cbc[:, k, :], ring[:, n % RING, k, :], start=(k == 0), stop=(k == KT - 1))
                last.then_inc(s["ada_mm"], 1)

            pe.wait_ge(s["cbc_ready"], 1)
            pe.wait_ge(s["cq_ready"], 2)
            pe.wait_ge(s["act"], 2)
            ada(0)
            ada(1)
            pe.wait_ge(s["quad_ready"], 1)
            for q in range(4):
                last = tr(bank[2][:, q * DG:(q + 1) * DG], quad[:, q].rearrange("p a b -> p (a b)"), ident[0:DG, 0:DG])
            last.then_inc(s["af_psum"], 1)
            pe.wait_ge(s["af_ready"], 1)
            pe.wait_ge(s["bx_ready"], 4)
            for n in range(2, ADA_CHUNKS):
                ada(n)
            pe.wait_ge(s["inraw_ready"], 1)
            for n in range(DG // 4):
                if n >= 4:
                    pe.wait_ge(s["in_done"], n - 3)
                for g in range(4):
                    last = tr(bank[2 + n % 4][:, g * P:(g + 1) * P], inT[:, 4 * n + g, :], ident[:])
                last.then_inc(s["in_tr"], 1)
            pe.wait_ge(s["outm_ready"], 1)
            for n in range(NG // 2):
                if n >= 2:
                    pe.wait_ge(s["k_ev"], n - 1)
                for q in range(2):
                    g = 2 * n + q
                    o = q * 240
                    mm(bank[6 + n % 2][0:GC, o + 112:o + 240], P2[:, :, g],
                       outM[:, g, 0:STEPS, :].rearrange("p l c -> p (l c)"), start=(q == 0), stop=False, skip_group_check=True)
                    last = mm(bank[6 + n % 2][0:GC, o:o + P], P2[:, :, NG + g],
                              outM[:, NG + g, 1:STEPS + 1, :].rearrange("p l c -> p (l c)"), start=False, stop=(q == 1),
                              skip_group_check=True)
                last.then_inc(s["k_mm"], 1)
            pe.wait_ge(s["ada_ev"], ADA_CHUNKS)
            pe.wait_ge(s["in_done"], DG // 4)
            for t in range(NT):
                pe.wait_ge(s["h_ready"], t + 1)
                if t >= 2:
                    pe.wait_ge(s["h_ev"], 2 * (t - 1))
                for k in range(KT):
                    last = tr(bank[2 * (t % 2) + k // 4][:, (k % 4) * P:(k % 4) * P + P], xt[:, t % 2, k * P:(k + 1) * P], ident[:])
                last.then_inc(s["h_tr"], 1)
            pe.wait_ge(s["h_ev"], 2 * NT)
            pe.wait_ge(ring_sem[U_CHUNK % RING], 16 * (U_CHUNK // RING + 1))
            for n in range(4):
                for k in range(KT):
                    last = mm(bank[n][:], ring[:, U_CHUNK % RING, k, n * P:(n + 1) * P], hT[:, k, :],
                              start=(k == 0), stop=(k == KT - 1))
                last.then_inc(s["u_mm"], 1)
            def proj(c, t, bk):
                if t == 0:
                    pe.wait_ge(ring_sem[c % RING], 16 * (c // RING + 1))
                for k in range(KT):
                    last = mm(bk[:], hT[:, k, t * P:(t + 1) * P], ring[:, c % RING, k, :], start=(k == 0), stop=(k == KT - 1))
                last.then_inc(s["q_mm"], 1)

            def qk_tr(n):
                bk = bank[4 + n] if n < 4 else bank[n - 4]
                pe.wait_ge(s["q_n"], n + 1)
                for b in range(4):
                    last = tr(bk[:, b * P:(b + 1) * P], stg[:, n % 2, b * P:(b + 1) * P], ident[:])
                last.then_inc(s["q_tr"], 1)
            pe.wait_ge(s["k_ev"], NG // 2)
            pe.wait_ge(s["sq1"], 2 * NT)
            def chunk_inputs(n):
                for k in range(2):
                    if n >= 2:
                        pe.wait_ge(s["s_ev"], 2 * (n - 2) + k + 1)
                    bk = bank[4 + 2 * (n % 2) + k]
                    for g in range(8):
                        d = 8 * n + g
                        if k == 0:
                            last = mm(bk[:, g * 64:g * 64 + 64], inT[:, d, :], U[:, d % NG, :], start=True, stop=True)
                        else:
                            mm(bk[0:64, g * 64:g * 64 + 64], inT[:, d, 64:128], U[:, d % NG, :], start=True, stop=True)
                            last = mm(bk[64:128, g * 64:g * 64 + 64], inT[:, d, 0:64], U[:, d % NG, :], start=True, stop=True)
                    last.then_inc(s["s_mm"], 1)
            for t in range(NT):
                proj(Q_CHUNK, t, bank[4 + t])
            pe.wait_ge(s["u_ev"], 4)
            for t in range(NT):
                proj(K_CHUNK, t, bank[t])
                qk_tr(t)
            pe.wait_ge(s["q_ev"], 4)
            pe.wait_ge(s["u_loaded"], 16 * STEPS)
            for n in range(DG // 8):
                chunk_inputs(n)
                if n % 2:
                    qk_tr(4 + n // 2)
            pe.wait_ge(s["s_ev"], 2 * DG // 8)
            for t in range(NT):
                proj(V_CHUNK, t, bank[4 + t])
            pe.wait_ge(s["q_ev"], 8)
            pe.wait_ge(s["v_ev"], 4)

            def scores(n):
                t, h = n // HEADS, n % HEADS
                if n >= 2:
                    pe.wait_ge(s["sc_exp"], 2 * (n - 1))
                if h == 0:
                    pe.wait_ge(s["qm_ready"], 4 * (t + 1))
                for c in range(2):
                    g = 2 * h + c
                    mm(bank[2 * (n % 2) + c][:], qm[:, t % 2, g % 4, g // 4, :], qkT[:, 1, g // 4, :],
                       start=True, stop=True).then_inc(s["sc_mm"], 1)

            def values(n):
                t, h = n // HEADS, n % HEADS
                pe.wait_ge(s["a_ev"], n + 1)
                if h == 0 and t:
                    pe.wait_ge(s["o_copied"], t)
                for k in range(NT):
                    last = mm(bank[6][:, h * DV:(h + 1) * DV], aT[:, n % 2, k, :], vv[:, k, h * DV:(h + 1) * DV],
                              start=(k == 0), stop=(k == NT - 1))
                last.then_inc(s["pv_mm"], 1)

            def o_tr(t):
                pe.wait_ge(s["o_n"], t + 1)
                if t:
                    pe.wait_ge(s["o_ev"], t)
                for k in range(4):
                    last = tr(bank[7][:, k * P:(k + 1) * P], o_n[:, 0, k * P:(k + 1) * P], ident[:])
                last.then_inc(s["o_tr"], 1)
            for n in range(NT * HEADS + 3):
                if n < NT * HEADS:
                    scores(n)
                if 2 <= n <= NT * HEADS + 1:
                    m = n - 2
                    pe.wait_ge(s["a_ready"], m + 1)
                    if m >= 2:
                        pe.wait_ge(s["a_ev"], m - 1)
                    for k in range(NT):
                        last = tr(bank[4 + m % 2][:, k * P:(k + 1) * P], ee[:, m % 2, 0, k * P:(k + 1) * P], ident[:])
                    last.then_inc(s["a_tr"], 1)
                if n >= 3:
                    values(n - 3)
                if n % HEADS == 4 and n > HEADS:
                    o_tr(n // HEADS - 1)
            o_tr(NT - 1)
            pe.wait_ge(s["scan_done"], 2)
            pe.wait_ge(s["kp_half"], 32 * STEPS)
            pe.wait_ge(s["sc_exp"], 2 * NT * HEADS)
            for n in range(4):
                for q in range(8):
                    g = 8 * n + q
                    o = 64 * q
                    mm(bank[n][:, o:o + 64], toep[:, g, :], U[:, g, :], start=True, stop=False, skip_group_check=True)
                    mm(bank[n][:, o + 1:o + 64], outM[:, g, 1:STEPS + 1, :].rearrange("p l c -> p (l c)"),
                       S1[:, g, 0:63], start=False, stop=False, skip_group_check=True)
                    last = mm(bank[n][:, o:o + 63], outM[:, NG + g, 0:STEPS, :].rearrange("p l c -> p (l c)"),
                              S1[:, NG + g, 1:64], start=False, stop=True, skip_group_check=True)
                last.then_inc(s["y_mm"], 1)
            pe.wait_ge(s["y_loaded"], 16)
            pe.wait_ge(s["gluw_loaded"], 16)
            pe.wait_ge(s["o_ev"], NT)
            for n in range(4):
                for k in range(4):
                    last = mm(bank[4 + n][:], gluw[:, k, n * P:(n + 1) * P], yT[:, k, :], start=(k == 0), stop=(k == 3))
                last.then_inc(s["g_mm"], 1)
            pe.wait_ge(s["s_sq"], 4)
            pe.wait_ge(s["y_ev"], 4)
            pe.wait_ge(s["consts2"], 1)
            for k in range(4):
                last = mm(bank[0][:], ones[:], sqT[:, k, :], start=(k == 0), stop=(k == 3))
            last.then_inc(s["n_mm"], 1)
            pe.wait_ge(s["s5_done"], 4)
            pe.wait_ge(s["wout_loaded"], 16)

            def mix(t):
                if t >= 2:
                    pe.wait_ge(s["x1_ready"], t - 1)
                for k in range(2):
                    for c in range(KT):
                        last = mm(bank[2 * (t % 2) + k][:], catT[:, c, t * P:(t + 1) * P],
                                  wout[:, c, 512 * k:512 * k + 512], start=(c == 0), stop=(c == KT - 1))
                last.then_inc(s["mix_mm"], 1)

            def route(t):
                pe.wait_ge(s["h2_ready"], t + 1)
                if t == 0:
                    pe.wait_ge(s["g_sig"], 4)
                else:
                    pe.wait_ge(s["h2_ev"], 2 * t)
                for k in range(KT):
                    last = tr(bank[4 + k // 4][:, (k % 4) * P:(k % 4) * P + P], h2[:, t % 2, k * P:(k + 1) * P], ident[:])
                last.then_inc(s["h2_tr"], 1)
                pe.wait_ge(s["h2_ev"], 2 * (t + 1))
                if t == 0:
                    pe.wait_ge(s["rw_loaded"], 32)
                else:
                    pe.wait_ge(s["lg_ready"], t)
                for k in range(KT):
                    last = mm(bank[6][:, 0:E], h2T[:, k, :], rw[:, k, :], start=(k == 0), stop=(k == KT - 1))
                last.then_inc(s["r_mm"], 1)

            mix(0)
            mix(1)
            for t in range(NT):
                route(t)
                if t + 2 < NT:
                    mix(t + 2)
            pe.wait_ge(s["mask_ready"], NT)
            for t in range(NT):
                for q in range(t + 1):
                    mm(bank[7][:, t * E:(t + 1) * E], tri[:] if q == t else onb[:], mask[:, q, :], start=(q == 0), stop=(q == t))
            for q in range(NT):
                last = mm(bank[7][:, NT * E:(NT + 1) * E], onb[:], mask[:, q, :], start=(q == 0), stop=(q == NT - 1))
            last.then_inc(s["pos_mm"], 1)
            pe.wait_ge(s["blocks_ready"], 2)
            n_blocks = pe.value_load(nbi[0:1, 0:1], min_val=1, max_val=MAXB)

            def rows(v):
                pe.wait_ge(s["oh_ready"], v)
                for q in range(NT * TOPK):
                    last = mm(bank[6][:, 0:4], ohs[:, q, :], tokid[:, q, :], start=(q == 0), stop=(q == NT * TOPK - 1))
                last.then_inc(s["idx_mm"], 1)

            def split_mm(banks, x, c, w, stop, x_low_ready=None):
                for i, j in ((0, 0), (0, 1), (1, 0)):
                    if i == 1 and x_low_ready is not None:
                        pe.wait_ge(*x_low_ready)
                    for q in range(2):
                        last = mm(banks[q][:], x[i][:, c, :], w[j][:, 512 * q:512 * q + 512], start=False, stop=(stop and i == 1))
                last.then_inc(w_used, 1)

            def x_turn(k, v):
                pe.wait_ge(s["xs_loaded"], v * 16)
                for c in range(4):
                    last = tr(bank[7 - k][:, c * P:(c + 1) * P], xs[:, (4 * k + c) * P:(4 * k + c + 1) * P], ident[:])
                last.then_inc(s["xs_tr"], 1)

            def up(k, b):
                if k == 0:
                    pe.wait_ge(s["sel_ready"], b + 1)
                for q in range(2):
                    mm(bank[2 * k + q][:], selb[:], bcat[:, (2 * k + q) * 512:(2 * k + q + 1) * 512], start=True, stop=False)
                for c in range(KT * k, KT * k + KT):
                    if c == 4:
                        rows(b + 2)
                    pe.wait_ge(*low_ready(c, b))
                    split_mm(bank[2 * k:2 * k + 2], xT, c % KT, w_split[c % SPLIT], c % KT == KT - 1)

            def act_turn(k, b):
                pe.wait_ge(s["act_ready"], b * 2 + (k + 1))
                if k == 0:
                    pe.wait_ge(s["idx_ready"], b * 2 + 4)
                else:
                    pe.wait_ge(s["x_lo"], b * 2 + 3)
                for c in range(4):
                    last = tr(bank[6 + k][:, c * P:(c + 1) * P], lin[:, k, c * P:(c + 1) * P], ident[:])
                last.then_inc(s["act_tr"], 1)

            def down(k, b):
                if k == 0:
                    pe.wait_ge(s["y2_ev"], b * 2 + 2)
                    for q in range(2):
                        mm(bank[4 + q][:], selb[:], bcat[:, 2048 + 512 * q:2560 + 512 * q], start=True, stop=False)
                pe.wait_ge(s["act_ev"], b * 2 + (k + 1))
                for c in range(W1C + 4 * k, W1C + 4 * k + 4):
                    pe.wait_ge(*low_ready(c, b))
                    split_mm(bank[4:6], actT, c - W1C, w_split[c % SPLIT], c == WCH - 1,
                             (s["act_lo"], b * 2 + (k + 1)) if c % 4 == 0 else None)

            pe.wait_ge(s["bias_ready"], 1)
            rows(1)
            x_turn(0, 1)
            x_turn(1, 1)
            with pe.Fori(0, n_blocks) as b:
                pe.wait_ge(s["x_lo"], b * 2 + 2)
                up(0, b)
                up(1, b)
                act_turn(0, b)
                x_turn(0, b + 2)
                down(0, b)
                act_turn(1, b)
                x_turn(1, b + 2)
                down(1, b)


def o_norm_act(act, ch, s, bank, o_n, att_s, qk_s, sgn, catT, t):
    act.wait_ge(s["o_ss"], t + 1)
    act.activation(qk_s[:, 1, 0:8], qk_s[:, 0, 0:8], ACT.Sqrt, scale=1.0 / DV, bias=sgn[:, 2:3]).then_inc(s["o_rt"], 1)
    act.wait_ge(s["o_tr"], t + 1)
    act.activation(catT[:, 0:4, t * P:(t + 1) * P], bank[7][:].rearrange("p (k n) -> p k n", n=P),
                   ACT.Identity).then_inc(s["o_ev"], 1)


NAMES = ["x", "c", "positions", "ada_w", "ada_b", "norm1_w", "w_in", "q_norm_w", "k_norm_w", "lambda_q1", "lambda_k1",
         "lambda_q2", "lambda_k2", "subln_w", "s5_lambda_re", "s5_lambda_im", "s5_log_step", "s5_b_re", "s5_b_im",
         "s5_cmat_re", "s5_cmat_im", "s5_d", "s5_glu_w", "s5_glu_b", "s5_out_norm_w", "w_out", "norm2_w", "router_w",
         "router_b", "mlp1_w", "mlp1_b", "mlp2_w", "mlp2_b"]


def kernel(**inputs):
    from concourse import bacc
    from concourse.bass_utils import run_bass_kernel_spmd

    nc = bacc.Bacc("TRN2", target_bir_lowering=False, num_devices=1)
    arrays = {n: np.ascontiguousarray(inputs[n]) for n in NAMES}
    params = {n: nc.dram_tensor(n, a.shape, mybir.dt.from_np(a.dtype), kind="ExternalInput").ap()
              for n, a in arrays.items()}
    out = nc.dram_tensor("out", (1, S, D), F32, kind="ExternalOutput").ap()
    program(nc, params, out)
    r = run_bass_kernel_spmd(nc, [arrays], core_ids=[0])
    return r.results[0]["out"]
```

```python
import math
from contextlib import ExitStack

import numpy as np

import concourse.bass as bass
from concourse import mybir

F32 = mybir.dt.float32
F32R = mybir.dt.float32r
BF16 = mybir.dt.bfloat16
I32 = mybir.dt.int32
U32 = mybir.dt.uint32
ALU = mybir.AluOpType
ACT = mybir.ActivationFunctionType
AX = mybir.AxisListType

P = 128
KIB = 1024
S, D = 512, 1024
KT = D // P
NT = S // P
HEADS, QK, DV = 8, 32, 64
ROT_HALF = 4
ROPE_THETA = 500000.0
STEPS = 8
POOL_LAGS = (4, 5, 6, 7, 8)
CHUNKS = S // STEPS
GC, NG, NP = 16, 32, 64
DG = 2 * NG
E, TOPK, FF = 32, 4, 1024
MAXB = S * TOPK // P + E
EPS = 1e-6
LAMBDA_INIT = 0.8 - 0.6 * math.exp(0.0)
C1, C2 = 6.28125, 0.0019350051879882812
C3 = 2 * math.pi - C1 - C2
GELU_A, GELU_B = 2 * math.sqrt(2 / math.pi), 0.044715
ADA_CHUNKS = 6 * D // 512
U_CHUNK, Q_CHUNK, K_CHUNK, V_CHUNK = range(ADA_CHUNKS, ADA_CHUNKS + 4)
RING = 3
W1C, W2C = 16, 8
WCH = W1C + W2C
SPLIT = 6
POOL_LOW = (8, 13, 18, 23)
DVE_LOW = tuple(c for c in range(WCH) if c not in POOL_LOW)
UNUSED = 4096.0
SBUF0 = 16512


def bc(ap, axis, n, shape):
    return ap.unsqueeze(axis).to_broadcast(shape)


class Chain:

    def __init__(self, eng, sem):
        self.eng, self.sem, self.n = eng, sem, 0

    def __call__(self, ins):
        self.n += 1
        ins.then_inc(self.sem, 1)
        self.eng.wait_ge(self.sem, self.n)

    def free(self, ins):
        self.n += 1
        ins.then_inc(self.sem, 1)

    def sync(self):
        self.eng.wait_ge(self.sem, self.n)


def program(nc, I, out):
    ctx = ExitStack()

    def at(name, kib, shape, dt=F32):
        return nc.alloc_sbuf_tensor_at(name, shape, dt, offset=SBUF0 + int(kib * KIB))

    def sem(name):
        return ctx.enter_context(nc.semaphore(name))

    with ctx:
        A, B, C, DD, EE, FV = 0, 64, 96, 132, 156, 172
        G = 196
        K0 = 204.5
        ident = at("ident", K0, [P, P])
        sgn = at("sgn", K0 + 0.5, [P, 4])
        ab8 = at("ab8", K0 + 0.5 + 0.0625, [P, 2, DG])
        cs = at("rope", K0 + 1.0625 + 0.0625, [P, 2, NT, ROT_HALF])
        qkw = at("qkw", K0 + 1.25, [P, 2, QK])
        subw = at("subw", K0 + 1.5, [P, DV])
        lamv = at("lamv", K0 + 1.75, [P, 8])
        strip = at("strip_mask", K0 + 1.78125, [P, 4])
        dcol = at("dcol", K0 + 1.8125, [P, NG])
        glub = at("glub", K0 + 1.9375, [P, 4])
        outw = at("outw", K0 + 1.9375 + 0.03125, [P, 4])
        att_s = at("att_small", K0 + 2.0, [P, 2, 8])
        qk_s = at("qk_small", K0 + 2.0625, [P, 3, 2 * HEADS])
        sq_s = at("sq_small", K0 + 2.25, [P, 32])
        ring = at("dense_ring", A, [P, RING, KT, 512])
        toep = at("toeplitz", A + 48, [P, NG, P])
        cbc = at("c_bcast", A + 48, [P, KT, P])
        S1 = at("state_ri", A + 32, [P, DG, CHUNKS])
        S2 = at("state_ir", A + 16, [P, DG, CHUNKS])
        scan_t = at("scan_tmp", B + 22, [P, 4, 256])
        Y = at("s5_y", A, [P, NG, CHUNKS])
        aT = at("probs_T", A + 8, [P, 2, NT, P])
        o_n = at("o_norm", A + 12, [P, 2, 512])
        yT = at("y_T", A + 16, [P, 4, S])
        gluw = at("glu_w", A + 24, [P, 4, 512])
        sT = at("s_T", A + 32, [P, 4, S])
        sqT = at("sq_T", A + 40, [P, 4, S])
        w1 = at("w1_ring", A, [P, W1C, 1024])
        inT = at("in_ops", B, [P, DG, P])
        wout = at("w_out", B, [P, KT, D])
        w2 = at("w2_ring", B, [P, W2C, 1024])
        outM = at("out_ops", C, [P, DG, STEPS + 1, GC])
        mod = at("modulation", DD, [P, 6, D])
        uT = at("u_T", DD, [P, 4, S])
        U = at("u_chunks", DD, [P, NG, CHUNKS])
        P2 = at("p2", EE, [P, GC, DG])
        Q2 = at("q2", EE + 4, [P, GC, DG])
        CP = at("cp", EE + 8, [P, DG, GC])
        CQ = at("cq", EE + 12, [P, DG, GC])
        BB = at("b_nat", FV, [DG, 3, NP * GC])
        tB = at("tmp_b", FV, [P, 1024])
        CC = at("c_nat", FV + 12, [P, 8, 3, NP])
        PW = at("powers", FV + 18, [P, 2, STEPS + 1, DG])
        t1 = at("tmp_1", FV + 22.5, [P, 1024])
        quad = at("quad", FV + 26.5, [DG, 4, 2, NP])
        AF = at("a_f", FV + 28.5, [P, 4, DG])
        lam_t = at("lam_tiles", FV + 22.5, [DG, 16, NP])
        kpad = at("kpad", FV, [GC, NG // 2, 15, GC])
        ccol = at("c_col", FV + 29.5, [P, 4, KT])
        lam_in = at("lam_in", FV + 29.625, [P, 4, QK])
        lam_w = at("lam_w", FV + 30.125, [P, 2, QK])
        posi = at("pos_i", FV + 30.5, [P, NT], I32)
        rope_t = at("rope_tmp", FV + 30.5625, [P, 8, NT, ROT_HALF])
        rope_i = at("rope_int", FV + 31.0625, [P, 64], I32)
        lstep = at("log_step", FV + 31.3125, [DG, 2])
        n1w = at("norm1_w", FV + 15, [P, D])
        BS = at("b_scaled", FV + 19, [P, GC, DG])
        pool_tmp = at("tmp_pool", FV + 4, [P, DG, GC])
        hT = at("h_T", EE, [P, KT, S])
        catT = at("cat_T", EE, [P, 8, S])
        qkT = at("qk_T", FV, [P, 2, 4, S])
        vv = at("v", FV + 16, [P, NT, 512])
        xt = at("x_tile", G, [P, 2, D])
        stg = at("qk_stage", G, [P, 2, 512])
        sqb = at("qk_square", G + 4, [P, 2, 512])
        ee = at("probs", G, [P, 2, 2, 512])
        psq = at("chunk_powers", B + 16, [P, 2, 9, DG])
        scan_w = at("power_tmp", B + 20.75, [P, 4 * DG])
        qm = at("q_T_masked", B, [P, 2, 4, 4, P])
        xr = at("x_again", C, [P, 2, D])
        x1 = at("x1_tile", C + 8, [P, 2, D])
        h2 = at("h2_tile", C + 16, [P, 2, D])
        h2T = at("h2_T", C + 24, [P, KT, P])
        n2w = at("norm2_w", C + 28, [P, D])
        packed = [C + 32]

        def pack(name, shape, dt=F32):
            t = at(name, packed[0], shape, dt)
            packed[0] += -(-int(np.prod(shape[1:])) * (2 if dt == BF16 else 4) // 32) / 32
            assert packed[0] <= DD
            return t

        rw = pack("router_w", [P, KT, E])
        rb = pack("router_b", [P, E])
        lg = pack("logits", [P, E])
        mx8 = pack("max8", [P, 8])
        ix8 = pack("ix8", [P, 8], U32)
        ixf = pack("ixf", [P, 8])
        gat = pack("gates", [P, NT, TOPK])
        gs = pack("gate_sum", [P, 8])
        iotaE = pack("iota_e", [P, MAXB])
        tri = pack("tri", [P, P], BF16)
        onb = pack("ones_bf", [P, P], BF16)
        mask = pack("mask", [P, NT, E], BF16)
        oh4 = at("onehot4", FV + 18, [P, NT, TOPK, E])
        slotE = at("slot_e", EE + 2, [P, NT, E])
        rt = at("route_tmp", EE + 2.5, [P, 8, E])
        ec = at("expert_counts", EE + 12, [P, 3, 2, E])
        cmpl = at("load_cmp", G, [P, E + 2, E])
        tabf = at("tables_f", G + 4.25, [P, 3, MAXB + 2])
        cmpb = at("block_cmp", EE + 4, [P, MAXB, E])
        prod = at("route_prod", EE + 10, [P, NT * TOPK, E])
        tokid = pack("tok_id", [P, NT * TOPK, 4], BF16)
        dslot = pack("slots", [P, NT * TOPK])
        ebf = pack("block_expert", [P, MAXB + 2])
        load_expert = pack("load_expert", [P, E + 2], I32)
        load_after = pack("load_after", [P, E + 2], I32)
        block_load = pack("block_load", [P, MAXB + 2], I32)
        nbi = pack("n_blocks", [P, 2], I32)
        eye96 = pack("sel_cols", [96, MAXB + 2], BF16)
        pm = pack("part_mod", [P, 4])
        ones = pack("ones", [P, P])
        xs = at("xs", EE, [P, D])
        xT = [at("xs_T_hi", EE + 4, [P, KT, P], F32R), at("xs_T_lo", G, [P, KT, P], F32R)]
        actT = [at("act_T_hi", EE + 8, [P, KT, P], F32R), at("act_T_lo", G + 4, [P, KT, P], F32R)]
        w_split = [[at(f"w_{part}{i}", (C if i < 4 else DD - 32) + 8 * i + 4 * j, [P, 1024], F32R)
                    for j, part in enumerate(("hi", "lo"))] for i in range(SPLIT)]
        ysb = at("y_rows_sb", EE + 12, [P, D])
        glu = at("glu", FV, [P, 3, 512])
        lin = at("lin", FV + 6, [P, 3, 512])
        bsrc = at("b_src", FV, [96, 3072])
        bcat = at("b_cat", FV + 12, [96, 3072], BF16)
        ohs = at("slot_onehot", FV + 18, [P, NT * TOPK, P], BF16)
        iotab = at("iota_slots", FV + 22, [P, P])
        selb = at("expert_sel", FV + 22.5, [96, P], BF16)
        idx = at("row_idx", FV + 22.75, [P, 4], I32)
        idf = at("row_idx_f", FV + 22.8125, [P, 2])
        fing = at("final_rows", A, [P, 16, D])
        fx1 = at("final_x1", B, [P, NT, D])
        facc = at("final_acc", B + 16, [P, NT, D])

        def raw(c):
            return w1[:, c, :] if c < W1C else w2[:, c - W1C, :]
        bank = [ctx.enter_context(nc.psum_tensor(f"bank{i}", [P, 512], F32)) for i in range(8)]

        dram = {n: nc.dram_tensor(n, sh, F32, kind="Internal").ap() for n, sh in {
            "u_rows": [512, 512], "y_rows": [512, 512], "x1_rows": [S, D], "h2_rows": [S, D],
            "ys_rows": [S * TOPK, D]}.items()}

        names = """ident_ready  s5_nat lam_loaded c_loaded adab_loaded x_loaded0 x_loaded1 n1w_loaded misc_loaded param_loaded
          pe_prep cq_ready bx_ready quad_ready af_psum af_ready inraw_ready in_tr in_done outm_ready k_mm k_ev kp_half
           sg_ready cbc_ready ada_mm ada_ev dve act pool   lam_e act_lam act_trig act_rope
          sq1 rs1 h_ready h_tr h_ev u_mm u_ev u_stored u_loaded q_mm q_sq q_ss q_rt q_n q_tr q_ev v_ev qm_ready s_mm s_ev scan_done
          sc_mm sc_max sc_exp a_ready a_tr a_ev pv_mm o_sq o_copied o_ss o_rt o_n o_tr o_ev 
          y_mm y_ev y_gp y_sig y_done y_stored0 y_stored1 y_cube y_loaded gluw_loaded g_mm g_sig s_act s_sq n_mm n_rt s5_done
          wout_loaded n2w_loaded rw_loaded mix_mm x1_ready x1_stored0 x1_stored1 m_sq m_rt h2_ready h2_stored0 h2_stored1 h2_tr h2_ev
          r_mm lg_ready g_exp mask_ready pos_mm blocks_ready consts2 bias_src bias_ready d_ready
          oh_ready idx_mm idx_ready xs_loaded idx_sum scat_ready xs_tr xs_ev x_lo sel_ready hi_done lo_dve lo_pool
          g_min g_sg l_a l_b act_ready act_tr act_ev act_lo y2_ev y2_stored
          fin_g0 fin_g1 fin_g2 fin_g3 fin_x1 fin_done fin_stored""".split()
        s = {n: sem(n) for n in names}
        ring_sem = [sem(f"ring_loaded{i}") for i in range(RING)]
        w_loaded = [sem(f"w_loaded{c}") for c in range(WCH // 2)]
        w_used = sem("w_used")
        ctx.enter_context(nc.allow_non_contiguous_dma(reason="vectors of a few hundred words"))
        ctx.enter_context(nc.allow_low_precision(reason="sums of a one and zeros, or small whole numbers"))
        block = ctx.enter_context(nc.Block())

        ada_v = I["ada_w"][0].rearrange("(k p) n -> p k n", p=P)
        win_v = I["w_in"][0].rearrange("(k p) n -> p k n", p=P)
        xv = I["x"][0].rearrange("(j i) d -> i j d", i=STEPS)
        ov = out[0].rearrange("(j i) d -> i j d", i=STEPS)

        def ada_bank(n):
            return (0, 1, 3, 4, 5, 6, 7)[n % 7]

        def low_ready(c, b):
            mine, name = (POOL_LOW, "lo_pool") if c in POOL_LOW else (DVE_LOW, "lo_dve")
            return s[name], b * len(mine) + (mine.index(c) + 1)

        @block.sync
        def _(sp):
            for k, n in enumerate(("s5_cmat_re", "s5_cmat_im", "s5_cmat_re")):
                sp.dma_start(CC[:, :, k, :], I[n][0].rearrange("d g c p -> (d g c) p")
                             .rearrange("(t q) p -> q t p", q=P)).then_inc(s["s5_nat"], 16)
            for k, n in enumerate(("s5_b_re", "s5_b_im", "s5_b_re")):
                sp.dma_start(BB[:, k, :], I[n][0].rearrange("d g p c -> (d g) (p c)")).then_inc(s["s5_nat"], 16)
            sp.dma_start(lam_t[:, 0, :], I["s5_lambda_re"][0].rearrange("d g p -> (d g) p")).then_inc(s["lam_loaded"], 16)
            sp.dma_start(lam_t[:, 1, :], I["s5_lambda_im"][0].rearrange("d g p -> (d g) p")).then_inc(s["lam_loaded"], 16)
            sp.dma_start(lstep[:, 0:1], I["s5_log_step"][0].rearrange("d (g o) -> (d g) o", o=1)).then_inc(s["lam_loaded"], 16)
            w_in_at = {U_CHUNK: 3, Q_CHUNK: 0, K_CHUNK: 1, V_CHUNK: 2}

            def dense(n):
                if n - RING >= ADA_CHUNKS:
                    sp.wait_ge(s["u_mm"], 4)
                elif n >= RING:
                    sp.wait_ge(s["ada_mm"], n - RING + 1)
                src = ada_v[:, :, n * 512:(n + 1) * 512] if n < ADA_CHUNKS else \
                    win_v[:, :, w_in_at[n] * 512:(w_in_at[n] + 1) * 512]
                sp.dma_start(ring[:, n % RING], src).then_inc(ring_sem[n % RING], 16)
            for n in range(V_CHUNK):
                dense(n)
                if n == 0:
                    sp.dma_start(mod[:].rearrange("p a d -> p (a d)"),
                                 I["ada_b"][0].partition_broadcast(P)).then_inc(s["adab_loaded"], 16)
            sp.wait_ge(s["inraw_ready"], 1)
            sp.wait_ge(s["outm_ready"], 2)
            sp.wait_ge(s["lam_e"], 3)
            sp.dma_start(n1w[:], I["norm1_w"][0].partition_broadcast(P)).then_inc(s["n1w_loaded"], 16)

            def x_tile(t):
                if t >= 2:
                    sp.wait_ge(s["h_tr"], t - 1)
                for k in range(2):
                    sp.dma_start(xt[64 * k:64 * k + 64, t % 2, :], xv[2 * t + k]).then_inc(s[f"x_loaded{t % 2}"], 16)

            def toeplitz(half):
                sp.wait_ge(s["k_ev"], 8 * (half + 1))
                gsl = slice(half * NG // 2, (half + 1) * NG // 2)
                for i in range(STEPS):
                    sp.dma_start(toep[i * GC:(i + 1) * GC, gsl, :].rearrange("p g (a c) -> p g a c", c=GC),
                                 kpad[:, :, 7 - i:15 - i, :]).then_inc(s["kp_half"], 16)
                if half == 0:
                    sp.wait_ge(s["kp_half"], 16 * STEPS)
            for t in range(3):
                x_tile(t)
            sp.wait_ge(s["ada_mm"], ADA_CHUNKS)
            toeplitz(0)
            x_tile(3)
            toeplitz(1)
            dense(V_CHUNK)
            sp.wait_ge(s["u_ev"], 4)
            sp.dma_start(dram["u_rows"].rearrange("(t p) n -> p t n", p=P), uT[:]).then_inc(s["u_stored"], 16)
            sp.wait_ge(s["u_stored"], 16)
            u_v = dram["u_rows"].rearrange("(g c) (i j) -> i c g j", c=GC, i=STEPS)
            for i in range(STEPS):
                sp.dma_start(U[i * GC:(i + 1) * GC], u_v[i]).then_inc(s["u_loaded"], 16)
            sp.wait_ge(s["scan_done"], 3)
            sp.dma_start(gluw[:], I["s5_glu_w"][0].rearrange("(k p) n -> p k n", p=P)).then_inc(s["gluw_loaded"], 16)
            sp.wait_ge(s["sc_mm"], 2 * NT * HEADS)
            sp.dma_start(wout[:], I["w_out"][0].rearrange("(k p) n -> p k n", p=P)).then_inc(s["wout_loaded"], 16)
            y_v = dram["y_rows"].rearrange("(g c) (i j) -> i c g j", c=GC, i=STEPS)
            for half in range(2):
                sp.wait_ge(s["y_done"], 2 * half + 2)
                g = slice(half * NG // 2, (half + 1) * NG // 2)
                for i in range(STEPS):
                    sp.dma_start(y_v[i, :, g], Y[i * GC:(i + 1) * GC, g]).then_inc(s[f"y_stored{half}"], 16)
            for half in range(2):
                sp.wait_ge(s[f"y_stored{half}"], 128)
                sp.dma_start(yT[:, 2 * half:2 * half + 2], dram["y_rows"][256 * half:256 * half + 256]
                             .rearrange("(t p) n -> p t n", p=P)).then_inc(s["y_loaded"], 16)
            sp.dma_start(n2w[:], I["norm2_w"][0].partition_broadcast(P)).then_inc(s["n2w_loaded"], 16)
            sp.dma_start(rw[:], I["router_w"][0].rearrange("(k p) n -> p k n", p=P)).then_inc(s["rw_loaded"], 16)
            sp.dma_start(rb[:], I["router_b"][0].partition_broadcast(P)).then_inc(s["rw_loaded"], 16)
            sp.wait_ge(s["pv_mm"], NT * HEADS)
            for q in range(3):
                sp.dma_start(bsrc[32 * q:32 * q + 32, 0:2048], I["mlp1_b"][0]).then_inc(s["bias_src"], 16)
                sp.dma_start(bsrc[32 * q:32 * q + 32, 2048:3072], I["mlp2_b"][0]).then_inc(s["bias_src"], 16)
            for t in range(NT):
                if t >= 2:
                    sp.wait_ge(s["x1_ready"], t - 1)
                for k in range(2):
                    sp.dma_start(xr[64 * k:64 * k + 64, t % 2, :], xv[2 * t + k]).then_inc(s[f"x_loaded{t % 2}"], 16)
                sp.wait_ge(s["x1_ready"], t + 1)
                sp.dma_start(dram["x1_rows"][t * P:(t + 1) * P, :], x1[:, t % 2, :]).then_inc(s[f"x1_stored{t % 2}"], 16)
                sp.wait_ge(s["h2_ready"], t + 1)
                sp.dma_start(dram["h2_rows"][t * P:(t + 1) * P, :], h2[:, t % 2, :]).then_inc(s[f"h2_stored{t % 2}"], 16)
            sp.wait_ge(s["s5_done"], 4)
            sp.wait_ge(s["mix_mm"], NT)
            sp.wait_ge(s["blocks_ready"], 1)
            n_blocks = sp.value_load(nbi[0:1, 0:1], min_val=1, max_val=MAXB)
            n_loads = sp.value_load(nbi[0:1, 1:2], min_val=1, max_val=E)

            def weights(chunks, n):
                e = sp.value_load(load_expert[0:1, bass.ds(n, 1)], min_val=0, max_val=E - 1)
                first = isinstance(n, int) and n == 0
                if not first:
                    last_block = sp.value_load(load_after[0:1, bass.ds(n, 1)], min_val=0, max_val=MAXB - 1)
                for c in chunks:
                    if not first:
                        sp.wait_ge(*low_ready(c, last_block))
                    half, k = c // KT, c % KT
                    src = I["mlp1_w"][0, bass.ds(e, 1), k * P:(k + 1) * P, half * 1024:half * 1024 + 1024] \
                        if c < W1C else I["mlp2_w"][0, bass.ds(e, 1), k * P:(k + 1) * P, :]
                    sp.dma_start(raw(c), src.rearrange("e p n -> (e p) n")).then_inc(w_loaded[c // 2], 16)

            weights(range(SPLIT), 0)
            sp.wait_ge(s["xs_loaded"], 16)
            weights(range(SPLIT, WCH), 0)
            weights(range(SPLIT), 1)
            with sp.Fori(1, n_loads) as n:
                weights(range(SPLIT, WCH), n)
                weights(range(SPLIT), n + 1)
            sp.wait_ge(s["fin_done"], 1)
            sp.dma_start(fx1[:], dram["x1_rows"].rearrange("(t p) n -> p t n", p=P)).then_inc(s["fin_x1"], 16)
            sp.wait_ge(s["y2_stored"], n_blocks * 16 + 16)
            for t in range(NT):
                sp.dma_start(fing[:, TOPK * t:TOPK * t + TOPK, :].rearrange("p k d -> p (k d)"),
                             dram["ys_rows"][t * P * TOPK:(t + 1) * P * TOPK, :]
                             .rearrange("(p k) d -> p (k d)", k=TOPK)).then_inc(s[f"fin_g{t}"], 16)
            for t in range(NT):
                sp.wait_ge(s["fin_done"], t + 2)
                for k in range(2):
                    sp.dma_start(ov[2 * t + k], facc[64 * k:64 * k + 64, t, :]).then_inc(s["fin_stored"], 16)
            sp.wait_ge(s["fin_stored"], 32 * NT)

        @block.gpsimd
        def _(pool):
            ch = Chain(pool, s["pool"])
            ch(pool.memset(ident[:], 0.0))
            ch(pool.memset(ones[:], 1.0))
            pool.affine_select(out=ident[:], in_=ident[:], compare_op=ALU.not_equal, fill=1.0, base=0,
                               pattern=[[-1, P]], channel_multiplier=1).then_inc(s["ident_ready"], 1)
            pool.wait_ge(s["ident_ready"], 1)
            ch(pool.memset(sgn[0:64, 0:1], -1.0))
            ch(pool.memset(sgn[64:128, 0:1], 1.0))
            ch(pool.memset(sgn[0:64, 1:2], 1.0))
            ch(pool.memset(sgn[64:128, 1:2], -1.0))
            ch(pool.memset(sgn[:, 2:3], EPS))
            ch(pool.memset(strip[:], 0.0))
            for m in range(4):
                ch(pool.memset(strip[32 * m:32 * m + 32, m:m + 1], 1.0))
            ch.sync()
            pool.dma_start(qkw[:, 0], I["q_norm_w"][0].partition_broadcast(P)).then_inc(s["param_loaded"], 16)
            pool.dma_start(qkw[:, 1], I["k_norm_w"][0].partition_broadcast(P)).then_inc(s["param_loaded"], 16)
            pool.dma_start(subw[:], I["subln_w"][0].partition_broadcast(P)).then_inc(s["param_loaded"], 16)
            for i in range(STEPS):
                pool.dma_start(dcol[i * GC:(i + 1) * GC, :], I["s5_d"][0].rearrange("(g c) -> c g", c=GC)).then_inc(s["param_loaded"], 16)
            pool.dma_start(glub[:], I["s5_glu_b"][0].rearrange("(t p) -> p t", p=P)).then_inc(s["param_loaded"], 16)
            pool.dma_start(outw[:], I["s5_out_norm_w"][0].rearrange("(t p) -> p t", p=P)).then_inc(s["param_loaded"], 16)
            pool.wait_ge(s["sg_ready"], 1)
            pool.wait_ge(s["cq_ready"], 2)
            pool.wait_ge(s["act"], 2)
            for l in POOL_LAGS:
                for di, pwr in ((0, l), (1, 8 - l)):
                    g = slice(di * NG, di * NG + NG)
                    pr, pi = (bc(PW[:, q, pwr, g], 2, GC, [P, NG, GC]) for q in range(2))
                    ch(pool.tensor_tensor(outM[:, g, l, :], CP[:, g, :], pr, ALU.mult))
                    ch(pool.tensor_tensor(pool_tmp[:, g, :], CQ[:, g, :], pi, ALU.mult))
                ch(pool.tensor_tensor(outM[:, :, l, :], outM[:, :, l, :], pool_tmp[:], ALU.add))
            pool.wait_ge(s["outm_ready"], 1)
            pool.tensor_copy(BS[:], P2[:]).then_inc(s["outm_ready"], 1)
            pool.wait_ge(s["s_mm"], 2 * DG // 8)

            def cmul(dst, x, y, n):
                X = [psq[:, q, x:x + n, :] for q in range(2)]
                Yb = [bc(psq[:, q, y, :], 1, n, [P, n, DG]) for q in range(2)]
                T = scan_w[:, 0:n * DG].rearrange("p (n g) -> p n g", g=DG)
                O = [psq[:, q, dst:dst + n, :] for q in range(2)]
                ch(pool.tensor_tensor(O[0], X[0], Yb[0], ALU.mult))
                ch(pool.tensor_tensor(T, X[1], Yb[1], ALU.mult))
                ch(pool.tensor_tensor(O[0], O[0], T, ALU.subtract))
                ch(pool.tensor_tensor(O[1], X[0], Yb[1], ALU.mult))
                ch(pool.tensor_tensor(T, X[1], Yb[0], ALU.mult))
                ch(pool.tensor_tensor(O[1], O[1], T, ALU.add))

            ch(pool.tensor_copy(psq[:, 0, 1, :], ab8[:, 0, :]))
            ch(pool.tensor_copy(psq[:, 1, 1, :], ab8[:, 1, :]))
            cmul(2, 1, 1, 1)
            cmul(3, 1, 2, 2)
            cmul(5, 1, 4, 4)
            pool.wait_ge(s["s_ev"], 2 * DG // 8)
            dirs = ((0, range(1, 8), -1), (1, range(6, -1, -1), 1))

            def view(T, di):
                return T[:, di * NG:(di + 1) * NG, :].rearrange("p g (c m) -> p g c m", m=8)

            def step(x1n, x2n, x1p, x2p, are, aim, shape, keep2=True):
                T = [scan_t[:, q, 0:int(np.prod(shape))].rearrange("p (g c) -> p g c", g=NG) for q in range(4)]
                ch(pool.tensor_tensor(T[0], x1p, are, ALU.mult))
                if keep2:
                    ch(pool.tensor_tensor(T[2], x2p, are, ALU.mult))
                    ch(pool.tensor_tensor(T[3], x1p, aim, ALU.mult))
                ch(pool.tensor_tensor(T[1], x2p, aim, ALU.mult))
                ch(pool.tensor_tensor(x1n, x1n, T[0], ALU.add))
                if keep2:
                    ch(pool.tensor_tensor(x2n, x2n, T[2], ALU.add))
                ch.sync()
                if keep2:
                    ch(pool.tensor_tensor(x2n, x2n, T[3], ALU.subtract))
                ch(pool.tensor_tensor(x1n, x1n, T[1], ALU.add))

            for di, order, back in dirs:
                V1, V2 = view(S1, di), view(S2, di)
                gs_ = slice(di * NG, (di + 1) * NG)

                def pw(q, k, n):
                    return bc(psq[:, q, k, gs_], 2, n, [P, NG, n])
                for m in order:
                    step(V1[:, :, :, m], V2[:, :, :, m], V1[:, :, :, m + back], V2[:, :, :, m + back],
                         pw(0, 1, 8), pw(1, 1, 8), [NG, 8])
                end = 7 if di == 0 else 0
                for c in (range(1, 8) if di == 0 else range(6, -1, -1)):
                    step(V1[:, :, c:c + 1, end], V2[:, :, c:c + 1, end], V1[:, :, c + back:c + back + 1, end],
                         V2[:, :, c + back:c + back + 1, end], pw(0, 8, 1), pw(1, 8, 1), [NG, 1])
                if di == 1:
                    break
                for m in range(7) if di == 0 else range(7, 0, -1):
                    k = m + 1 if di == 0 else 8 - m
                    dst = slice(1, 8) if di == 0 else slice(0, 7)
                    src = slice(0, 7) if di == 0 else slice(1, 8)
                    step(V1[:, :, dst, m], None, V1[:, :, src, end], V2[:, :, src, end],
                         pw(0, k, 7), pw(1, k, 7), [NG, 7], keep2=False)
                pool.nop().then_inc(s["scan_done"], 1)
            pool.nop().then_inc(s["scan_done"], 1)
            pool.wait_ge(s["y_ev"], 4)
            ch(pool.iota(iotaE[:], pattern=[[1, MAXB]], base=0, channel_multiplier=0, allow_small_or_imprecise_dtypes=True))
            ch(pool.memset(onb[:], 1.0))
            ch(pool.memset(tri[:], 1.0))
            ch(pool.memset(ones[:], 1.0))
            for q in range(3):
                ch(pool.iota(pm[32 * q:32 * q + 32, 0:1], pattern=[[1, 1]], base=0, channel_multiplier=1, allow_small_or_imprecise_dtypes=True))
            for col, pat, mult in ((0, [[0, NT], [0, TOPK]], 4), (1, [[TOPK * P, NT], [0, TOPK]], 0),
                                   (2, [[0, NT], [1, TOPK]], 0)):
                ch(pool.iota(tokid[:, :, col].rearrange("p (t k) -> p t k", k=TOPK), pattern=pat, base=0,
                             channel_multiplier=mult, allow_small_or_imprecise_dtypes=True))
            ch(pool.memset(tokid[:, :, 3:4], -UNUSED))
            ch.sync()
            pool.affine_select(out=tri[:], in_=tri[:], compare_op=ALU.is_gt, fill=0.0, base=0,
                               pattern=[[1, P]], channel_multiplier=-1).then_inc(s["consts2"], 1)
            pool.wait_ge(s["bias_src"], 96)
            ch(pool.tensor_copy(bcat[:], bsrc[:]))
            for q in (1, 2):
                ch(pool.tensor_tensor(bsrc[32 * q:32 * q + 32], bsrc[32 * q:32 * q + 32],
                                           bcat[32 * q:32 * q + 32], ALU.subtract))
            ch.sync()
            for q in (1, 2):
                ch(pool.tensor_copy(bcat[32 * q:32 * q + 32], bsrc[32 * q:32 * q + 32]))
            ch.sync()
            ch(pool.tensor_tensor(bsrc[64:96], bsrc[64:96], bcat[64:96], ALU.subtract))
            pool.tensor_copy(bcat[64:96], bsrc[64:96]).then_inc(s["bias_ready"], 1)
            pool.wait_ge(s["bias_ready"], 1)
            pool.iota(iotab[:], pattern=[[1, P]], base=0, channel_multiplier=0,
                      allow_small_or_imprecise_dtypes=True).then_inc(s["bias_ready"], 1)
            pool.wait_ge(s["h2_stored0"], 32)
            pool.wait_ge(s["h2_stored1"], 32)
            pool.wait_ge(s["blocks_ready"], 2)
            n_blocks = pool.value_load(nbi[0:1, 0:1], min_val=1, max_val=MAXB)

            last_token, last_row = pool.to_reg(S - 1), pool.to_reg(S * TOPK - 1)

            def low(c, b):
                pool.wait_ge(s["hi_done"], b * WCH + (c + 1))
                hi, lo = w_split[c % SPLIT]
                pool.tensor_tensor(out=lo[:], in0=raw(c), in1=hi[:].bitcast(F32), op=ALU.subtract).then_inc(s["lo_pool"], 1)

            def gather(first):
                pool.wait_ge(s["idx_ready"], first)
                pool.sem_inc(s["pool"], 1)
                pool.indirect_dma_start(out=xs[:], out_offset=None, in_=dram["h2_rows"],
                                        in_offset=bass.IndirectOffsetOnAxis(ap=idx[:, 0:1], axis=0),
                                        bounds_check=last_token).then_inc(s["xs_loaded"], 16)
            gather(1)
            pool.dma_start(ysb[:, 0:E], dram["h2_rows"][0:P, 0:E]).then_inc(s["y2_stored"], 16)
            with pool.Fori(0, n_blocks) as b:
                v, next2 = b + 1, b * 2 + 4
                low(POOL_LOW[0], b)
                pool.wait_ge(s["xs_tr"], b * 2 + 2)
                gather(b * 2 + 3)
                pool.wait_ge(s["idx_ready"], b * 2 + 2)
                pool.wait_ge(s["y2_stored"], v * 16)
                pool.sem_inc(s["pool"], 1)
                pool.tensor_copy(idx[:, 2:3], idx[:, 1:2]).then_inc(s["scat_ready"], 1)
                low(POOL_LOW[1], b)
                for c in POOL_LOW[2:]:
                    low(c, b)
                pool.wait_ge(s["y2_ev"], next2)
                pool.wait_ge(s["scat_ready"], v)
                pool.sem_inc(s["pool"], 1)
                pool.indirect_dma_start(out=dram["ys_rows"], in_=ysb[:], in_offset=None,
                                        out_offset=bass.IndirectOffsetOnAxis(ap=idx[:, 2:3], axis=0),
                                        bounds_check=last_row, oob_is_err=False).then_inc(s["y2_stored"], 16)
        @block.scalar
        def _(act):
            ch = Chain(act, s["act"])
            act.dma_start(ccol[:, 0, :], I["c"][0].rearrange("(t p) -> p t", p=P)).then_inc(s["c_loaded"], 16)
            for k, n in enumerate(("lambda_q1", "lambda_q2", "lambda_k1", "lambda_k2")):
                act.dma_start(lam_in[:, k], I[n][0].partition_broadcast(P)).then_inc(s["misc_loaded"], 16)
            pos_v = I["positions"][0].rearrange("(j t h) -> h j t", t=NT, h=2)
            for k in range(2):
                act.dma_start(posi[64 * k:64 * k + 64, :], pos_v[k]).then_inc(s["misc_loaded"], 16)
            act.wait_ge(s["c_loaded"], 16)
            act.activation(ccol[:, 1, :], ccol[:, 0, :], ACT.Sigmoid).then_inc(s["lam_e"], 1)
            act.wait_ge(s["ident_ready"], 1)
            act.wait_ge(s["pool"], 7)
            act.wait_ge(s["pe_prep"], 1)
            for b in range(2):
                ch.free(act.activation(CP[:].rearrange("p g c -> p (g c)")[:, 512 * b:512 * b + 512], bank[b][:], ACT.Identity,
                                       scale=sgn[:, 1:2]))
                act.activation(CQ[:].rearrange("p g c -> p (g c)")[:, 512 * b:512 * b + 512], bank[2 + b][:], ACT.Identity,
                               scale=-1.0).then_inc(s["cq_ready"], 1)
            ch.sync()
            act.wait_ge(s["pe_prep"], 2)
            for b in range(2):
                act.activation(P2[:].rearrange("p c g -> p (c g)")[:, 512 * b:512 * b + 512], bank[4 + b][:], ACT.Identity).then_inc(s["bx_ready"], 1)
                act.activation(Q2[:].rearrange("p c g -> p (c g)")[:, 512 * b:512 * b + 512], bank[6 + b][:], ACT.Identity,
                               scale=sgn[:, 0:1]).then_inc(s["bx_ready"], 1)
            act.wait_ge(s["lam_loaded"], 48)
            ch(act.activation(lstep[:, 1:2], lstep[:, 0:1], ACT.Exp))
            act.activation(lam_t[:, 2, :], lam_t[:, 0, :], ACT.Exp, scale=lstep[:, 1:2]).then_inc(s["act_lam"], 1)
            act.wait_ge(s["act_trig"], 1)
            act.activation(lam_t[:, 4:6, :], lam_t[:, 4:6, :], ACT.Sin).then_inc(s["lam_e"], 1)
            act.wait_ge(s["af_psum"], 1)
            act.activation(AF[:].rearrange("p a g -> p (a g)"), bank[2][:, 0:4 * DG], ACT.Identity).then_inc(s["af_ready"], 1)
            act.wait_ge(s["act_rope"], 1)
            act.activation(lamv[:, 2:4], lamv[:, 0:2], ACT.Exp).then_inc(s["act_lam"], 1)
            act.wait_ge(s["act_rope"], 2)
            act.activation(cs[:].rearrange("p a t k -> p (a t k)"), rope_t[:, 0:2].rearrange("p a t k -> p (a t k)"),
                           ACT.Sin).then_inc(s["lam_e"], 1)
            for n in range(DG // 4):
                act.wait_ge(s["in_tr"], n + 1)
                act.activation(inT[:, 4 * n:4 * n + 4, :].rearrange("p g m -> p (g m)"), bank[2 + n % 4][:], ACT.Identity).then_inc(s["in_done"], 1)
            def kernels(first):
                for n in range(first, first + 4):
                    act.wait_ge(s["k_mm"], n + 1)
                    if n == 8:
                        act.wait_ge(s["kp_half"], 16 * STEPS)
                    act.activation(kpad[:, 2 * (n % 8):2 * (n % 8) + 2].rearrange("p g a c -> p (g a c)"),
                                   bank[6 + n % 2][0:GC, 0:480], ACT.Identity).then_inc(s["k_ev"], 1)

            def x_norm(t):
                act.wait_ge(s[f"x_loaded{t % 2}"], 32 * (t // 2 + 1))
                if t:
                    act.wait_ge(s["rs1"], t)
                for k in range(2):
                    ch.free(act.activation(bank[4 + k][:], xt[:, t % 2, 512 * k:512 * k + 512], ACT.Square,
                                           accum_out=sq_s[:, k:k + 1]))
                ch.sync()
                act.nop().then_inc(s["sq1"], 1)
                act.wait_ge(s["m_sq"], t + 1)
                act.activation(sq_s[:, 3:4], sq_s[:, 2:3], ACT.Sqrt, scale=1.0 / D, bias=sgn[:, 2:3]).then_inc(s["sq1"], 1)

            def h_out(t):
                act.wait_ge(s["h_tr"], t + 1)
                for k in range(2):
                    act.activation(hT[:, 4 * k:4 * k + 4, t * P:(t + 1) * P],
                                   bank[2 * (t % 2) + k][:].rearrange("p (k n) -> p k n", n=P), ACT.Identity).then_inc(s["h_ev"], 1)
            act.wait_ge(s["in_done"], DG // 4)
            x_norm(0)
            kernels(0)
            x_norm(1)
            act.wait_ge(s["outm_ready"], 2)
            h_out(0)
            kernels(4)
            x_norm(2)
            h_out(1)
            x_norm(3)
            h_out(2)
            kernels(8)
            h_out(3)
            kernels(12)
            for n in range(4):
                act.wait_ge(s["u_mm"], n + 1)
                act.activation(uT[:, n, :], bank[n][:], ACT.Identity).then_inc(s["u_ev"], 1)
            def qk_rms(n):
                bk = bank[4 + n] if n < 4 else bank[n - 4]
                act.wait_ge(s["q_mm"], n + 1)
                if n >= 2:
                    act.wait_ge(s["q_ss"], n - 1)
                act.activation(sqb[:, n % 2, :], bk[:], ACT.Square).then_inc(s["q_sq"], 1)
                act.wait_ge(s["q_ss"], n + 1)
                act.activation(qk_s[:, 1, :], qk_s[:, 0, :], ACT.Sqrt, scale=1.0 / QK, bias=sgn[:, 2:3]).then_inc(s["q_rt"], 1)

            def qk_out(n):
                act.wait_ge(s["q_tr"], n + 1)
                bk = bank[4 + n] if n < 4 else bank[n - 4]
                act.activation(qkT[:, n // 4, :, (n % 4) * P:(n % 4) * P + P],
                               bk[:].rearrange("p (b n) -> p b n", n=P), ACT.Identity).then_inc(s["q_ev"], 1)
            def scan_inputs(n):
                for k in range(2):
                    act.wait_ge(s["s_mm"], 2 * n + k + 1)
                    act.activation((S1, S2)[k][:, 8 * n:8 * n + 8, :].rearrange("p g j -> p (g j)"),
                                   bank[4 + 2 * (n % 2) + k][:], ACT.Identity).then_inc(s["s_ev"], 1)
            for n in range(8):
                qk_rms(n)
                if n == 0:
                    act.wait_ge(s["kp_half"], 32 * STEPS)
                if n >= 4:
                    scan_inputs(2 * n - 8)
                    scan_inputs(2 * n - 7)
                qk_out(n)
            for n in range(4):
                act.wait_ge(s["q_mm"], 8 + n + 1)
                act.activation(vv[:, n, :], bank[4 + n][:], ACT.Identity).then_inc(s["v_ev"], 1)
            scale = QK ** -0.5
            act.wait_ge(s["q_ev"], 8)
            act.wait_ge(s["pool"], 12)

            def q_masked(t, m):
                act.activation(qm[:, t % 2, m], qkT[:, 0, :, t * P:(t + 1) * P], ACT.Identity,
                               scale=strip[:, m:m + 1]).then_inc(s["qm_ready"], 1)
            for m in range(4):
                q_masked(0, m)

            def o_root(t):
                act.wait_ge(s["o_ss"], t + 1)
                act.activation(qk_s[:, 1, 0:8], qk_s[:, 0, 0:8], ACT.Sqrt, scale=1.0 / DV, bias=sgn[:, 2:3]).then_inc(s["o_rt"], 1)

            def o_out(t):
                act.wait_ge(s["o_tr"], t + 1)
                act.activation(catT[:, 0:4, t * P:(t + 1) * P], bank[7][:].rearrange("p (k n) -> p k n", n=P),
                               ACT.Identity).then_inc(s["o_ev"], 1)

            def probs_out(m):
                act.wait_ge(s["a_tr"], m + 1)
                if m >= 2:
                    act.wait_ge(s["pv_mm"], m - 1)
                act.activation(aT[:, m % 2].rearrange("p k q -> p (k q)"), bank[4 + m % 2][:],
                               ACT.Identity).then_inc(s["a_ev"], 1)
            for n in range(NT * HEADS):
                t, h = n // HEADS, n % HEADS
                act.wait_ge(s["sc_max"], n + 1)
                if n >= 2:
                    act.wait_ge(s["a_tr"], n - 1)
                for c in range(2):
                    act.activation(ee[:, n % 2, c, :], bank[2 * (n % 2) + c][:], ACT.Exp, scale=scale,
                                   bias=att_s[:, n % 2, 2 + c:3 + c],
                                   accum_out=att_s[:, n % 2, 4 + c:5 + c]).then_inc(s["sc_exp"], 1)
                if n >= 2:
                    probs_out(n - 2)
                if h < 4 and t + 1 < NT:
                    if t:
                        act.wait_ge(s["sc_mm"], 2 * HEADS * t)
                    q_masked(t + 1, h)
                if h == 4 and t:
                    o_root(t - 1)
                if h == 7 and t:
                    o_out(t - 1)
            probs_out(NT * HEADS - 2)
            probs_out(NT * HEADS - 1)
            o_root(NT - 1)
            o_out(NT - 1)
            cube = [S2[:, 8 * n:8 * n + 8, :] for n in range(4)]

            def y_square(n):
                act.wait_ge(s["y_gp"], n + 1)
                act.activation(cube[n], Y[:, 8 * n:8 * n + 8, :], ACT.Square).then_inc(s["y_ev"], 1)

            def y_sigmoid(n):
                act.wait_ge(s["y_cube"], n + 1)
                act.activation(cube[n], cube[n], ACT.Sigmoid, scale=GELU_A * GELU_B).then_inc(s["y_sig"], 1)
            y_square(0)
            y_square(1)
            y_sigmoid(0)
            y_square(2)
            y_sigmoid(1)
            y_square(3)
            y_sigmoid(2)
            y_sigmoid(3)
            for n in range(4):
                act.wait_ge(s["g_mm"], n + 1)
                if n == 0:
                    act.wait_ge(s["param_loaded"], 16 * 13)
                act.activation(sT[:, n, :], bank[4 + n][:], ACT.Sigmoid, bias=glub[:, n:n + 1]).then_inc(s["g_sig"], 1)
            for n in range(4):
                act.wait_ge(s["s_act"], n + 1)
                act.activation(sqT[:, n, :], sT[:, n, :], ACT.Square).then_inc(s["s_sq"], 1)
            act.wait_ge(s["n_mm"], 1)
            act.activation(gluw[:, 0, :], bank[4][:], ACT.Sqrt, scale=1.0 / 512, bias=sgn[:, 2:3]).then_inc(s["n_rt"], 1)
            for t in range(NT):
                act.wait_ge(s["x1_ready"], t + 1)
                if t:
                    act.wait_ge(s["h2_ready"], t)
                if t >= 2:
                    act.wait_ge(s[f"h2_stored{t % 2}"], 16 * (t // 2))
                    act.wait_ge(s["h2_tr"], t - 1)
                for k in range(2):
                    ch.free(act.activation(h2[:, t % 2, 512 * k:512 * k + 512], x1[:, t % 2, 512 * k:512 * k + 512],
                                           ACT.Square, accum_out=sq_s[:, 8 + k:9 + k]))
                ch.sync()
                act.nop().then_inc(s["o_sq"], 1)
                act.wait_ge(s["m_rt"], t + 1)
                act.activation(sq_s[:, 11:12], sq_s[:, 10:11], ACT.Sqrt, scale=1.0 / D, bias=sgn[:, 2:3]).then_inc(s["o_sq"], 1)
                act.wait_ge(s["h2_tr"], t + 1)
                for k in range(2):
                    act.activation(h2T[:, 4 * k:4 * k + 4, :].rearrange("p k n -> p (k n)"), bank[4 + k][:],
                                   ACT.Identity).then_inc(s["h2_ev"], 1)
                act.wait_ge(s["lg_ready"], t + 1)
                act.activation(gat[:, t, :], mx8[:, 0:TOPK], ACT.Exp, bias=gs[:, 2:3], accum_out=gs[:, 0:1]).then_inc(s["g_exp"], 1)
            act.wait_ge(s["blocks_ready"], 2)
            n_blocks = act.value_load(nbi[0:1, 0:1], min_val=1, max_val=MAXB)

            act.wait_ge(s["h2_stored0"], 32)
            act.wait_ge(s["h2_stored1"], 32)
            act.wait_ge(s["x1_stored0"], 32)
            act.wait_ge(s["x1_stored1"], 32)

            def loaded(b):
                return act.value_load(block_load[0:1, bass.ds(b, 1)], min_val=32, max_val=32 * (E + 1))

            def high(chunks, b, w_in, first=False):
                for c in chunks:
                    if c % 2 == 0 or c == chunks[0]:
                        act.wait_ge(w_loaded[c // 2], w_in)
                    if not first:
                        act.wait_ge(w_used, b * WCH + (c + 1 - SPLIT))
                    act.activation(w_split[c % SPLIT][0][:], raw(c), ACT.Identity).then_inc(s["hi_done"], 1)

            def x_out(k, b2):
                act.wait_ge(s["xs_tr"], b2 + (k + 1))
                act.activation(xT[0][:, 4 * k:4 * k + 4, :].rearrange("p k n -> p (k n)"), bank[7 - k][:],
                               ACT.Identity).then_inc(s["xs_ev"], 1)

            def gate(k, b2):
                act.wait_ge(s["g_min"], b2 + (k + 1))
                act.activation(glu[:, 1 + k, :] if k == 0 else lin[:, 2, :], glu[:, 0, :] if k == 0 else glu[:, 2, :],
                               ACT.Sigmoid, scale=1.702).then_inc(s["g_sg"], 1)

            def act_out(k, b2):
                act.wait_ge(s["act_tr"], b2 + (k + 1))
                act.activation(actT[0][:, 4 * k:4 * k + 4, :].rearrange("p k n -> p (k n)"), bank[6 + k][:],
                               ACT.Identity).then_inc(s["act_ev"], 1)
            high(range(SPLIT), 0, 32, first=True)
            x_out(0, 0)
            x_out(1, 0)
            act.sem_inc(s["y2_ev"], 2)
            with act.Fori(0, n_blocks) as b:
                b2, w_in, next_w_in = b * 2, loaded(b), loaded(b + 1)
                high(range(SPLIT, 14), b, w_in)
                gate(0, b2)
                high(range(14, 21), b, w_in)
                act_out(0, b2)
                gate(1, b2)
                x_out(0, b2 + 2)
                high(range(21, WCH), b, w_in)
                high(range(0, 1), b + 1, next_w_in)
                act_out(1, b2)
                x_out(1, b2 + 2)
                high(range(1, SPLIT), b + 1, next_w_in)
                act.wait_ge(w_used, b * WCH + WCH)
                act.wait_ge(s["scat_ready"], b + 1)
                for k in range(2):
                    act.activation(ysb[:, 512 * k:512 * k + 512], bank[4 + k][:], ACT.Identity).then_inc(s["y2_ev"], 1)

        @block.vector
        def _(dve):
            ch = Chain(dve, s["dve"])

            def tt(o, a, b_, op):
                return dve.tensor_tensor(o, a, b_, op)

            dve.wait_ge(s["c_loaded"], 16)
            dve.wait_ge(s["lam_e"], 1)
            ch(tt(ccol[:, 2, :], ccol[:, 0, :], ccol[:, 1, :], ALU.mult))
            dve.tensor_copy(cbc[:], bc(ccol[:, 2, :], 2, P, [P, KT, P])).then_inc(s["cbc_ready"], 1)

            def reduce_angle(dst, src, shift, tmp, tmpi):
                ch(dve.tensor_scalar(tmp, src, 1 / (2 * math.pi), shift / (2 * math.pi), ALU.mult, ALU.add))
                ch(dve.tensor_copy(tmpi, tmp))
                ch(dve.tensor_copy(tmp, tmpi))
                ch(dve.scalar_tensor_tensor(dst, tmp, -C1, src, ALU.mult, ALU.add))
                ch(dve.scalar_tensor_tensor(dst, tmp, -C2, dst, ALU.mult, ALU.add))
                ch(dve.scalar_tensor_tensor(dst, tmp, -C3, dst, ALU.mult, ALU.add))
                if shift:
                    ch(dve.tensor_scalar(dst, dst, shift, None, ALU.add))
                ch(dve.tensor_scalar(tmp, dst, -math.pi, 2 * math.pi, ALU.is_lt, ALU.mult))
                ch(tt(dst, dst, tmp, ALU.add))
                ch(dve.tensor_scalar(tmp, dst, math.pi, -2 * math.pi, ALU.is_gt, ALU.mult))
                ch(tt(dst, dst, tmp, ALU.add))
                ch(dve.tensor_scalar(dst, dst, 3.1415925, -3.1415925, ALU.min, ALU.max))

            L = [lam_t[:, k, :] for k in range(16)]
            dve.wait_ge(s["lam_loaded"], 48)
            dve.wait_ge(s["act_lam"], 1)
            ch(dve.tensor_scalar(L[3], L[1], lstep[:, 1:2], None, ALU.mult))
            reduce_angle(L[4], L[3], 0.0, L[6], rope_i[0:DG, :])
            reduce_angle(L[5], L[3], math.pi / 2, L[6], rope_i[0:DG, :])
            dve.nop().then_inc(s["act_trig"], 1)
            dve.wait_ge(s["lam_e"], 2)
            ch.free(tt(quad[:, 0, 0, :], L[2], L[5], ALU.mult))
            ch.free(tt(quad[:, 1, 0, :], L[2], L[4], ALU.mult))
            ch.free(tt(L[7], L[0], L[0], ALU.mult))
            ch(tt(L[8], L[1], L[1], ALU.mult))
            ch.free(tt(L[7], L[7], L[8], ALU.add))
            ch(dve.tensor_scalar(L[9], quad[:, 0, 0, :], -1.0, None, ALU.add))
            ch.free(dve.reciprocal(L[7], L[7]))
            ch.free(tt(L[10], L[9], L[0], ALU.mult))
            ch.free(tt(L[11], quad[:, 1, 0, :], L[1], ALU.mult))
            ch.free(tt(L[12], quad[:, 1, 0, :], L[0], ALU.mult))
            ch(tt(L[13], L[9], L[1], ALU.mult))
            ch.free(tt(L[10], L[10], L[11], ALU.add))
            ch(tt(L[12], L[12], L[13], ALU.subtract))
            ch.free(tt(quad[:, 2, 0, :], L[10], L[7], ALU.mult))
            ch(tt(quad[:, 3, 0, :], L[12], L[7], ALU.mult))
            dve.tensor_copy(quad[:, :, 1, :], quad[:, :, 0, :]).then_inc(s["quad_ready"], 1)
            modf = mod[:].rearrange("p a d -> p (a d)")
            dve.wait_ge(s["adab_loaded"], 16)

            def ada_out(n):
                dve.wait_ge(s["ada_mm"], n + 1)
                tt(modf[:, n * 512:(n + 1) * 512], bank[ada_bank(n)][:], modf[:, n * 512:(n + 1) * 512],
                   ALU.add).then_inc(s["ada_ev"], 1)
            ada_out(0)
            dve.wait_ge(s["af_ready"], 1)
            ch.free(dve.memset(PW[:, 0, 0, :], 1.0))
            ch.free(dve.memset(PW[:, 1, 0, :], 0.0))
            ch.free(dve.tensor_copy(PW[:, 0, 1, :], AF[:, 0, :]))
            ch(dve.tensor_copy(PW[:, 1, 1, :], AF[:, 1, :]))

            def cmul(dst, x, y, n):
                X = [PW[:, q, x:x + n, :] for q in range(2)]
                Yb = [bc(PW[:, q, y, :], 1, n, [P, n, DG]) for q in range(2)]
                T = t1[:, 0:n * DG].rearrange("p (n g) -> p n g", g=DG)
                O = [PW[:, q, dst:dst + n, :] for q in range(2)]
                ch.free(tt(O[0], X[0], Yb[0], ALU.mult))
                ch(tt(T, X[1], Yb[1], ALU.mult))
                ch(tt(O[0], O[0], T, ALU.subtract))
                ch.free(tt(O[1], X[0], Yb[1], ALU.mult))
                ch(tt(T, X[1], Yb[0], ALU.mult))
                ch(tt(O[1], O[1], T, ALU.add))
            cmul(2, 1, 1, 1)
            cmul(3, 1, 2, 2)
            cmul(5, 1, 4, 4)
            ch.free(dve.tensor_copy(ab8[:, 0, :], PW[:, 0, 8, :]))
            dve.tensor_scalar(ab8[:, 1, :], PW[:, 1, 8, :], sgn[:, 0:1], None, ALU.mult).then_inc(s["sg_ready"], 1)
            dve.wait_ge(s["misc_loaded"], 16 * 6)
            ch(tt(lam_w[:], lam_in[:, 0:2], lam_in[:, 2:4], ALU.mult))
            dve.tensor_reduce(lamv[:, 0:2], lam_w[:], AX.X, ALU.add).then_inc(s["act_rope"], 1)
            inv = [np.float32(ROPE_THETA) ** np.float32(-2 * k / (2 * ROT_HALF)) for k in range(ROT_HALF)]
            ch(dve.tensor_copy(rope_t[:, 2, :, 0], posi[:]))
            for k in range(ROT_HALF):
                ch.free(dve.tensor_scalar(rope_t[:, 3, :, k], rope_t[:, 2, :, 0], float(inv[k]), None, ALU.mult))
            ch.sync()

            def flat(k):
                return rope_t[:, k].rearrange("p t k -> p (t k)")
            reduce_angle(flat(0), flat(3), math.pi / 2, flat(4), rope_i[:, 0:16])
            reduce_angle(flat(1), flat(3), 0.0, flat(4), rope_i[:, 0:16])
            dve.nop().then_inc(s["act_rope"], 1)
            dve.wait_ge(s["act_lam"], 2)
            ch(tt(lamv[:, 4:5], lamv[:, 3:4], lamv[:, 2:3], ALU.subtract))
            ch(dve.tensor_scalar(lamv[:, 5:6], lamv[:, 4:5], -LAMBDA_INIT, None, ALU.add))
            dve.wait_ge(s["bx_ready"], 4)
            dve.wait_ge(s["pe_prep"], 2)
            fr, fi = (bc(AF[:, 2 + q, :], 1, GC, [P, GC, DG]) for q in range(2))
            T1, TB = (x[:].rearrange("p (c g) -> p c g", g=DG) for x in (t1, tB))
            ch.free(tt(T1, Q2[:], fi, ALU.mult))
            ch(tt(TB, P2[:], fi, ALU.mult))
            ch.free(tt(P2[:], P2[:], fr, ALU.mult))
            ch(tt(Q2[:], Q2[:], fr, ALU.mult))
            ch.free(tt(P2[:], P2[:], T1, ALU.add))
            ch(tt(Q2[:], Q2[:], TB, ALU.subtract))
            TG = t1[:].rearrange("p (g c) -> p g c", c=GC)
            TH = tB[:].rearrange("p (g c) -> p g c", c=GC)
            p2g, q2g = (x[:].rearrange("p c g -> p g c") for x in (P2, Q2))
            inv_v = inT[:].rearrange("p g (i c) -> p g i c", c=GC)
            for i in range(STEPS):
                for di, pwr in ((0, 7 - i), (1, i)):
                    g = slice(di * NG, di * NG + NG)
                    pr, pi = (bc(PW[:, q, pwr, g], 2, GC, [P, NG, GC]) for q in range(2))
                    ch.free(tt(inv_v[:, g, i, :], p2g[:, g, :], pr, ALU.mult))
                    ch.free(tt(TG[:, g, :], q2g[:, g, :], pi, ALU.mult))
                ch.sync()
                ch(tt(inv_v[:, :, i, :], inv_v[:, :, i, :], TG, ALU.add))
                if i % 2 == 0:
                    ada_out(1 + i // 2)
            dve.nop().then_inc(s["inraw_ready"], 1)
            dve.wait_ge(s["cq_ready"], 2)
            dve.wait_ge(s["act"], 2)
            lags = [l for l in range(STEPS + 1) if l not in POOL_LAGS]
            for l in lags:
                for di, pwr in ((0, l), (1, 8 - l)):
                    g = slice(di * NG, di * NG + NG)
                    pr, pi = (bc(PW[:, q, pwr, g], 2, GC, [P, NG, GC]) for q in range(2))
                    ch.free(tt(outM[:, g, l, :], CP[:, g, :], pr, ALU.mult))
                    ch.free(tt((TG, TH)[l % 2][:, g, :], CQ[:, g, :], pi, ALU.mult))
                ch.sync()
                ch(tt(outM[:, :, l, :], outM[:, :, l, :], (TG, TH)[l % 2], ALU.add))
                ada_out(5 + l)
            dve.nop().then_inc(s["outm_ready"], 1)
            for n in range(5 + len(lags), ADA_CHUNKS):
                ada_out(n)
            dve.wait_ge(s["ada_ev"], ADA_CHUNKS)
            dve.wait_ge(s["n1w_loaded"], 16)
            ch(dve.scalar_tensor_tensor(mod[:, 1], mod[:, 1], 1.0, n1w[:], ALU.add, ALU.mult))
            for t in range(NT):
                dve.wait_ge(s["sq1"], 2 * t + 1)
                tt(sq_s[:, 2:3], sq_s[:, 0:1], sq_s[:, 1:2], ALU.add).then_inc(s["m_sq"], 1)
                dve.wait_ge(s["sq1"], 2 * t + 2)
                dve.reciprocal(sq_s[:, 4:5], sq_s[:, 3:4]).then_inc(s["rs1"], 1)
                dve.wait_ge(s["rs1"], t + 1)
                ch(dve.scalar_tensor_tensor(xt[:, t % 2], xt[:, t % 2], sq_s[:, 4:5], mod[:, 1], ALU.mult, ALU.mult))
                tt(xt[:, t % 2], xt[:, t % 2], mod[:, 0], ALU.add).then_inc(s["h_ready"], 1)
            dve.wait_ge(s["h_tr"], NT)
            dve.wait_ge(s["param_loaded"], 16 * 13)
            for n in range(8):
                t, w = n % 4, n // 4
                bk = bank[4 + n] if n < 4 else bank[n - 4]
                dve.wait_ge(s["q_sq"], n + 1)
                dve.tensor_reduce(qk_s[:, 0, :], sqb[:, n % 2, :].rearrange("p (g d) -> p g d", d=QK), AX.X,
                                  ALU.add).then_inc(s["q_ss"], 1)
                dve.wait_ge(s["q_rt"], n + 1)
                ch(dve.reciprocal(qk_s[:, 2, :], qk_s[:, 1, :]))
                if n >= 2:
                    dve.wait_ge(s["q_tr"], n - 1)
                X = stg[:, n % 2, :].rearrange("p (g d) -> p g d", d=QK)
                NGP = 2 * HEADS
                ch(tt(X, bk[:].rearrange("p (g d) -> p g d", d=QK), bc(qk_s[:, 2, :], 2, QK, [P, NGP, QK]), ALU.mult))
                ch(tt(X, X, bc(qkw[:, w, :], 1, NGP, [P, NGP, QK]), ALU.mult))
                cb, sb_ = (bc(cs[:, q, t, :], 1, NGP, [P, NGP, ROT_HALF]) for q in range(2))
                a, b_ = X[:, :, 0:ROT_HALF], X[:, :, ROT_HALF:2 * ROT_HALF]
                R = sqb[:, n % 2, 0:256].rearrange("p (q g k) -> p q g k", q=4, k=ROT_HALF)
                if n == 0:
                    dve.wait_ge(s["lam_e"], 3)
                ch.free(tt(R[:, 0], a, cb, ALU.mult))
                ch.free(tt(R[:, 1], b_, sb_, ALU.mult))
                ch.free(tt(R[:, 2], b_, cb, ALU.mult))
                ch(tt(R[:, 3], a, sb_, ALU.mult))
                ch.free(tt(a, R[:, 0], R[:, 1], ALU.subtract))
                ch(tt(b_, R[:, 2], R[:, 3], ALU.add))
                dve.nop().then_inc(s["q_n"], 1)
            def o_norm(t):
                dve.wait_ge(s["pv_mm"], HEADS * (t + 1))
                bk = bank[6]
                if t:
                    dve.wait_ge(s["o_tr"], t)
                dve.tensor_copy(o_n[:, 0, :], bk[:]).then_inc(s["o_copied"], 1)
                dve.wait_ge(s["o_copied"], t + 1)
                ch(tt(o_n[:, 1, :], o_n[:, 0, :], o_n[:, 0, :], ALU.mult))
                dve.tensor_reduce(qk_s[:, 0, 0:8], o_n[:, 1, :].rearrange("p (h d) -> p h d", d=DV), AX.X,
                                  ALU.add).then_inc(s["o_ss"], 1)

            def o_scale(t):
                dve.wait_ge(s["o_rt"], t + 1)
                ch(dve.reciprocal(qk_s[:, 2, 0:8], qk_s[:, 1, 0:8]))
                O = o_n[:, 0, :].rearrange("p (h d) -> p h d", d=DV)
                ch(tt(O, O, bc(qk_s[:, 2, 0:8], 2, DV, [P, HEADS, DV]), ALU.mult))
                ch(tt(O, O, bc(subw[:], 1, HEADS, [P, HEADS, DV]), ALU.mult))
                dve.nop().then_inc(s["o_n"], 1)
            ch(dve.tensor_scalar(subw[:], subw[:], 1.0 - LAMBDA_INIT, None, ALU.mult))
            dve.wait_ge(s["q_ev"], 8)
            for n in range(NT * HEADS + 1):
                if n < NT * HEADS:
                    dve.wait_ge(s["sc_mm"], 2 * (n + 1))
                    for c in range(2):
                        ch.free(dve.tensor_reduce(att_s[:, n % 2, c:c + 1], bank[2 * (n % 2) + c][:], AX.X, ALU.max))
                    ch.sync()
                    dve.tensor_scalar(att_s[:, n % 2, 2:4], att_s[:, n % 2, 0:2], -(QK ** -0.5), None,
                                      ALU.mult).then_inc(s["sc_max"], 1)
                if n >= 1:
                    m = n - 1
                    dve.wait_ge(s["sc_exp"], 2 * n)
                    ch(dve.reciprocal(att_s[:, m % 2, 6:8], att_s[:, m % 2, 4:6]))
                    ch.free(dve.tensor_scalar(att_s[:, m % 2, 7:8], att_s[:, m % 2, 7:8], lamv[:, 5:6], None, ALU.mult))
                    ch(dve.tensor_scalar(ee[:, m % 2, 0, :], ee[:, m % 2, 0, :], att_s[:, m % 2, 6:7], None, ALU.mult))
                    dve.scalar_tensor_tensor(ee[:, m % 2, 0, :], ee[:, m % 2, 1, :], att_s[:, m % 2, 7:8],
                                             ee[:, m % 2, 0, :], ALU.mult, ALU.add).then_inc(s["a_ready"], 1)
                if n % HEADS == 3 and n > HEADS:
                    o_norm(n // HEADS - 1)
                if n % HEADS == 5 and n > HEADS:
                    o_scale(n // HEADS - 1)
            o_norm(NT - 1)
            o_scale(NT - 1)
            dve.wait_ge(s["param_loaded"], 16 * 13)
            dve.wait_ge(s["u_loaded"], 16 * STEPS)
            ch(tt(Y[:], U[:], bc(dcol[:], 2, CHUNKS, [P, NG, CHUNKS]), ALU.mult))
            dve.wait_ge(s["scan_done"], 2)
            V1, V2 = (T[:, NG:2 * NG, :].rearrange("p g (c m) -> p g c m", m=8) for T in (S1, S2))
            for m in range(7, 0, -1):
                T = [scan_t[:, 2 * (m % 2) + q, 0:NG * 7].rearrange("p (g c) -> p g c", g=NG) for q in range(2)]
                re, im = (bc(psq[:, q, 8 - m, NG:2 * NG], 2, 7, [P, NG, 7]) for q in range(2))
                ch.free(tt(T[0], V1[:, :, 1:8, 0], re, ALU.mult))
                ch(tt(T[1], V2[:, :, 1:8, 0], im, ALU.mult))
                ch(tt(V1[:, :, 0:7, m], V1[:, :, 0:7, m], T[0], ALU.add))
                last = tt(V1[:, :, 0:7, m], V1[:, :, 0:7, m], T[1], ALU.add)
                if m > 1:
                    ch.free(last)
            last.then_inc(s["scan_done"], 1)
            cube = [S2[:, 8 * n:8 * n + 8, :] for n in range(4)]
            y_ = [Y[:, 8 * n:8 * n + 8, :] for n in range(4)]
            def y_add(n):
                dve.wait_ge(s["y_mm"], n + 1)
                tt(y_[n], y_[n], bank[n][:].rearrange("p (g j) -> p g j", j=CHUNKS), ALU.add).then_inc(s["y_gp"], 1)

            def y_cubic(n):
                dve.wait_ge(s["y_ev"], n + 1)
                dve.scalar_tensor_tensor(cube[n], cube[n], 1.0 / GELU_B, y_[n], ALU.add, ALU.mult).then_inc(s["y_cube"], 1)

            def y_gelu(n):
                dve.wait_ge(s["y_sig"], n + 1)
                tt(y_[n], y_[n], cube[n], ALU.mult).then_inc(s["y_done"], 1)
            y_add(0)
            y_add(1)
            y_cubic(0)
            y_add(2)
            y_cubic(1)
            y_gelu(0)
            y_add(3)
            y_cubic(2)
            y_gelu(1)
            y_cubic(3)
            y_gelu(2)
            y_gelu(3)
            for n in range(4):
                dve.wait_ge(s["g_sig"], n + 1)
                tt(sT[:, n, :], sT[:, n, :], yT[:, n, :], ALU.mult).then_inc(s["s_act"], 1)
            dve.wait_ge(s["n_rt"], 1)
            dve.wait_ge(s["s_act"], 4)
            ch(dve.reciprocal(gluw[:, 1, :], gluw[:, 0, :]))
            for n in range(4):
                dve.scalar_tensor_tensor(catT[:, 4 + n, :], sT[:, n, :], outw[:, n:n + 1], gluw[:, 1, :],
                                         ALU.mult, ALU.mult).then_inc(s["s5_done"], 1)
            dve.wait_ge(s["n2w_loaded"], 16)
            ch(dve.scalar_tensor_tensor(mod[:, 4], mod[:, 4], 1.0, n2w[:], ALU.add, ALU.mult))
            dve.wait_ge(s["rw_loaded"], 32)
            dve.wait_ge(s["consts2"], 1)
            for t in range(NT):
                dve.wait_ge(s["mix_mm"], t + 1)
                dve.wait_ge(s[f"x_loaded{t % 2}"], 32 * (NT // 2 + t // 2 + 1))
                if t >= 2:
                    dve.wait_ge(s[f"x1_stored{t % 2}"], 16 * (t // 2))
                for k in range(2):
                    cc_ = slice(512 * k, 512 * k + 512)
                    ch.free(tt(x1[:, t % 2, cc_], bank[2 * (t % 2) + k][:], mod[:, 2, cc_], ALU.mult))
                ch.sync()
                tt(x1[:, t % 2], x1[:, t % 2], xr[:, t % 2], ALU.add).then_inc(s["x1_ready"], 1)
                dve.wait_ge(s["o_sq"], 2 * t + 1)
                tt(sq_s[:, 10:11], sq_s[:, 8:9], sq_s[:, 9:10], ALU.add).then_inc(s["m_rt"], 1)
                dve.wait_ge(s["o_sq"], 2 * t + 2)
                ch(dve.reciprocal(sq_s[:, 12:13], sq_s[:, 11:12]))
                ch(dve.scalar_tensor_tensor(h2[:, t % 2], x1[:, t % 2], sq_s[:, 12:13], mod[:, 4], ALU.mult, ALU.mult))
                tt(h2[:, t % 2], h2[:, t % 2], mod[:, 3], ALU.add).then_inc(s["h2_ready"], 1)
                dve.wait_ge(s["r_mm"], t + 1)
                ch(tt(lg[:], bank[6][:, 0:E], rb[:], ALU.add))
                ch(dve.max(mx8[:], lg[:]))
                ch.free(dve.max_index(ix8[:], mx8[:], lg[:]))
                dve.tensor_scalar(gs[:, 2:3], mx8[:, 0:1], -1.0, None, ALU.mult).then_inc(s["lg_ready"], 1)
                ch.sync()
                ch(dve.tensor_copy(ixf[:], ix8[:]))
                ch(tt(oh4[:, t], bc(iotaE[:, 0:E], 1, TOPK, [P, TOPK, E]), bc(ixf[:, 0:TOPK], 2, E, [P, TOPK, E]), ALU.is_equal))
                dve.tensor_reduce(mask[:, t], oh4[:, t].rearrange("p k e -> p e k"), AX.X, ALU.add).then_inc(s["mask_ready"], 1)
                dve.wait_ge(s["g_exp"], t + 1)
                ch(dve.reciprocal(gs[:, 1:2], gs[:, 0:1]))
                ch(dve.tensor_scalar(gat[:, t, :], gat[:, t, :], gs[:, 1:2], None, ALU.mult))
            dve.wait_ge(s["mix_mm"], NT)
            dve.wait_ge(s["pos_mm"], 1)
            R = [rt[:, k, :] for k in range(8)]
            cnt = bank[7][:, NT * E:NT * E + E]
            ch.free(dve.tensor_scalar(R[0], cnt, 0.5, None, ALU.is_gt))
            for k in range(1, NT):
                ch.free(dve.tensor_scalar(R[k], cnt, k * P + 0.5, None, ALU.is_gt))
            ch.sync()
            ch(tt(R[0], R[0], R[1], ALU.add))
            ch(tt(R[0], R[0], R[2], ALU.add))
            ch(tt(R[0], R[0], R[3], ALU.add))
            ch.free(dve.tensor_scalar(ec[:, 0, 1], R[0], 0.5, None, ALU.is_gt))
            ch(dve.tensor_copy(ec[:, 0, 0], R[0]))
            a, b_ = ec[:, 1], ec[:, 2]
            ch(dve.tensor_copy(a, ec[:, 0]))
            dist = 1
            while dist < E:
                ch.free(dve.tensor_copy(b_[:, :, 0:dist], a[:, :, 0:dist]))
                ch(tt(b_[:, :, dist:E], a[:, :, dist:E], a[:, :, 0:E - dist], ALU.add))
                a, b_ = b_, a
                dist *= 2
            end, loads = a[:, 0], a[:, 1]
            ch.free(dve.tensor_copy(nbi[:], a[:, :, E - 1]))
            nl = E + 2
            ch(tt(cmpl[:], bc(iotaE[:, 0:nl], 2, E, [P, nl, E]), bc(loads, 1, nl, [P, nl, E]), ALU.is_ge))
            ch(dve.tensor_reduce(tabf[:, 0, 0:nl], cmpl[:], AX.X, ALU.add))
            ch(tt(cmpl[:], cmpl[:], bc(ec[:, 0, 0], 1, nl, [P, nl, E]), ALU.mult))
            ch.free(dve.tensor_scalar(load_expert[:], tabf[:, 0, 0:nl], float(E - 1), None, ALU.min))
            ch(dve.tensor_reduce(tabf[:, 1, 0:nl], cmpl[:], AX.X, ALU.add))
            dve.tensor_scalar(load_after[:], tabf[:, 1, 0:nl], -1.0, 0.0, ALU.add, ALU.max).then_inc(s["blocks_ready"], 1)
            ch(tt(cmpb[:], bc(iotaE[:], 2, E, [P, MAXB, E]), bc(end, 1, MAXB, [P, MAXB, E]), ALU.is_ge))
            ch(dve.tensor_reduce(ebf[:, 0:MAXB], cmpb[:], AX.X, ALU.add))
            ch(tt(cmpb[:], cmpb[:], bc(ec[:, 0, 1], 1, MAXB, [P, MAXB, E]), ALU.mult))
            ch.free(dve.memset(tabf[:, 2, MAXB:MAXB + 2], 0.0))
            ch(dve.tensor_reduce(tabf[:, 2, 0:MAXB], cmpb[:], AX.X, ALU.add))
            ch.free(dve.tensor_scalar(block_load[:], tabf[:, 2], 1.0, 32.0, ALU.add, ALU.mult))
            ch(tt(R[3], end, R[0], ALU.subtract))
            ch(dve.tensor_scalar(R[4], R[3], float(P), None, ALU.mult))
            ch.free(dve.memset(ebf[:, MAXB:MAXB + 2], 0.0))
            ch.free(tt(slotE[:], bank[7][:, 0:NT * E].rearrange("p (t e) -> p t e", e=E), bc(R[4], 1, NT, [P, NT, E]), ALU.add))
            ch(dve.tensor_scalar(ebf[:, 0:MAXB], ebf[:, 0:MAXB], float(E - 1), None, ALU.min))
            ch.free(dve.tensor_scalar(eye96[:], ebf[0:96, :], pm[0:96, 0:1], None, ALU.is_equal))
            for t in range(NT):
                ch.free(tt(prod[:, TOPK * t:TOPK * t + TOPK], oh4[:, t], bc(slotE[:, t], 1, TOPK, [P, TOPK, E]), ALU.mult))
            ch.sync()
            ch(dve.tensor_reduce(dslot[:], prod[:], AX.X, ALU.add))
            dve.nop().then_inc(s["blocks_ready"], 1)
            n_blocks = dve.value_load(nbi[0:1, 0:1], min_val=1, max_val=MAXB)
            dve.wait_ge(s["bias_ready"], 2)

            def slots(v):
                tt(ohs[:], bc(iotab[:], 1, NT * TOPK, [P, NT * TOPK, P]), bc(dslot[:], 2, P, [P, NT * TOPK, P]),
                   ALU.is_equal).then_inc(s["oh_ready"], 1)
                dve.wait_ge(s["oh_ready"], v)
                dve.tensor_scalar(iotab[:], iotab[:], float(P), None, ALU.add).then_inc(s["d_ready"], 1)

            def rows(v):
                dve.wait_ge(s["idx_mm"], v)
                dve.tensor_reduce(idf[:, 0:1], bank[6][:, 0:2], AX.X, ALU.add).then_inc(s["idx_sum"], 1)
                dve.tensor_reduce(idf[:, 1:2], bank[6][:, 0:4], AX.X, ALU.add).then_inc(s["idx_sum"], 1)
                dve.wait_ge(s["idx_sum"], v * 2)
                dve.tensor_scalar(idx[:, 0:1], idf[:, 0:1], 1 / TOPK, None, ALU.mult).then_inc(s["idx_ready"], 1)

            def rows_out():
                dve.tensor_scalar(idx[:, 1:2], idf[:, 1:2], UNUSED, None, ALU.add).then_inc(s["idx_ready"], 1)

            def select(b):
                dve.tensor_copy(selb[:], eye96[:, bass.ds(b, 1)].to_broadcast([96, P])).then_inc(s["sel_ready"], 1)

            def low(chunks, b, first=False):
                for c in chunks:
                    if c in POOL_LOW:
                        continue
                    dve.wait_ge(s["hi_done"], c + 1 if first else b * WCH + (c + 1))
                    hi, lo = w_split[c % SPLIT]
                    tt(lo[:], raw(c), hi[:].bitcast(F32), ALU.subtract).then_inc(s["lo_dve"], 1)

            def x_low(k, b2):
                dve.wait_ge(s["xs_ev"], b2 + (k + 1))
                part = [x[:, 4 * k:4 * k + 4, :].rearrange("p k n -> p (k n)") for x in xT]
                tt(part[1], bank[7 - k][:], part[0].bitcast(F32), ALU.subtract).then_inc(s["x_lo"], 1)

            def act_low(k, b2):
                dve.wait_ge(s["act_ev"], b2 + (k + 1))
                part = [x[:, 4 * k:4 * k + 4, :].rearrange("p k n -> p (k n)") for x in actT]
                tt(part[1], bank[6 + k][:], part[0].bitcast(F32), ALU.subtract).then_inc(s["act_lo"], 1)

            def gate_parts(k):
                z = [bank[2 * k][:].rearrange("p (f two) -> p two f", two=2),
                     bank[2 * k + 1][:].rearrange("p (f two) -> p two f", two=2)]
                return z, glu[:, 0, :] if k == 0 else glu[:, 2, :], lin[:, k, :], glu[:, 1, :] if k == 0 else lin[:, 2, :]

            def gate_min(k, b):
                z, g, l, sg = gate_parts(k)
                dve.wait_ge(w_used, b * WCH + KT * (k + 1))
                for q in range(2):
                    dve.tensor_scalar(g[:, 256 * q:256 * q + 256], z[q][:, 0, :], 7.0, None, ALU.min).then_inc(s["l_a"], 1)
                dve.wait_ge(s["l_a"], b * 8 + (4 * k + 2))
                dve.nop().then_inc(s["g_min"], 1)

            def gated(k, b):
                z, g, l, sg = gate_parts(k)
                for q in range(2):
                    dve.tensor_scalar(l[:, 256 * q:256 * q + 256], z[q][:, 1, :], 7.0, -7.0, ALU.min,
                                      ALU.max).then_inc(s["l_a"], 1)
                dve.wait_ge(s["l_a"], b * 8 + (4 * k + 4))
                dve.scalar_tensor_tensor(l, l, 1.0, g, ALU.add, ALU.mult).then_inc(s["l_b"], 1)
                dve.wait_ge(s["l_b"], b * 2 + (k + 1))
                dve.wait_ge(s["g_sg"], b * 2 + (k + 1))
                tt(l, l, sg, ALU.mult).then_inc(s["act_ready"], 1)

            slots(1)
            select(0)
            rows(1)
            rows_out()
            low(range(SPLIT), 0, first=True)
            x_low(0, 0)
            x_low(1, 0)
            with dve.Fori(0, n_blocks) as b:
                b2 = b * 2
                dve.wait_ge(s["d_ready"], b + 1)
                slots(b + 2)
                low(range(SPLIT, 10), b)
                rows(b + 2)
                low(range(10, 14), b)
                gate_min(0, b)
                gated(0, b)
                dve.wait_ge(s["scat_ready"], b + 1)
                rows_out()
                low(range(14, 20), b)
                gate_min(1, b)
                act_low(0, b2)
                gated(1, b)
                low(range(20, 21), b)
                x_low(0, b2 + 2)
                low(range(21, 23), b)
                dve.wait_ge(w_used, b * WCH + W1C + 1)
                select(b + 1)
                low(range(23, WCH), b)
                act_low(1, b2)
                x_low(1, b2 + 2)
                low(range(SPLIT), b + 1)
            dve.wait_ge(s["lo_pool"], n_blocks * len(POOL_LOW))
            dve.wait_ge(*low_ready(SPLIT - 1, n_blocks))
            dve.sem_inc(s["fin_done"], 1)
            dve.wait_ge(s["fin_x1"], 16)
            for t in range(NT):
                dve.wait_ge(s[f"fin_g{t}"], 16)
                o = facc[:, t]
                ch(dve.tensor_scalar(o, fing[:, TOPK * t], gat[:, t, 0:1], None, ALU.mult))
                for k in range(1, TOPK):
                    ch(dve.scalar_tensor_tensor(o, fing[:, TOPK * t + k], gat[:, t, k:k + 1], o, ALU.mult, ALU.add))
                ch(tt(o, o, mod[:, 5], ALU.mult))
                tt(o, o, fx1[:, t], ALU.add).then_inc(s["fin_done"], 1)

        @block.tensor
        def _(pe):
            mm, tr = pe.matmul, pe.transpose
            pe.wait_ge(s["ident_ready"], 1)
            pe.wait_ge(s["s5_nat"], 96)
            for q in range(2):
                for n in range(8):
                    last = tr(bank[2 * q + n // 4][:, (n % 4) * P:(n % 4) * P + P],
                              CC[:, n, q:q + 2, :].rearrange("p a b -> p (a b)"), ident[:])
            last.then_inc(s["pe_prep"], 1)
            bbf = BB[:].rearrange("p a b -> p (a b)")
            for q in range(2):
                for c in range(GC):
                    o = q * NP * GC + c
                    last = tr(bank[4 + 2 * q + c // 8][:, (c % 8) * DG:(c % 8) * DG + DG],
                              bbf[:, o:o + GC * (P - 1) + 1:GC], ident[0:DG, 0:DG])
            last.then_inc(s["pe_prep"], 1)

            def ada(n):
                pe.wait_ge(ring_sem[n % RING], 16 * (n // RING + 1))
                if n >= 7:
                    pe.wait_ge(s["ada_ev"], n - 6)
                for k in range(KT):
                    last = mm(bank[ada_bank(n)][:], cbc[:, k, :], ring[:, n % RING, k, :], start=(k == 0), stop=(k == KT - 1))
                last.then_inc(s["ada_mm"], 1)

            pe.wait_ge(s["cbc_ready"], 1)
            pe.wait_ge(s["cq_ready"], 2)
            pe.wait_ge(s["act"], 2)
            ada(0)
            pe.wait_ge(s["quad_ready"], 1)
            for q in range(4):
                last = tr(bank[2][:, q * DG:(q + 1) * DG], quad[:, q].rearrange("p a b -> p (a b)"), ident[0:DG, 0:DG])
            last.then_inc(s["af_psum"], 1)
            ada(1)
            pe.wait_ge(s["bx_ready"], 4)
            for n in range(2, ADA_CHUNKS):
                ada(n)
            pe.wait_ge(s["inraw_ready"], 1)
            pe.wait_ge(s["ada_ev"], ADA_CHUNKS)
            for n in range(DG // 4):
                if n >= 4:
                    pe.wait_ge(s["in_done"], n - 3)
                for g in range(4):
                    last = tr(bank[2 + n % 4][:, g * P:(g + 1) * P], inT[:, 4 * n + g, :], ident[:])
                last.then_inc(s["in_tr"], 1)
            pe.wait_ge(s["outm_ready"], 2)

            def kernels(first):
                for n in range(first, first + 4):
                    if n >= 2:
                        pe.wait_ge(s["k_ev"], n - 1)
                    for q in range(2):
                        g = 2 * n + q
                        o = q * 240
                        mm(bank[6 + n % 2][0:GC, o + 112:o + 240], BS[:, :, g],
                           outM[:, g, 0:STEPS, :].rearrange("p l c -> p (l c)"), start=(q == 0), stop=False, skip_group_check=True)
                        last = mm(bank[6 + n % 2][0:GC, o:o + P], BS[:, :, NG + g],
                                  outM[:, NG + g, 1:STEPS + 1, :].rearrange("p l c -> p (l c)"), start=False, stop=(q == 1),
                                  skip_group_check=True)
                    last.then_inc(s["k_mm"], 1)

            def h_turn(t):
                pe.wait_ge(s["h_ready"], t + 1)
                if t >= 2:
                    pe.wait_ge(s["h_ev"], 2 * (t - 1))
                for k in range(KT):
                    last = tr(bank[2 * (t % 2) + k // 4][:, (k % 4) * P:(k % 4) * P + P], xt[:, t % 2, k * P:(k + 1) * P], ident[:])
                last.then_inc(s["h_tr"], 1)
            kernels(0)
            pe.wait_ge(s["in_done"], DG // 4)
            h_turn(0)
            kernels(4)
            h_turn(1)
            h_turn(2)
            kernels(8)
            h_turn(3)
            kernels(12)
            pe.wait_ge(s["h_ev"], 2 * NT)
            pe.wait_ge(ring_sem[U_CHUNK % RING], 16 * (U_CHUNK // RING + 1))
            for n in range(4):
                for k in range(KT):
                    last = mm(bank[n][:], ring[:, U_CHUNK % RING, k, n * P:(n + 1) * P], hT[:, k, :],
                              start=(k == 0), stop=(k == KT - 1))
                last.then_inc(s["u_mm"], 1)
            def proj(c, t, bk):
                if t == 0:
                    pe.wait_ge(ring_sem[c % RING], 16 * (c // RING + 1))
                for k in range(KT):
                    last = mm(bk[:], hT[:, k, t * P:(t + 1) * P], ring[:, c % RING, k, :], start=(k == 0), stop=(k == KT - 1))
                last.then_inc(s["q_mm"], 1)

            def qk_tr(n):
                bk = bank[4 + n] if n < 4 else bank[n - 4]
                pe.wait_ge(s["q_n"], n + 1)
                for b in range(4):
                    last = tr(bk[:, b * P:(b + 1) * P], stg[:, n % 2, b * P:(b + 1) * P], ident[:])
                last.then_inc(s["q_tr"], 1)
            pe.wait_ge(s["k_ev"], NG // 2)
            pe.wait_ge(s["sq1"], 2 * NT)
            def chunk_inputs(n):
                for k in range(2):
                    if n >= 2:
                        pe.wait_ge(s["s_ev"], 2 * (n - 2) + k + 1)
                    bk = bank[4 + 2 * (n % 2) + k]
                    for g in range(8):
                        d = 8 * n + g
                        if k == 0:
                            last = mm(bk[:, g * 64:g * 64 + 64], inT[:, d, :], U[:, d % NG, :], start=True, stop=True)
                        else:
                            mm(bk[0:64, g * 64:g * 64 + 64], inT[:, d, 64:128], U[:, d % NG, :], start=True, stop=True)
                            last = mm(bk[64:128, g * 64:g * 64 + 64], inT[:, d, 0:64], U[:, d % NG, :], start=True, stop=True)
                    last.then_inc(s["s_mm"], 1)
            for t in range(NT):
                proj(Q_CHUNK, t, bank[4 + t])
            pe.wait_ge(s["u_ev"], 4)
            for t in range(NT):
                proj(K_CHUNK, t, bank[t])
                qk_tr(t)
            pe.wait_ge(s["q_ev"], 4)
            pe.wait_ge(s["u_loaded"], 16 * STEPS)
            for n in range(DG // 8):
                chunk_inputs(n)
                if n % 2:
                    qk_tr(4 + n // 2)
            pe.wait_ge(s["s_ev"], 2 * DG // 8)
            for t in range(NT):
                proj(V_CHUNK, t, bank[4 + t])
            pe.wait_ge(s["q_ev"], 8)
            pe.wait_ge(s["v_ev"], 4)

            def scores(n):
                t, h = n // HEADS, n % HEADS
                if n >= 2:
                    pe.wait_ge(s["sc_exp"], 2 * (n - 1))
                if h == 0:
                    pe.wait_ge(s["qm_ready"], 4 * (t + 1))
                for c in range(2):
                    g = 2 * h + c
                    mm(bank[2 * (n % 2) + c][:], qm[:, t % 2, g % 4, g // 4, :], qkT[:, 1, g // 4, :],
                       start=True, stop=True).then_inc(s["sc_mm"], 1)

            def values(n):
                t, h = n // HEADS, n % HEADS
                pe.wait_ge(s["a_ev"], n + 1)
                if h == 0 and t:
                    pe.wait_ge(s["o_copied"], t)
                for k in range(NT):
                    last = mm(bank[6][:, h * DV:(h + 1) * DV], aT[:, n % 2, k, :], vv[:, k, h * DV:(h + 1) * DV],
                              start=(k == 0), stop=(k == NT - 1))
                last.then_inc(s["pv_mm"], 1)

            def o_tr(t):
                pe.wait_ge(s["o_n"], t + 1)
                if t:
                    pe.wait_ge(s["o_ev"], t)
                for k in range(4):
                    last = tr(bank[7][:, k * P:(k + 1) * P], o_n[:, 0, k * P:(k + 1) * P], ident[:])
                last.then_inc(s["o_tr"], 1)
            for n in range(NT * HEADS + 3):
                if n < NT * HEADS:
                    scores(n)
                if 2 <= n <= NT * HEADS + 1:
                    m = n - 2
                    pe.wait_ge(s["a_ready"], m + 1)
                    if m >= 2:
                        pe.wait_ge(s["a_ev"], m - 1)
                    for k in range(NT):
                        last = tr(bank[4 + m % 2][:, k * P:(k + 1) * P], ee[:, m % 2, 0, k * P:(k + 1) * P], ident[:])
                    last.then_inc(s["a_tr"], 1)
                if n >= 3:
                    values(n - 3)
                if n % HEADS == 6 and n > HEADS:
                    o_tr(n // HEADS - 1)
            pe.wait_ge(s["scan_done"], 1)
            pe.wait_ge(s["kp_half"], 32 * STEPS)
            pe.wait_ge(s["sc_exp"], 2 * NT * HEADS)
            for g in range(NG):
                bk, o = bank[g // 8], 64 * (g % 8)
                mm(bk[:, o:o + 64], toep[:, g, :], U[:, g, :], start=(g % 8 == 0), stop=False, skip_group_check=True)
                mm(bk[:, o + 1:o + 64], outM[:, g, 1:STEPS + 1, :].rearrange("p l c -> p (l c)"),
                   S1[:, g, 0:63], start=False, stop=False, skip_group_check=True)
            o_tr(NT - 1)
            pe.wait_ge(s["scan_done"], 3)
            for g in range(NG):
                bk, o = bank[g // 8], 64 * (g % 8)
                last = mm(bk[:, o:o + 63], outM[:, NG + g, 0:STEPS, :].rearrange("p l c -> p (l c)"),
                          S1[:, NG + g, 1:64], start=False, stop=(g % 8 == 7), skip_group_check=True)
                if g % 8 == 7:
                    last.then_inc(s["y_mm"], 1)

            def mix_part(t, part):
                for k in range(2):
                    for c in range(4 * part, 4 * part + 4):
                        last = mm(bank[2 * (t % 2) + k][:], catT[:, c, t * P:(t + 1) * P],
                                  wout[:, c, 512 * k:512 * k + 512], start=(c == 0), stop=(c == KT - 1))
                return last
            pe.wait_ge(s["y_gp"], 4)
            pe.wait_ge(s["o_ev"], NT)
            pe.wait_ge(s["wout_loaded"], 16)
            mix_part(0, 0)
            mix_part(1, 0)
            pe.wait_ge(s["y_loaded"], 32)
            pe.wait_ge(s["gluw_loaded"], 16)
            for n in range(4):
                for k in range(4):
                    last = mm(bank[4 + n][:], gluw[:, k, n * P:(n + 1) * P], yT[:, k, :], start=(k == 0), stop=(k == 3))
                last.then_inc(s["g_mm"], 1)
            pe.wait_ge(s["s_sq"], 4)
            pe.wait_ge(s["consts2"], 1)
            for k in range(4):
                last = mm(bank[4][:], ones[:], sqT[:, k, :], start=(k == 0), stop=(k == 3))
            last.then_inc(s["n_mm"], 1)
            pe.wait_ge(s["s5_done"], 4)

            def mix(t):
                if t >= 2:
                    pe.wait_ge(s["x1_ready"], t - 1)
                    mix_part(t, 0)
                mix_part(t, 1).then_inc(s["mix_mm"], 1)

            def route(t):
                pe.wait_ge(s["h2_ready"], t + 1)
                if t == 0:
                    pe.wait_ge(s["g_sig"], 4)
                else:
                    pe.wait_ge(s["h2_ev"], 2 * t)
                for k in range(KT):
                    last = tr(bank[4 + k // 4][:, (k % 4) * P:(k % 4) * P + P], h2[:, t % 2, k * P:(k + 1) * P], ident[:])
                last.then_inc(s["h2_tr"], 1)
                pe.wait_ge(s["h2_ev"], 2 * (t + 1))
                if t == 0:
                    pe.wait_ge(s["rw_loaded"], 32)
                else:
                    pe.wait_ge(s["lg_ready"], t)
                for k in range(KT):
                    last = mm(bank[6][:, 0:E], h2T[:, k, :], rw[:, k, :], start=(k == 0), stop=(k == KT - 1))
                last.then_inc(s["r_mm"], 1)

            mix(0)
            mix(1)
            for t in range(NT):
                route(t)
                if t + 2 < NT:
                    mix(t + 2)
            pe.wait_ge(s["mask_ready"], NT)
            for t in range(NT):
                for q in range(t + 1):
                    mm(bank[7][:, t * E:(t + 1) * E], tri[:] if q == t else onb[:], mask[:, q, :], start=(q == 0), stop=(q == t))
            for q in range(NT):
                last = mm(bank[7][:, NT * E:(NT + 1) * E], onb[:], mask[:, q, :], start=(q == 0), stop=(q == NT - 1))
            last.then_inc(s["pos_mm"], 1)
            pe.wait_ge(s["blocks_ready"], 2)
            n_blocks = pe.value_load(nbi[0:1, 0:1], min_val=1, max_val=MAXB)

            def rows(v):
                pe.wait_ge(s["oh_ready"], v)
                for q in range(NT * TOPK):
                    last = mm(bank[6][:, 0:4], ohs[:, q, :], tokid[:, q, :], start=(q == 0), stop=(q == NT * TOPK - 1))
                last.then_inc(s["idx_mm"], 1)

            def split_mm(banks, x, c, w, stop, x_low_ready=None):
                for i, j in ((0, 0), (0, 1), (1, 0)):
                    if i == 1 and x_low_ready is not None:
                        pe.wait_ge(*x_low_ready)
                    for q in range(2):
                        last = mm(banks[q][:], x[i][:, c, :], w[j][:, 512 * q:512 * q + 512], start=False, stop=(stop and i == 1))
                last.then_inc(w_used, 1)

            def x_turn(k, v):
                pe.wait_ge(s["xs_loaded"], v * 16)
                for c in range(4):
                    last = tr(bank[7 - k][:, c * P:(c + 1) * P], xs[:, (4 * k + c) * P:(4 * k + c + 1) * P], ident[:])
                last.then_inc(s["xs_tr"], 1)

            def up(k, b):
                if k == 0:
                    pe.wait_ge(s["sel_ready"], b + 1)
                for q in range(2):
                    mm(bank[2 * k + q][:], selb[:], bcat[:, (2 * k + q) * 512:(2 * k + q + 1) * 512], start=True, stop=False)
                for c in range(KT * k, KT * k + KT):
                    if c == 4:
                        rows(b + 2)
                    pe.wait_ge(*low_ready(c, b))
                    split_mm(bank[2 * k:2 * k + 2], xT, c % KT, w_split[c % SPLIT], c % KT == KT - 1)

            def act_turn(k, b):
                pe.wait_ge(s["act_ready"], b * 2 + (k + 1))
                if k == 0:
                    pe.wait_ge(s["idx_ready"], b * 2 + 4)
                else:
                    pe.wait_ge(s["x_lo"], b * 2 + 3)
                for c in range(4):
                    last = tr(bank[6 + k][:, c * P:(c + 1) * P], lin[:, k, c * P:(c + 1) * P], ident[:])
                last.then_inc(s["act_tr"], 1)

            def down(k, b):
                if k == 0:
                    pe.wait_ge(s["y2_ev"], b * 2 + 2)
                    for q in range(2):
                        mm(bank[4 + q][:], selb[:], bcat[:, 2048 + 512 * q:2560 + 512 * q], start=True, stop=False)
                pe.wait_ge(s["act_ev"], b * 2 + (k + 1))
                for c in range(W1C + 4 * k, W1C + 4 * k + 4):
                    pe.wait_ge(*low_ready(c, b))
                    split_mm(bank[4:6], actT, c - W1C, w_split[c % SPLIT], c == WCH - 1,
                             (s["act_lo"], b * 2 + (k + 1)) if c % 4 == 0 else None)

            pe.wait_ge(s["bias_ready"], 1)
            rows(1)
            x_turn(0, 1)
            x_turn(1, 1)
            with pe.Fori(0, n_blocks) as b:
                pe.wait_ge(s["x_lo"], b * 2 + 2)
                up(0, b)
                up(1, b)
                act_turn(0, b)
                x_turn(0, b + 2)
                down(0, b)
                act_turn(1, b)
                x_turn(1, b + 2)
                down(1, b)


NAMES = ["x", "c", "positions", "ada_w", "ada_b", "norm1_w", "w_in", "q_norm_w", "k_norm_w", "lambda_q1", "lambda_k1",
         "lambda_q2", "lambda_k2", "subln_w", "s5_lambda_re", "s5_lambda_im", "s5_log_step", "s5_b_re", "s5_b_im",
         "s5_cmat_re", "s5_cmat_im", "s5_d", "s5_glu_w", "s5_glu_b", "s5_out_norm_w", "w_out", "norm2_w", "router_w",
         "router_b", "mlp1_w", "mlp1_b", "mlp2_w", "mlp2_b"]


def kernel(**inputs):
    from concourse import bacc
    from concourse.bass_utils import run_bass_kernel_spmd

    nc = bacc.Bacc("TRN2", target_bir_lowering=False, num_devices=1)
    arrays = {n: np.ascontiguousarray(inputs[n]) for n in NAMES}
    params = {n: nc.dram_tensor(n, a.shape, mybir.dt.from_np(a.dtype), kind="ExternalInput").ap()
              for n, a in arrays.items()}
    out = nc.dram_tensor("out", (1, S, D), F32, kind="ExternalOutput").ap()
    program(nc, params, out)
    r = run_bass_kernel_spmd(nc, [arrays], core_ids=[0])
    return r.results[0]["out"]
```
